# Optimizing a Trainium2 kernel written in Bass

```python
import math
import jax, jax.numpy as jnp
from jax import lax
import numpy as np

D_MODEL = 1024
BATCH = 1
SEQ = 256
DEPTH = 2

ATT_GROUPS = ((128, 1), (512, 4), (2048, 16))
ATT_HEADS_PER_GROUP = 4
ATT_HEAD_DIM = 64
ATT_HEADS = len(ATT_GROUPS) * ATT_HEADS_PER_GROUP
ATT_WIDTH = ATT_HEADS * ATT_HEAD_DIM
ATT_OUT_WIDTH = ATT_HEADS_PER_GROUP * ATT_HEAD_DIM
BAND_BLOCK = 64
ROPE_THETA = 10000.0
DN_HEADS = 6
DN_HEAD_DIM = 128
DN_WIDTH = DN_HEADS * DN_HEAD_DIM
DN_CONV = 5
DN_CHUNK = 64
FFN_DIM = ((8 * D_MODEL // 3 + 127) // 128) * 128
IN_SIZES = (ATT_WIDTH, ATT_WIDTH, ATT_WIDTH, 3 * DN_WIDTH, DN_WIDTH, 2 * DN_HEADS, 2 * DN_HEADS, D_MODEL, D_MODEL)
N_IN = sum(IN_SIZES)
N_SUBLAYERS = 3
EPS = 1e-6
NEG_INF = -1e30

kernel_name = 'hybrid_dilated_attn_gated_deltanet_macaron_block'

def rmsnorm(t, gain):
    t32 = t.astype(jnp.float32)
    y = t32 * lax.rsqrt(jnp.mean(t32 * t32, axis=-1, keepdims=True) + EPS)
    return (y * gain.astype(jnp.float32)).astype(t.dtype)

def ada_pre(t, gain, shift, scale):
    return rmsnorm(t, gain) * (1.0 + scale[:, None, :]) + shift[:, None, :]

def swiglu(h, w_in, w_out):
    gu = h @ w_in
    g, u = jnp.split(gu, 2, axis=-1)
    return (jax.nn.silu(g) * u) @ w_out

def rotary(t, positions):
    e = t.shape[-1]
    half = e // 2
    inv = ROPE_THETA ** (-jnp.arange(half, dtype=jnp.float32) * 2.0 / e)
    ang = positions.astype(jnp.float32)[:, :, None] * inv
    cos = jnp.cos(ang)[:, :, None, :]
    sin = jnp.sin(ang)[:, :, None, :]
    t32 = t.astype(jnp.float32)
    t1, t2 = t32[..., :half], t32[..., half:]
    return jnp.concatenate([t1 * cos - t2 * sin, t2 * cos + t1 * sin], axis=-1).astype(t.dtype)

def dilated_window_attention(q, k, v, window, dilation):
    B, S, H, E = q.shape
    radius = window // (2 * dilation)
    L = S // dilation
    nb = -(-L // BAND_BLOCK)
    pad = nb * BAND_BLOCK - L

    def to_classes(t):
        return t.reshape(B, L, dilation, H, E).transpose(0, 2, 3, 1, 4)

    qb = jnp.pad(to_classes(q), ((0, 0), (0, 0), (0, 0), (0, pad), (0, 0)))
    qb = qb.reshape(B, dilation, H, nb, BAND_BLOCK, E)

    def key_windows(t):
        tp = jnp.pad(to_classes(t), ((0, 0), (0, 0), (0, 0), (BAND_BLOCK, pad + BAND_BLOCK), (0, 0)))
        tp = tp.reshape(B, dilation, H, nb + 2, BAND_BLOCK, E)
        return jnp.concatenate([tp[:, :, :, :-2], tp[:, :, :, 1:-1], tp[:, :, :, 2:]], axis=-2)

    kw = key_windows(k)
    vw = key_windows(v)
    scores = jnp.einsum('bdhnqe,bdhnke->bdhnqk', qb, kw, preferred_element_type=jnp.float32) * (E ** -0.5)
    qi = jnp.arange(BAND_BLOCK)[:, None]
    kj = jnp.arange(3 * BAND_BLOCK)[None, :] - BAND_BLOCK
    kpos = jnp.arange(nb)[:, None, None] * BAND_BLOCK + kj
    valid = (jnp.abs(kj - qi) <= radius) & (kpos >= 0) & (kpos < L)
    scores = jnp.where(valid, scores, NEG_INF)
    m = jnp.max(scores, axis=-1, keepdims=True)
    p = jnp.exp(scores - m)
    den = jnp.sum(p, axis=-1, keepdims=True)
    o = jnp.einsum('bdhnqk,bdhnke->bdhnqe', p, vw.astype(jnp.float32)) / den
    lse = (m + jnp.log(den))[..., 0]
    o = o.reshape(B, dilation, H, nb * BAND_BLOCK, E)[:, :, :, :L]
    o = o.transpose(0, 3, 1, 2, 4).reshape(B, S, H, E)
    lse = lse.reshape(B, dilation, H, nb * BAND_BLOCK)[..., :L]
    lse = lse.transpose(0, 3, 1, 2).reshape(B, S, H)
    return o, lse

def short_conv(t, w):
    C = t.shape[-1]
    pad = w.shape[0] // 2
    return lax.conv_general_dilated(t, w[:, None, :].astype(t.dtype), window_strides=(1,),
                                    padding=[(pad, pad)], dimension_numbers=('NWC', 'WIO', 'NWC'),
                                    feature_group_count=C)

def l2norm(t):
    return t * lax.rsqrt(jnp.sum(t * t, axis=-1, keepdims=True) + EPS)

def gated_delta_chunked(q, k, v, beta, g):
    B, H, S, DK = q.shape
    DV = v.shape[-1]
    C = DN_CHUNK
    N = S // C
    q = q.reshape(B, H, N, C, DK)
    k = k.reshape(B, H, N, C, DK)
    v = v.reshape(B, H, N, C, DV)
    beta = beta.reshape(B, H, N, C)
    G = jnp.cumsum(g.reshape(B, H, N, C), axis=-1)
    incl = jnp.tril(jnp.ones((C, C), dtype=bool))
    strict = jnp.tril(jnp.ones((C, C), dtype=bool), -1)
    decay = jnp.exp(jnp.where(incl, G[..., :, None] - G[..., None, :], NEG_INF))
    kb = k * beta[..., None]
    m_low = jnp.where(strict, jnp.einsum('bhnid,bhnjd->bhnij', kb, k) * decay, 0.0)
    tmat = m_low + jnp.eye(C, dtype=jnp.float32)
    rhs = jnp.concatenate([v * beta[..., None], kb * jnp.exp(G)[..., None]], axis=-1)
    sol = lax.linalg.triangular_solve(tmat, rhs, left_side=True, lower=True, unit_diagonal=True)
    u, w = sol[..., :DV], sol[..., DV:]
    attn = jnp.einsum('bhnid,bhnjd->bhnij', q, k) * decay
    qg = q * jnp.exp(G)[..., None]
    kdec = k * jnp.exp(G[..., -1:] - G)[..., None]
    glast = jnp.exp(G[..., -1])

    def step(state, inp):
        u_c, w_c, attn_c, qg_c, kdec_c, gl_c = inp
        v_new = u_c - jnp.einsum('bhcd,bhde->bhce', w_c, state)
        o_c = jnp.einsum('bhcd,bhde->bhce', qg_c, state) + jnp.einsum('bhij,bhje->bhie', attn_c, v_new)
        state = state * gl_c[..., None, None] + jnp.einsum('bhcd,bhce->bhde', kdec_c, v_new)
        return state, o_c

    xs = tuple(jnp.moveaxis(t, 2, 0) for t in (u, w, attn, qg, kdec, glast))
    _, o = lax.scan(step, jnp.zeros((B, H, DK, DV), jnp.float32), xs)
    return jnp.moveaxis(o, 0, 2).reshape(B, H, S, DV)

def hybrid_mixer(h, positions, w_in, conv_w, a_log, dt_bias, dn_norm_w, w_branch_att, w_branch_dn, w_out):
    B, S, _ = h.shape
    proj = h @ w_in
    split_idx = [int(i) for i in np.cumsum(IN_SIZES)[:-1]]
    q_a, k_a, v_a, dn_qkv, z, beta_raw, alpha_raw, gate_att, gate_dn = jnp.split(proj, split_idx, axis=-1)

    def att_heads(t):
        return t.reshape(B, S, ATT_HEADS, ATT_HEAD_DIM)
    q_a = rotary(att_heads(q_a), positions)
    k_a = rotary(att_heads(k_a), positions)
    v_a = att_heads(v_a)
    outs, lses = [], []
    for gi, (window, dilation) in enumerate(ATT_GROUPS):
        sl = slice(gi * ATT_HEADS_PER_GROUP, (gi + 1) * ATT_HEADS_PER_GROUP)
        o_g, lse_g = dilated_window_attention(q_a[:, :, sl], k_a[:, :, sl], v_a[:, :, sl], window, dilation)
        outs.append(o_g)
        lses.append(lse_g)
    mix = jax.nn.softmax(jnp.stack(lses, axis=0), axis=0)
    o_att = jnp.sum(mix[..., None] * jnp.stack(outs, axis=0), axis=0)
    o_att = o_att.reshape(B, S, ATT_OUT_WIDTH).astype(h.dtype)

    dn = jax.nn.silu(short_conv(dn_qkv, conv_w))
    q_d, k_d, v_d = jnp.split(dn, 3, axis=-1)

    def dn_heads(t):
        return t.reshape(B, S, DN_HEADS, DN_HEAD_DIM).transpose(0, 2, 1, 3).astype(jnp.float32)
    q_d = l2norm(dn_heads(q_d)) * (DN_HEAD_DIM ** -0.5)
    k_d = l2norm(dn_heads(k_d))
    v_d = dn_heads(v_d)
    beta = jax.nn.sigmoid(beta_raw.astype(jnp.float32)).reshape(B, S, 2, DN_HEADS).transpose(2, 0, 3, 1)
    alpha = alpha_raw.astype(jnp.float32).reshape(B, S, 2, DN_HEADS).transpose(2, 0, 3, 1)
    log_decay = -jnp.exp(a_log.astype(jnp.float32))[:, None, :, None] * jax.nn.softplus(
        alpha + dt_bias.astype(jnp.float32)[:, None, :, None])
    o_fwd = gated_delta_chunked(q_d, k_d, v_d, beta[0], log_decay[0])
    rev = lambda t: jnp.flip(t, axis=2)
    o_bwd = rev(gated_delta_chunked(rev(q_d), rev(k_d), rev(v_d), rev(beta[1]), rev(log_decay[1])))
    o_dn = (o_fwd + o_bwd).transpose(0, 2, 1, 3)
    o_dn = o_dn * lax.rsqrt(jnp.mean(o_dn * o_dn, axis=-1, keepdims=True) + EPS) * dn_norm_w.astype(jnp.float32)
    o_dn = o_dn * jax.nn.silu(z.astype(jnp.float32).reshape(B, S, DN_HEADS, DN_HEAD_DIM))
    o_dn = o_dn.reshape(B, S, DN_WIDTH).astype(h.dtype)

    y = jax.nn.sigmoid(gate_att) * (o_att @ w_branch_att) + jax.nn.sigmoid(gate_dn) * (o_dn @ w_branch_dn)
    return y @ w_out

def setup_inputs(seed: int = 0) -> dict:
    key = jax.random.key(seed)
    ks = jax.random.split(key, 20)
    f32 = jnp.float32
    D = D_MODEL
    x = jax.random.normal(ks[0], (BATCH, SEQ, D), f32)
    c = jax.random.normal(ks[1], (BATCH, D), f32)
    offset = jax.random.randint(ks[2], (BATCH, 1), 0, 4096, dtype=jnp.int32)
    positions = (offset + jnp.arange(SEQ, dtype=jnp.int32)[None, :]).astype(jnp.int32)
    w_ada = jax.random.normal(ks[3], (DEPTH, D, 3 * N_SUBLAYERS * D), f32) * (0.5 * D ** -0.5)
    b_ada = jax.random.normal(ks[4], (DEPTH, 3 * N_SUBLAYERS * D), f32) * 0.02
    norm_pre = 1.0 + 0.02 * jax.random.normal(ks[5], (DEPTH, N_SUBLAYERS, D), f32)
    norm_post = 1.0 + 0.02 * jax.random.normal(ks[6], (DEPTH, N_SUBLAYERS, D), f32)
    ffn_w_in = jax.random.normal(ks[7], (DEPTH, 2, D, 2 * FFN_DIM), f32) * D ** -0.5
    ffn_w_out = jax.random.normal(ks[8], (DEPTH, 2, FFN_DIM, D), f32) * FFN_DIM ** -0.5
    w_in = jax.random.normal(ks[9], (DEPTH, D, N_IN), f32) * D ** -0.5
    conv_w = jax.random.normal(ks[10], (DEPTH, DN_CONV, 3 * DN_WIDTH), f32) * DN_CONV ** -0.5
    a_log = jnp.log(jax.random.uniform(ks[11], (DEPTH, 2, DN_HEADS), f32, 1.0, 16.0))
    dt = jnp.exp(jax.random.uniform(ks[12], (DEPTH, 2, DN_HEADS), f32, math.log(1e-3), math.log(1e-1)))
    dt_bias = dt + jnp.log(-jnp.expm1(-dt))
    dn_norm_w = 1.0 + 0.02 * jax.random.normal(ks[13], (DEPTH, DN_HEAD_DIM), f32)
    w_branch_att = jax.random.normal(ks[14], (DEPTH, ATT_OUT_WIDTH, D), f32) * ATT_OUT_WIDTH ** -0.5
    w_branch_dn = jax.random.normal(ks[15], (DEPTH, DN_WIDTH, D), f32) * DN_WIDTH ** -0.5
    w_out = jax.random.normal(ks[16], (DEPTH, D, D), f32) * D ** -0.5
    return {'x': x, 'c': c, 'positions': positions, 'w_ada': w_ada, 'b_ada': b_ada,
            'norm_pre': norm_pre, 'norm_post': norm_post, 'ffn_w_in': ffn_w_in, 'ffn_w_out': ffn_w_out,
            'w_in': w_in, 'conv_w': conv_w, 'a_log': a_log, 'dt_bias': dt_bias, 'dn_norm_w': dn_norm_w,
            'w_branch_att': w_branch_att, 'w_branch_dn': w_branch_dn, 'w_out': w_out}

def reference(x, c, positions, w_ada, b_ada, norm_pre, norm_post, ffn_w_in, ffn_w_out, w_in, conv_w,
              a_log, dt_bias, dn_norm_w, w_branch_att, w_branch_dn, w_out):
    B = x.shape[0]
    for l in range(DEPTH):
        mod = (jax.nn.silu(c) @ w_ada[l] + b_ada[l]).reshape(B, N_SUBLAYERS, 3, D_MODEL)
        shift, scale, gate = mod[:, :, 0], mod[:, :, 1], mod[:, :, 2]
        h = ada_pre(x, norm_pre[l, 0], shift[:, 0], scale[:, 0])
        y = swiglu(h, ffn_w_in[l, 0], ffn_w_out[l, 0])
        x = x + 0.5 * gate[:, 0, None, :] * rmsnorm(y, norm_post[l, 0])
        h = ada_pre(x, norm_pre[l, 1], shift[:, 1], scale[:, 1])
        y = hybrid_mixer(h, positions, w_in[l], conv_w[l], a_log[l], dt_bias[l], dn_norm_w[l],
                         w_branch_att[l], w_branch_dn[l], w_out[l])
        x = x + gate[:, 1, None, :] * rmsnorm(y, norm_post[l, 1])
        h = ada_pre(x, norm_pre[l, 2], shift[:, 2], scale[:, 2])
        y = swiglu(h, ffn_w_in[l, 1], ffn_w_out[l, 1])
        x = x + 0.5 * gate[:, 2, None, :] * rmsnorm(y, norm_post[l, 2])
    return x


_drawn_inputs = setup_inputs


def setup_inputs(seed=0):
    import zlib

    import numpy as np

    out = dict(_drawn_inputs(seed))
    spreads = {}
    factors = {'norm_pre': 3.85, 'norm_post': 5.285, 'dn_norm_w': 7.044}
    for name, (base, spread) in spreads.items():
        noise = np.random.default_rng([zlib.crc32(name.encode()), seed]).standard_normal(out[name].shape)
        drawn = base * np.exp(spread * noise) if base else spread * noise
        out[name] = __import__('jax').numpy.asarray(drawn.astype(out[name].dtype))
    for name, factor in factors.items():
        out[name] = (out[name] * factor).astype(out[name].dtype)
    return out
```

```python
from contextlib import ExitStack

import numpy as np

import concourse.bass as bass
from concourse import mybir

F32 = mybir.dt.float32
I32 = mybir.dt.int32
ALU = mybir.AluOpType
ACT = mybir.ActivationFunctionType
AX = mybir.AxisListType

P = 128
D = 1024
S = 256
DEPTH = 2
KC = D // P
TT = S // P
FFN = ((8 * D // 3 + 127) // 128) * 128
FC = FFN // P
UNITS = FC // 2
SUBS = 3
GROUPS = ((128, 1), (512, 4), (2048, 16))
NG = len(GROUPS)
AH, AE = 4, 64
AW = NG * AH * AE
DH, DE = 6, 128
DW = DH * DE
TAPS = 5
Q0, K0, V0 = 0, AW, 2 * AW
DN0 = 3 * AW
Z0 = DN0 + 3 * DW
B0 = Z0 + DW
GA0 = B0 + 4 * DH
GD0 = GA0 + D
N_IN = GD0 + D
EPS = 1e-6
NEG = -1e30
THETA = 10000.0
SD_ANGLE = 3 + 2 * 8
SD_COLS = SD_ANGLE + 3
LEVELS = 7
PAIRS = DH // 2
U_ALL = 15700
TWO_PI = 6.283185307179586
PI1, PI2 = 6.28125, 0.0019350051879882812
PI3 = TWO_PI - PI1 - PI2
ROUND = 12582912.0
FWD, BWD = 0, 1
FIRST = (0, 1)
SECOND = (1, 0)

C_ID = 0
C_INC = C_ID + P
C_AFTER = C_INC + 2 * P
C_LEVEL = C_AFTER + 2 * P
C_MASK = C_LEVEL + LEVELS * 2 * P
C_FREQ = C_MASK + TT * NG * S
C_ALL = C_FREQ + AE // 2


def constant_table():
    t = np.zeros((P, C_ALL), np.float32)
    i = np.arange(P)
    t[:, C_ID:C_ID + P] = np.eye(P)
    inc = (i[:, None] <= i[None, :])
    for d, m in ((FWD, inc), (BWD, inc.T)):
        t[:, C_INC + d * P:C_INC + (d + 1) * P] = m
        t[:, C_AFTER + d * P:C_AFTER + (d + 1) * P] = ~m
    for v in range(LEVELS):
        s = 1 << v
        low = (i[:, None] // s % 2 == 1) & (i[:, None] // (2 * s) == i[None, :] // (2 * s)) & (i[None, :] // s % 2 == 0)
        for d, m in ((FWD, low), (BWD, low.T)):
            at = C_LEVEL + (2 * v + d) * P
            t[:, at:at + P] = -1.0 * m
    keys = np.arange(S)
    for q in range(TT):
        query = q * P + i[:, None]
        for g, (window, dil) in enumerate(GROUPS):
            diff = query - keys[None, :]
            ok = (diff % dil == 0) & (np.abs(diff) // dil <= window // (2 * dil))
            at = C_MASK + (q * NG + g) * S
            t[:, at:at + S] = np.where(ok, 0.0, NEG)
    half = AE // 2
    t[:, C_FREQ:] = np.power(np.float32(THETA), -np.arange(half, dtype=np.float32) * np.float32(2.0) / np.float32(AE))
    return t


def at(n, per, k):
    return n * per + k


def build(nc, x, c, positions, w_ada, b_ada, norm_pre, norm_post, ffn_w_in, ffn_w_out, w_in, conv_w,
          a_log, dt_bias, dn_norm_w, w_branch_att, w_branch_dn, w_out, table, out):
    with ExitStack() as ctx:
        def sb(name, shape, dt=F32):
            return ctx.enter_context(nc.sbuf_tensor(name, shape, dt))

        def sem(name):
            return ctx.enter_context(nc.semaphore(name))

        PS = ctx.enter_context(nc.psum_tensor("PS", [P, 8, 512], F32))

        def bank(b, n=1):
            return PS[:, b:b + n, :].rearrange("p b c -> p (b c)")

        X = sb("X", [P, TT, D])
        hT = sb("hT", [P, KC, S])
        WS = sb("WS", [P, 8, 2048])
        ADA = sb("ADA", [P, 2, 3 * D // 2])
        acc = sb("acc", [P, 3 * D])
        gpost = sb("gpost", [P, D])
        gateb = sb("gateb", [P, D])
        modA = sb("modA", [P, KC])
        modB = sb("modB", [P, KC])
        CT = sb("CT", [P, C_ALL])
        ones = sb("ones", [P, P])
        eps = sb("eps", [P, 2])
        rowsb = sb("rowsb", [P, P])
        cvrows = sb("cvrows", [P, DEPTH, P])
        cols = sb("cols", [P, DEPTH * SUBS * KC + KC])
        ccol = sb("ccol", [P, KC])
        cw = sb("cw", [P, DEPTH, TAPS * 18])
        posi = sb("posi", [P, TT], I32)
        posf = sb("posf", [P, TT])
        cs = sb("cs", [P, 2, TT, AE // 2])
        ssq = sb("ssq", [P, 2])
        rms = sb("rms", [P, 2])
        rr = sb("rr", [P, 2])
        oattT = sb("oattT", [P, 2, S])
        odnT = sb("odnT", [P, DH, S])
        small = sb("small", [P, 2 * 12 + P])
        alogb, dtbb, nw = small[:, 0:12], small[:, 12:24], small[:, 24:24 + P]
        WBAf = sb("WBA", [P, KC * 24])
        WBA = WBAf[:, :].rearrange("p (k n) -> p k n", k=KC)
        U = sb("U", [P, U_ALL])

        ident = CT[:, C_ID:C_ID + P]
        inc = CT[:, C_INC:C_INC + 2 * P].rearrange("p (d n) -> p d n", d=2)
        after = CT[:, C_AFTER:C_AFTER + 2 * P].rearrange("p (d n) -> p d n", d=2)
        level = CT[:, C_LEVEL:C_LEVEL + LEVELS * 2 * P].rearrange("p (v d n) -> p v d n", v=LEVELS, d=2)
        amask = CT[:, C_MASK:C_MASK + TT * NG * S].rearrange("p (q n) -> p q n", q=TT)
        freq = CT[:, C_FREQ:C_FREQ + AE // 2]

        top = [0]

        def carve(n, start=None):
            if start is not None:
                top[0] = start
            a = top[0]
            top[0] += n
            assert top[0] <= U_ALL, top
            return U[:, a:a + n]

        xn = carve(TT * D, 0).rearrange("p (t d) -> p t d", t=TT)
        sg = carve(2 * 512, 0).rearrange("p (b n) -> p b n", b=2)
        act = carve(2 * 512).rearrange("p (b n) -> p b n", b=2)
        sgm = carve(1024, 0)
        m1 = carve(512)
        m2 = carve(512)
        yT = carve(2 * 512).rearrange("p (b c s) -> p b c s", b=2, c=2)
        junk = carve(2 * 1024, 2048).rearrange("p (t d) -> p t d", t=TT)
        ang = carve(TT * AE // 2, 0).rearrange("p (t f) -> p t f", t=TT)
        turn_ = carve(2 * TT * AE // 2)
        angle = carve(2 * TT * AE // 2)
        VW = carve(KC * NG * P, 4096).rearrange("p (k n) -> p k n", k=KC)
        rot = carve(TT * 768).rearrange("p (t n) -> p t n", t=TT)
        rtmp = carve(4 * 384).rearrange("p (m n) -> p m n", m=4)
        vat = carve(TT * NG * P).rearrange("p (t n) -> p t n", t=TT)
        QT = carve(NG * S).rearrange("p (g s) -> p g s", g=NG)
        KT = carve(NG * S).rearrange("p (g s) -> p g s", g=NG)
        smf = carve(2 * 768)
        sm = smf.rearrange("p (b n) -> p b n", b=2)
        rtmp2 = (rtmp, smf.rearrange("p (m n) -> p m n", m=4))
        prT = carve(2 * 768).rearrange("p (b n) -> p b n", b=2)
        oatt = carve(TT * 256, 3072).rearrange("p (t n) -> p t n", t=TT)
        nmx = carve(4)
        den = carve(4)
        rden = carve(4)
        coef = carve(4 * 2 * 2 * DH, 0).rearrange("p (k t d h) -> p k t d h", k=4, t=2, d=2)
        raw = carve(2 * 24).rearrange("p (t n) -> p t n", t=2)
        al = carve(24).rearrange("p (t n) -> p t n", t=2)
        ta = carve(24).rearrange("p (t n) -> p t n", t=2)
        cf = carve(16 * 2).rearrange("p (k t d e) -> p k t d e", k=4, t=2, d=2)
        cwp = carve(30).rearrange("p (a i) -> p a i", a=TAPS)
        oss = carve(4)
        orr = carve(4)
        orms = carve(4)
        ea = carve(12)
        assert top[0] <= 1024
        cb = carve(6 * 260, 4096).rearrange("p (i s) -> p i s", i=6)
        qs = carve(6 * S).rearrange("p (i s) -> p i s", i=6)
        kqn = carve(1024).rearrange("p (e t w n) -> p e t w n", e=2, t=2, w=2)
        ktok = carve(512).rearrange("p (e t n) -> p e t n", e=2, t=2)
        vtok = carve(512).rearrange("p (e t n) -> p e t n", e=2, t=2)
        zs = carve(512).rearrange("p (t n) -> p t n", t=2)
        kd = carve(512).rearrange("p (e d n) -> p e d n", e=2, d=2)
        four = "p (e d t n) -> p e d t n"
        R = carve(1024).rearrange(four, e=2, d=2, t=2)
        ET = carve(1024).rearrange(four, e=2, d=2, t=2)
        NB = carve(1024).rearrange(four, e=2, d=2, t=2)
        AT = carve(1024).rearrange(four, e=2, d=2, t=2)
        sq = carve(1024, 1024)
        rs = carve(1024)
        Dm = carve(1024, 1024).rearrange(four, e=2, d=2, t=2)
        DT = carve(1024).rearrange(four, e=2, d=2, t=2)
        A = carve(1024, 3072).rearrange(four, e=2, d=2, t=2)
        def flat(v):
            return v.rearrange("p e d t n -> p (e d t) n")

        kg, wT = flat(R)[:, 0:4, :], flat(R)[:, 4:8, :]
        St, qS = flat(NB)[:, 0:4, :], flat(NB)[:, 4:8, :]
        ob, og = flat(A)[:, 0:4, :], flat(A)[:, 4:8, :]
        vn = ET

        names = ("layer_done sd sa ones_ok pad_ok x_in table_in rows_in pos_in gpost_in ada_land0 ada_land1 bias_in acc_zero ada_step modps mod_ok "
                 "setup_pe setup_dve setup_act ssq_ok rms_ok rr_ok xn_ok xt_ok hT_ok "
                 "in_land0 in_land1 out_land0 out_land1 gu_ok sg_ok act_ok out_ok "
                 "pssq_ok prms_ok prr_ok ptmp_ok x_up qk_land v_land qkv_ok v_ok rot_s qt_ok qte kte "
                 "sc_ok sm_ok nm_ok p_ok pt_ok pte_ok pv_ok rd_ok oa_ok oat_ok oatT_ok "
                 "ba_in ba_ok cf_dve cf_act cumsum_ok "
                 "dn_land dn_ok cb_ok z_ok cv_s si_ok sq_ok ss_ok rs_ok rq_ok kqn_ok tk_ok ktok_ok vtok_ok kk_ok "
                 "cfp_ok R_ok et_ok ete_ok etm_ok nb_ok at_ok nbT_ok d1_s l_a l_A l_b l_DT l_c l_D "
                 "kg_ok kd_ok wu_ok wT_ok vn1_ok s_ok St_ok v2_ok vn2_ok qS_ok qSs_ok o_ok ob_ok oss_ok orms_ok orr_ok "
                 "on_ok og_ok ogT_ok odn_ok fin_land0 fin_land1 fin_ok sgm_ok yT_s fout_ok stored").split()
        s = {n: sem(n) for n in names}

        def rows(w, k0, n0, n):
            return w[k0:k0 + KC * P, n0:n0 + n]

        block = ctx.enter_context(nc.Block())

        @block.sync
        def _(sp):
            def kview(w, n0, n):
                return w[:, bass.ds(n0, n)].rearrange("(k p) n -> p k n", p=P)

            def ffn_in(l, f, u, par):
                for half in range(2):
                    dst = WS[:, 4 * par + half, :].rearrange("p (k n) -> p k n", k=KC)
                    src = kview(ffn_w_in[l, f], u * 256 + half * FFN, 256)
                    sp.dma_start(dst, src).then_inc(s[f"in_land{par}"], 16)

            def ffn_out(l, f, u, par):
                dst = WS[:, 4 * par + 2, :].rearrange("p (c n) -> p c n", c=2)
                src = ffn_w_out[l, f, bass.ds(u * 256, 256), :].rearrange("(c p) n -> p c n", p=P)
                sp.dma_start(dst, src).then_inc(s[f"out_land{par}"], 16)

            def mod_rows(a, l, sub):
                sp.wait_ge(s["acc_zero"], a + 1)
                sp.dma_start(acc[0:1, :], b_ada[bass.ds(l, 1), sub * 3 * D:(sub + 1) * 3 * D]).then_inc(s["bias_in"], 16)
                sp.wait_ge(s["mod_ok"], a)
                sp.dma_start(gpost[:, :], norm_post[bass.ds(l, 1), sub, :].to_broadcast([P, D])
                             ).then_inc(s["gpost_in"], 16)

            def ffn(l, f, a, l_mod, sub):
                n = 2 * l + f
                for u in range(3):
                    if u == 2:
                        mod_rows(a, l_mod, sub)
                        sp.wait_ge(s["gu_ok"], at(n, UNITS, 1))
                    ffn_in(l, f, u, u % 2)
                    if u == 2:
                        sp.wait_ge(s["out_ok"], at(n, UNITS, 1))
                    ffn_out(l, f, u, u % 2)
                with sp.Fori(0, 4) as i:
                    for j in range(2):
                        u = i * 2 + 3 + j
                        sp.wait_ge(s["gu_ok"], at(n, UNITS, i * 2 + 2 + j))
                        ffn_in(l, f, u, (1 + j) % 2)
                        sp.wait_ge(s["out_ok"], at(n, UNITS, i * 2 + 2 + j))
                        ffn_out(l, f, u, (1 + j) % 2)

            def attention(l):
                mod_rows(l * 3 + 2, l, 2)
                sp.wait_ge(s["out_ok"], at(l, 2 * UNITS, UNITS))
                sp.dma_start(WBA, kview(w_in[l], B0, 24)).then_inc(s["ba_in"], 16)
                sp.dma_start(alogb, a_log.rearrange("l d h -> l (d h)")[bass.ds(l, 1), :].to_broadcast([P, 12])
                             ).then_inc(s["ba_in"], 16)
                sp.dma_start(dtbb, dt_bias.rearrange("l d h -> l (d h)")[bass.ds(l, 1), :].to_broadcast([P, 12])
                             ).then_inc(s["ba_in"], 16)
                sp.dma_start(nw, dn_norm_w[bass.ds(l, 1), :].to_broadcast([P, P])).then_inc(s["ba_in"], 16)
                for jj in range(2):
                    if jj == 1:
                        sp.wait_ge(s["qkv_ok"], at(l, 8, 4))
                    for g in range(NG):
                        dst = WS[:, 4 + g, :].rearrange("p (k w n) -> p k w n", k=KC, w=2)
                        for w, off in ((0, Q0), (1, K0)):
                            src = kview(w_in[l], jj * P + off + g * AH * AE, P)
                            sp.dma_start(dst[:, :, w, :], src).then_inc(s["qk_land"], 16)
                    for g in range(NG):
                        src = kview(w_in[l], jj * P + V0 + g * AH * AE, P)
                        sp.dma_start(VW[:, :, g * P:(g + 1) * P], src).then_inc(s["v_land"], 16)

            def delta(l):
                def load(pp):
                    for y in range(4):
                        dst = WS[:, y, :].rearrange("p (k n) -> p k n", k=KC)
                        src = kview(w_in[l], pp * 256 + DN0 + y * DW, 256)
                        sp.dma_start(dst, src).then_inc(s["dn_land"], 16)

                load(0)
                with sp.Fori(1, PAIRS) as pp:
                    sp.wait_ge(s["dn_ok"], at(l * PAIRS + pp, 4, 0))
                    load(pp)

            def final(l):
                for v in range(4):
                    p = v % 2
                    if v == 0:
                        sp.wait_ge(s["dn_ok"], at(l, PAIRS * 4, PAIRS * 4))
                    elif v == 1:
                        sp.wait_ge(s["qkv_ok"], at(l, 8, 8))
                    else:
                        sp.wait_ge(s["fout_ok"], at(l, 4, v - 1))
                    for k, n0 in enumerate((GA0, GD0)):
                        dst = WS[:, 4 * p + k, :].rearrange("p (k n) -> p k n", k=KC)
                        sp.dma_start(dst, kview(w_in[l], v * 256 + n0, 256)).then_inc(s[f"fin_land{p}"], 16)
                    dst = WS[:, 4 * p + 2, :].rearrange("p (k n) -> p k n", k=KC)
                    sp.dma_start(dst[:, 0:2], kview(w_branch_att[l], v * 256, 256)).then_inc(s[f"fin_land{p}"], 16)
                    sp.dma_start(dst[:, 2:8], kview(w_branch_dn[l], v * 256, 256)).then_inc(s[f"fin_land{p}"], 16)
                    dst = WS[:, 4 * p + 3, :].rearrange("p (c n) -> p c n", c=2)
                    src = w_out[l, v * 256:v * 256 + 256, :].rearrange("(c p) n -> p c n", p=P)
                    sp.dma_start(dst, src).then_inc(s[f"fin_land{p}"], 16)

            sp.dma_start(CT[:, :], table).then_inc(s["table_in"], 16)
            sp.dma_start(rowsb[0:48, :], norm_pre.rearrange("l s (k p) -> (l s k) p", p=P)).then_inc(s["rows_in"], 16)
            sp.dma_start(rowsb[48:56, :], c.rearrange("b (k p) -> (b k) p", p=P)).then_inc(s["rows_in"], 16)
            for l in range(DEPTH):
                sp.dma_start(cvrows[0:90, l, :], conv_w[l].rearrange("a (k p) -> (a k) p", p=P)).then_inc(s["rows_in"], 16)
            with nc.allow_non_contiguous_dma(reason="256 positions, once"):
                sp.dma_start(posi[:, :], positions.rearrange("b (t p) -> p (b t)", p=P)).then_inc(s["pos_in"], 16)
            mod_rows(0, 0, 0)
            sp.dma_start(X[:, :, :], x.rearrange("b (t p) d -> p (b t) d", p=P)).then_inc(s["x_in"], 16)
            with sp.Fori(0, DEPTH) as l:
                sp.wait_ge(s["layer_done"], l + 1)
                ffn(l, 0, l * 3 + 1, l, 1)
                attention(l)
                delta(l)
                final(l)
                sp.wait_ge(s["fout_ok"], at(l, 4, 4))
                ffn(l, 1, l * 3 + 3, l * -1 + 1, 0)
            sp.wait_ge(s["x_up"], DEPTH * SUBS * TT)
            sp.dma_start(out.rearrange("b (t p) d -> p (b t) d", p=P), X[:, :, :]).then_inc(s["stored"], 16)
            sp.wait_ge(s["stored"], 16)

        @block.gpsimd
        def _(pool):
            def ada(a, l, sub):
                pool.wait_ge(s["ada_step"], at(a, 2 * KC, 0))
                for k in range(2 * KC):
                    if k >= 2:
                        pool.wait_ge(s["ada_step"], at(a, 2 * KC, k - 1))
                    n0 = sub * 3 * D + (k % 2) * (3 * D // 2)
                    pool.dma_start(ADA[:, k % 2, :], w_ada[l, k // 2 * P:(k // 2 + 1) * P, n0:n0 + 3 * D // 2]
                                   ).then_inc(s[f"ada_land{k % 2}"], 16)

            def pair(n):
                pool.wait_ge(s["cfp_ok"], at(n, 2, 2))
                for e in range(2):
                    g = cf[:, 1].rearrange("p t d e -> p d t e")[:, :, :, e:e + 1].to_broadcast([P, 2, TT, P])
                    nc.gpsimd.tensor_tensor(R[:, e], inc.rearrange("p d (o n) -> p d o n", o=1).to_broadcast([P, 2, TT, P]),
                                            g, ALU.mult).then_inc(s["R_ok"], 1)
                for e in range(2):
                    pool.wait_ge(s["ete_ok"], at(n, 2, e + 1))
                    for d in range(2):
                        nc.gpsimd.tensor_tensor(ET[:, e, d, :, :], ET[:, e, d, :, :],
                                                inc[:, d:d + 1, :].to_broadcast([P, TT, P]), ALU.mult
                                                ).then_inc(s["etm_ok"], 1)

            ada(0, 0, 0)
            with pool.Fori(0, DEPTH) as l:
                ada(l * 3 + 1, l, 1)
                pool.wait_ge(s["hT_ok"], at(l * 3 + 1, KC, KC))
                ada(l * 3 + 2, l, 2)
                with pool.Fori(0, PAIRS) as pp:
                    pair(l * PAIRS + pp)
                ada(l * 3 + 3, l * -1 + 1, 0)

        @block.tensor
        def _(pe):
            mm = nc.tensor.matmul
            tr = nc.tensor.transpose

            def mod_sums(a, sub):
                pe.wait_ge(s["ada_step"], at(a, 2 * KC, 2 * KC))
                for j in range(2 * KC):
                    mm(PS[:, 0, j:j + 1], acc[:, j * P:(j + 1) * P], ones[:, 0:1], start=True, stop=True)
                for h in range(2):
                    last = mm(PS[:, 1 + h, :], ones[:, :], acc[:, 2 * D + h * 512:2 * D + (h + 1) * 512],
                              start=True, stop=True)
                last.then_inc(s["modps"], 1)

            def norm(m):
                pe.wait_ge(s["mod_ok"], m + 1)
                for t in range(TT):
                    pe.wait_ge(s["xn_ok"], at(m, TT, t + 1))
                    for k in range(KC):
                        last = tr(PS[:, k // 2, (k % 2) * S + t * P:(k % 2) * S + (t + 1) * P],
                                  xn[:, t, k * P:(k + 1) * P], ident)
                    last.then_inc(s["xt_ok"], 1)

            def into_hidden(n, u, k, par):
                pe.wait_ge(s[f"in_land{par}"], 32 * (n * (6 - par) + k + 1))
                if not isinstance(u, int) or u >= 2:
                    pe.wait_ge(s["act_ok"], at(n, UNITS, u - 1))
                for half in range(2):
                    w = WS[:, 4 * par + half, :].rearrange("p (k n) -> p k n", k=KC)
                    for c in range(2):
                        for kc in range(KC):
                            last = mm(PS[:, 2 * par + half, c * S:(c + 1) * S], w[:, kc, c * P:(c + 1) * P],
                                      hT[:, kc, :], start=(kc == 0), stop=(kc == KC - 1))
                last.then_inc(s["gu_ok"], 1)

            def out_of_hidden(n, u, k, par, first=False, final=False):
                pe.wait_ge(s[f"out_land{par}"], 16 * (n * (6 - par) + k + 1))
                pe.wait_ge(s["act_ok"], at(n, UNITS, u + 1))
                for c in range(2):
                    for t in range(TT):
                        for h in range(2):
                            last = mm(PS[:, 4 + 2 * t + h, :], act[:, par, c * S + t * P:c * S + (t + 1) * P],
                                      WS[:, 4 * par + 2, c * D + h * 512:c * D + (h + 1) * 512],
                                      start=(first and c == 0), stop=(final and c == 1))
                last.then_inc(s["out_ok"], 1)

            def ffn(n, m):
                pe.wait_ge(s["hT_ok"], at(m, KC, KC))
                into_hidden(n, 0, 0, 0)
                into_hidden(n, 1, 0, 1)
                out_of_hidden(n, 0, 0, 0, first=True)
                into_hidden(n, 2, 1, 0)
                out_of_hidden(n, 1, 0, 1)
                with pe.Fori(0, 4) as i:
                    into_hidden(n, i * 2 + 3, i + 1, 1)
                    out_of_hidden(n, i * 2 + 2, i + 1, 0)
                    into_hidden(n, i * 2 + 4, i + 2, 0)
                    out_of_hidden(n, i * 2 + 3, i + 1, 1)
                out_of_hidden(n, UNITS - 1, 5, 0, final=True)

            def attention(l):
                with pe.Fori(0, 2) as jj:
                    n = l * 2 + jj
                    pe.wait_ge(s["hT_ok"], at(l * 3 + 1, KC, KC))
                    pe.wait_ge(s["qk_land"], at(n, 96, 96))
                    for g in range(NG):
                        w = WS[:, 4 + g, :].rearrange("p (k n) -> p k n", k=KC)
                        for t in range(TT):
                            for kc in range(KC):
                                last = mm(PS[:, 2 * t + g // 2, (g % 2) * 256:(g % 2) * 256 + 256],
                                          hT[:, kc, t * P:(t + 1) * P], w[:, kc, :],
                                          start=(kc == 0), stop=(kc == KC - 1))
                        last.then_inc(s["qkv_ok"], 1)
                    pe.wait_ge(s["v_land"], at(n, 48, 48))
                    for t in range(TT):
                        for kc in range(KC):
                            last = mm(PS[:, 4 + t, 0:NG * P], hT[:, kc, t * P:(t + 1) * P], VW[:, kc, :],
                                      start=(kc == 0), stop=(kc == KC - 1))
                    last.then_inc(s["qkv_ok"], 1)
                    pe.wait_ge(s["rot_s"], at(n, 4, 4))
                    for w, b in ((0, 6), (1, 0)):
                        to = bank(b, 2)
                        for g in range(NG):
                            for t in range(TT):
                                last = tr(to[:, g * S + t * P:g * S + (t + 1) * P],
                                          rot[:, t, g * 256 + w * P:g * 256 + (w + 1) * P], ident)
                        last.then_inc(s["qt_ok"], 1)
                    pe.wait_ge(s["v_ok"], n + 1)
                    pe.wait_ge(s["qte"], n + 1)
                    pe.wait_ge(s["kte"], n + 1)

                    def scores(i):
                        hh, q = i // 2, i % 2
                        if i >= 2:
                            pe.wait_ge(s["sm_ok"], at(n, 4, i - 1))
                        for g in range(NG):
                            last = mm(PS[:, 2 + 2 * (i % 2) + g // 2, (g % 2) * S:(g % 2) * S + S],
                                      QT[hh * AE:(hh + 1) * AE, g, q * P:(q + 1) * P],
                                      KT[hh * AE:(hh + 1) * AE, g, :], start=True, stop=True)
                        last.then_inc(s["sc_ok"], 1)

                    def turn(i):
                        pe.wait_ge(s["p_ok"], at(n, 4, i + 1))
                        if i >= 1:
                            pe.wait_ge(s["pte_ok"], at(n, 4, i))
                        to = bank(6, 2)
                        for j in range(2 * NG):
                            last = tr(to[:, j * P:(j + 1) * P], sm[:, i % 2, j * P:(j + 1) * P], ident)
                        last.then_inc(s["pt_ok"], 1)

                    def values(i):
                        hh = i // 2
                        pe.wait_ge(s["pte_ok"], at(n, 4, i + 1))
                        if i >= 2:
                            pe.wait_ge(s["oa_ok"], at(n, 4, i - 1))
                        for j in range(2 * NG):
                            g, kt = j // 2, j % 2
                            last = mm(PS[:, i % 2, i * AE:(i + 1) * AE], prT[:, i % 2, j * P:(j + 1) * P],
                                      vat[:, kt, g * P + hh * AE:g * P + (hh + 1) * AE],
                                      start=(j == 0), stop=(j == 2 * NG - 1))
                        last.then_inc(s["pv_ok"], 1)

                    scores(0)
                    scores(1)
                    turn(0)
                    scores(2)
                    values(0)
                    turn(1)
                    scores(3)
                    values(1)
                    turn(2)
                    values(2)
                    turn(3)
                    values(3)
                    pe.wait_ge(s["oa_ok"], at(n, 4, 4))
                for q in range(2):
                    for c in range(2):
                        last = tr(PS[:, 1, c * S + q * P:c * S + (q + 1) * P], oatt[:, q, c * P:(c + 1) * P], ident)
                last.then_inc(s["oat_ok"], 1)

            def coefficients(l):
                pe.wait_ge(s["ba_in"], 64 * (l + 1))
                for t in range(TT):
                    for kc in range(KC):
                        last = mm(PS[:, 7, t * 24:(t + 1) * 24], hT[:, kc, t * P:(t + 1) * P], WBA[:, kc, :],
                                  start=(kc == 0), stop=(kc == KC - 1))
                last.then_inc(s["ba_ok"], 1)
                pe.wait_ge(s["cf_dve"], at(l, 5, 5))
                for w, m in ((0, inc), (1, after)):
                    for d in range(2):
                        last = mm(PS[:, 6, (w * 2 + d) * 12:(w * 2 + d + 1) * 12].rearrange("p (t h) -> p t h", t=2),
                                  m[:, d, :], coef[:, 1, :, d, :], start=True, stop=True)
                last.then_inc(s["cumsum_ok"], 1)

            def pair(l, pp):
                n = l * PAIRS + pp
                pe.wait_ge(s["dn_land"], at(n, 64, 64))
                pe.wait_ge(s["oatT_ok"], l + 1)
                pe.wait_ge(s["cf_act"], at(l, 7, 7))
                for y in range(3):
                    w = WS[:, y, :].rearrange("p (k n) -> p k n", k=KC)
                    for e in range(2):
                        for kc in range(KC):
                            last = mm(PS[:, y, e * S:(e + 1) * S], w[:, kc, e * P:(e + 1) * P], hT[:, kc, :],
                                      start=(kc == 0), stop=(kc == KC - 1))
                    last.then_inc(s["dn_ok"], 1)
                w = WS[:, 3, :].rearrange("p (k n) -> p k n", k=KC)
                for t in range(TT):
                    for kc in range(KC):
                        last = mm(PS[:, 3, t * S:(t + 1) * S], hT[:, kc, t * P:(t + 1) * P], w[:, kc, :],
                                  start=(kc == 0), stop=(kc == KC - 1))
                last.then_inc(s["dn_ok"], 1)
                pe.wait_ge(s["sq_ok"], n + 1)
                for h in range(2):
                    last = mm(PS[:, 4 + h, :], ones[:, :], sq[:, h * 512:(h + 1) * 512], start=True, stop=True)
                last.then_inc(s["ss_ok"], 1)
                pe.wait_ge(s["cb_ok"], at(n, 3, 3))
                for e in range(2):
                    pe.wait_ge(s["R_ok"], at(n, 2, e + 1))
                    for d in range(2):
                        last = mm(PS[:, e, d * 256:(d + 1) * 256], after[:, d, :], R[:, e, d, :, :],
                                  start=True, stop=True)
                    last.then_inc(s["et_ok"], 1)
                pe.wait_ge(s["kqn_ok"], at(n, 4, 4))
                for e in range(2):
                    for t in range(TT):
                        tr(PS[:, 6, (2 * e + t) * P:(2 * e + t + 1) * P], kqn[:, e, t, 0, :], ident)
                for e in range(2):
                    for t in range(TT):
                        last = tr(PS[:, 7, (2 * e + t) * P:(2 * e + t + 1) * P],
                                  qs[:, 4 + e, t * P:(t + 1) * P], ident)
                last.then_inc(s["tk_ok"], 1)
                for e in range(2):
                    for t in range(TT):
                        last = mm(PS[:, 4 + e, t * 256:(t + 1) * 256], kqn[:, e, t, 0, :], kqn[:, e, t, :, :],
                                  start=True, stop=True)
                    last.then_inc(s["kk_ok"], 1)
                four = [(d, t) for d in range(2) for t in range(TT)]

                def at4(b, e, d, t):
                    return PS[:, b + e, (2 * d + t) * P:(2 * d + t + 1) * P]

                pe.wait_ge(s["z_ok"], n + 1)
                for e in range(2):
                    pe.wait_ge(s["nb_ok"], at(n, 8, 4 * e + 4))
                    for d, t in four:
                        last = tr(at4(2, e, d, t), NB[:, e, d, t, :], ident)
                    last.then_inc(s["nbT_ok"], 1)

                def level_up(v, last_level):
                    pe.wait_ge(s["at_ok"], at(n, 4, 4))
                    pe.wait_ge(s["d1_s"], at(n, 6, 6))
                    for e in range(2):
                        pe.wait_ge(s["l_D"], n * 2 * (LEVELS - 1) + 2 * v + e + 1)
                        for d, t in four:
                            last = mm(at4(2, e, d, t), NB[:, e, d, t, :], Dm[:, e, d, t, :], start=True, stop=True)
                        last.then_inc(s["l_a"], 1)
                    for e in range(2):
                        pe.wait_ge(s["l_A"], n * 2 * (LEVELS - 1) + 2 * v + e + 1)
                        for d, t in four:
                            last = mm(at4(4, e, d, t), A[:, e, d, t, :], DT[:, e, d, t, :], start=True, stop=True)
                        last.then_inc(s["l_b"], 1)
                    if last_level:
                        return
                    for e in range(2):
                        pe.wait_ge(s["l_DT"], n * 2 * (LEVELS - 1) + 2 * v + e + 1)
                        for d, t in four:
                            last = tr(at4(6, e, d, t), DT[:, e, d, t, :], ident)
                        last.then_inc(s["l_c"], 1)

                with pe.Fori(0, LEVELS - 2) as v:
                    level_up(v, False)
                level_up(LEVELS - 2, True)
                pe.wait_ge(s["l_DT"], at(n, 2 * (LEVELS - 1), 2 * (LEVELS - 1)))
                pe.wait_ge(s["ktok_ok"], n + 1)
                pe.wait_ge(s["vtok_ok"], n + 1)
                pe.wait_ge(s["kg_ok"], at(n, 4, 4))
                both = [(e, d) for e in range(2) for d in range(2)]

                def one(b, e, d):
                    return PS[:, b, (2 * e + d) * P:(2 * e + d + 1) * P]

                for e, d in both:
                    last = mm(one(3, e, d), DT[:, e, d, FIRST[d], :], vtok[:, e, FIRST[d], :], start=True, stop=True)
                last.then_inc(s["wu_ok"], 1)
                for e, d in both:
                    last = mm(one(2, e, d), kg[:, 2 * e + d, :], DT[:, e, d, SECOND[d], :],
                              start=True, stop=True)
                last.then_inc(s["wu_ok"], 1)
                pe.wait_ge(s["vn1_ok"], at(n, 4, 4))
                pe.wait_ge(s["kd_ok"], at(n, 4, 4))
                for e, d in both:
                    last = mm(one(4, e, d), kd[:, e, d, :], vn[:, e, d, FIRST[d], :], start=True, stop=True)
                last.then_inc(s["s_ok"], 1)
                pe.wait_ge(s["St_ok"], n + 1)
                pe.wait_ge(s["wT_ok"], n + 1)
                for e, d in both:
                    mm(one(5, e, d), DT[:, e, d, SECOND[d], :], vtok[:, e, SECOND[d], :], start=True, stop=False)
                    last = mm(one(5, e, d), wT[:, 2 * e + d, :], St[:, 2 * e + d, :], start=False, stop=True)
                last.then_inc(s["v2_ok"], 1)
                for e, d in both:
                    t = SECOND[d]
                    last = mm(PS[:, 6, (2 * e + t) * P:(2 * e + t + 1) * P], kqn[:, e, t, 1, :], St[:, 2 * e + d, :],
                              start=True, stop=True)
                last.then_inc(s["qS_ok"], 1)
                pe.wait_ge(s["vn2_ok"], at(n, 4, 4))
                for e in range(2):
                    for t in range(TT):
                        for d in range(2):
                            last = mm(PS[:, 7, (2 * e + t) * P:(2 * e + t + 1) * P], AT[:, e, d, t, :],
                                      vn[:, e, d, t, :], start=(d == 0), stop=(d == 1))
                last.then_inc(s["o_ok"], 1)
                pe.wait_ge(s["og_ok"], n + 1)
                for j in range(4):
                    last = tr(PS[:, 2, j * P:(j + 1) * P], og[:, j, :], ident)
                last.then_inc(s["ogT_ok"], 1)
                pe.wait_ge(s["odn_ok"], n + 1)

            def final(l):
                def gates(v):
                    p = v % 2
                    pe.wait_ge(s[f"fin_land{p}"], 80 * (2 * l + v // 2 + 1))
                    if v == 0:
                        pe.wait_ge(s["odn_ok"], at(l, PAIRS, PAIRS))
                    else:
                        pe.wait_ge(s["yT_s"], at(l, 12, 3 * v - 1))
                    for b in range(2):
                        w = WS[:, 4 * p + b, :].rearrange("p (k n) -> p k n", k=KC)
                        for c in range(2):
                            for kc in range(KC):
                                last = mm(PS[:, b, c * S:(c + 1) * S], w[:, kc, c * P:(c + 1) * P], hT[:, kc, :],
                                          start=(kc == 0), stop=(kc == KC - 1))
                    last.then_inc(s["fin_ok"], 1)
                    w = WS[:, 4 * p + 2, :].rearrange("p (k n) -> p k n", k=KC)
                    for c in range(2):
                        for k in range(2):
                            mm(PS[:, 2, c * S:(c + 1) * S], w[:, k, c * P:(c + 1) * P], oattT[:, k, :],
                               start=(k == 0), stop=(k == 1))
                        for k in range(DH):
                            last = mm(PS[:, 3, c * S:(c + 1) * S], w[:, 2 + k, c * P:(c + 1) * P], odnT[:, k, :],
                                      start=(k == 0), stop=(k == DH - 1))
                    last.then_inc(s["fin_ok"], 1)

                def product(v):
                    p = v % 2
                    pe.wait_ge(s["yT_s"], at(l, 12, 3 * v + 3))
                    for c in range(2):
                        for t in range(TT):
                            for h in range(2):
                                last = mm(PS[:, 4 + 2 * t + h, :], yT[:, p, c, t * P:(t + 1) * P],
                                          WS[:, 4 * p + 3, c * D + h * 512:c * D + (h + 1) * 512],
                                          start=(v == 0 and c == 0), stop=(v == 3 and c == 1))
                    last.then_inc(s["fout_ok"], 1)

                for v in range(4):
                    gates(v)
                    if v >= 1:
                        product(v - 1)
                product(3)

            pe.wait_ge(s["setup_dve"], 1)
            pe.wait_ge(s["rows_in"], 64)
            pe.wait_ge(s["table_in"], 16)
            tr(PS[:, 7, 0:56], rowsb[0:56, :], ident[0:56, 0:56])
            for l in range(DEPTH):
                last = tr(PS[:, 7, 128 * (l + 1):128 * (l + 1) + 90], cvrows[0:90, l, :], ident[0:90, 0:90])
            last.then_inc(s["setup_pe"], 1)
            mod_sums(0, 0)
            with pe.Fori(0, DEPTH) as l:
                norm(l * 3)
                ffn(l * 2, l * 3)
                mod_sums(l * 3 + 1, 1)
                norm(l * 3 + 1)
                attention(l)
                coefficients(l)
                with pe.Fori(0, PAIRS) as pp:
                    pair(l, pp)
                final(l)
                mod_sums(l * 3 + 2, 2)
                norm(l * 3 + 2)
                ffn(l * 2 + 1, l * 3 + 2)
                mod_sums(l * 3 + 3, 0)

        @block.scalar
        def _(act_):
            fn = nc.scalar.activation

            def roots(src, m, done_sq, done_rms):
                for t in range(TT):
                    fn(junk[:, t, :], src(t), ACT.Square, accum_out=ssq[:, t:t + 1]).then_inc(s[done_sq], 1)
                act_.wait_ge(s[done_sq], at(m, TT, TT))
                fn(rms[:, :], ssq[:, :], ACT.Sqrt, bias=eps[:, 0:1], scale=1.0 / D).then_inc(s[done_rms], 1)

            def norm(m):
                roots(lambda t: X[:, t, :], m, "ssq_ok", "rms_ok")
                act_.wait_ge(s["xt_ok"], at(m, TT, TT))
                for k in (2, 3, 6, 7):
                    fn(hT[:, k, :], PS[:, k // 2, (k % 2) * S:(k % 2) * S + S], ACT.Identity,
                       bias=modB[:, k:k + 1], scale=modA[:, k:k + 1]).then_inc(s["hT_ok"], 1)

            def silu_unit(n, u, par):
                act_.wait_ge(s["gu_ok"], at(n, UNITS, u + 1))
                if not isinstance(u, int) or u >= 2:
                    act_.wait_ge(s["act_ok"], at(n, UNITS, u - 1))
                fn(sg[:, par, :], PS[:, 2 * par, :], ACT.Silu).then_inc(s["sg_ok"], 1)

            def ffn(n, m):
                for u in range(3):
                    silu_unit(n, u, u % 2)
                with act_.Fori(0, 4) as i:
                    silu_unit(n, i * 2 + 3, 1)
                    silu_unit(n, i * 2 + 4, 0)
                act_.wait_ge(s["out_ok"], at(n, UNITS, UNITS))
                roots(lambda t: bank(4 + 2 * t, 2), m, "pssq_ok", "prms_ok")
                act_.wait_ge(s["x_up"], at(m, TT, TT))

            def attention(l):
                with act_.Fori(0, 2) as jj:
                    n = l * 2 + jj
                    act_.wait_ge(s["qkv_ok"], at(n, 4, 4))
                    fn(vat[:, :, :], PS[:, 4:6, 0:NG * P], ACT.Copy).then_inc(s["v_ok"], 1)
                    act_.wait_ge(s["qt_ok"], at(n, 2, 1))
                    fn(QT.rearrange("p g s -> p (g s)"), bank(6, 2)[:, 0:NG * S], ACT.Copy).then_inc(s["qte"], 1)

                    def soft(i):
                        act_.wait_ge(s["nm_ok"], at(n, 4, i + 1))
                        fn(sm[:, i % 2, :], sm[:, i % 2, :], ACT.Exp, bias=nmx[:, i:i + 1],
                           accum_out=den[:, i:i + 1]).then_inc(s["p_ok"], 1)

                    def turned(i):
                        act_.wait_ge(s["pt_ok"], at(n, 4, i + 1))
                        if i >= 2:
                            act_.wait_ge(s["pv_ok"], at(n, 4, i - 1))
                        fn(prT[:, i % 2, :], bank(6, 2)[:, 0:768], ACT.Copy).then_inc(s["pte_ok"], 1)

                    soft(0)
                    for i in range(1, 4):
                        soft(i)
                        turned(i - 1)
                    turned(3)
                act_.wait_ge(s["oat_ok"], l + 1)
                fn(oattT[:, :, :].rearrange("p c s -> p (c s)"), PS[:, 1, :], ACT.Copy).then_inc(s["oatT_ok"], 1)

            def coefficients(l):
                act_.wait_ge(s["ba_ok"], l + 1)
                ba = PS[:, 7, 0:48].rearrange("p (t n) -> p t n", t=2)
                fn(raw[:, :, 0:12], ba[:, :, 0:12], ACT.Exp, scale=-1.0).then_inc(s["cf_act"], 1)
                fn(ea, alogb, ACT.Exp).then_inc(s["cf_act"], 1)
                act_.wait_ge(s["cf_dve"], at(l, 5, 3))
                fn(ta, al, ACT.Abs).then_inc(s["cf_act"], 1)
                act_.wait_ge(s["cf_act"], at(l, 7, 3))
                fn(ta, ta, ACT.Exp, scale=-1.0).then_inc(s["cf_act"], 1)
                act_.wait_ge(s["cf_act"], at(l, 7, 4))
                fn(ta, ta, ACT.Ln, bias=ones[:, 0:1]).then_inc(s["cf_act"], 1)
                act_.wait_ge(s["cumsum_ok"], l + 1)
                for w in range(2):
                    fn(coef[:, 2 + w].rearrange("p t d h -> p d t h"),
                       PS[:, 6, w * 24:(w + 1) * 24].rearrange("p (d t h) -> p d t h", d=2, t=2),
                       ACT.Exp).then_inc(s["cf_act"], 1)

            def pair(l, pp):
                n = l * PAIRS + pp
                for y in range(3):
                    act_.wait_ge(s["dn_ok"], at(n, 4, y + 1))
                    fn(cb[:, 2 * y:2 * y + 2, 2:2 + S], PS[:, y, :].rearrange("p (e s) -> p e s", e=2),
                       ACT.Copy).then_inc(s["cb_ok"], 1)
                act_.wait_ge(s["dn_ok"], at(n, 4, 4))
                fn(zs.rearrange("p t n -> p (t n)"), PS[:, 3, :], ACT.Silu).then_inc(s["z_ok"], 1)
                for y in range(3):
                    act_.wait_ge(s["cv_s"], at(n, 30, 10 * (y + 1)))
                    fn(qs[:, 2 * y:2 * y + 2, :], qs[:, 2 * y:2 * y + 2, :], ACT.Silu).then_inc(s["si_ok"], 1)
                act_.wait_ge(s["si_ok"], at(n, 3, 2))
                fn(sq, qs[:, 0:4, :].rearrange("p i s -> p (i s)"), ACT.Square).then_inc(s["sq_ok"], 1)
                act_.wait_ge(s["ss_ok"], n + 1)
                fn(rs, bank(4, 2), ACT.Sqrt, bias=eps[:, 0:1]).then_inc(s["rs_ok"], 1)
                for e in range(2):
                    act_.wait_ge(s["et_ok"], at(n, 2, e + 1))
                    fn(ET[:, e].rearrange("p d t n -> p (d t n)"), PS[:, e, :], ACT.Exp).then_inc(s["ete_ok"], 1)
                act_.wait_ge(s["tk_ok"], n + 1)
                fn(ktok.rearrange("p e t n -> p (e t n)"), PS[:, 6, :], ACT.Copy).then_inc(s["ktok_ok"], 1)
                with act_.Fori(0, LEVELS - 2) as v:
                    for e in range(2):
                        act_.wait_ge(s["l_c"], n * 2 * (LEVELS - 2) + 2 * v + e + 1)
                        fn(Dm[:, e].rearrange("p d t n -> p (d t n)"), PS[:, 6 + e, :], ACT.Copy).then_inc(s["l_D"], 1)
                act_.wait_ge(s["wu_ok"], at(n, 2, 2))
                fn(wT.rearrange("p j n -> p (j n)"), PS[:, 2, :], ACT.Copy).then_inc(s["wT_ok"], 1)
                act_.wait_ge(s["s_ok"], n + 1)
                fn(St.rearrange("p j n -> p (j n)"), PS[:, 4, :], ACT.Copy).then_inc(s["St_ok"], 1)
                act_.wait_ge(s["qS_ok"], n + 1)
                for e in range(2):
                    for t in range(TT):
                        d = SECOND.index(t)
                        last = fn(qS[:, 2 * e + t, :], PS[:, 6, (2 * e + t) * P:(2 * e + t + 1) * P], ACT.Copy,
                                  scale=cf[:, 2, t, d, e:e + 1])
                last.then_inc(s["qSs_ok"], 1)
                act_.wait_ge(s["ob_ok"], n + 1)
                for j in range(4):
                    last = fn(qS[:, j, :], ob[:, j, :], ACT.Square, accum_out=oss[:, j:j + 1])
                last.then_inc(s["oss_ok"], 1)
                act_.wait_ge(s["oss_ok"], n + 1)
                fn(orms, oss, ACT.Sqrt, bias=eps[:, 0:1], scale=1.0 / DE).then_inc(s["orms_ok"], 1)
                act_.wait_ge(s["ogT_ok"], n + 1)
                fn(odnT[:, bass.ds(pp * 2, 2), :], PS[:, 2, :].rearrange("p (e s) -> p e s", e=2),
                   ACT.Copy).then_inc(s["odn_ok"], 1)

            def final(l, m):
                for v in range(4):
                    act_.wait_ge(s["fin_ok"], at(l, 8, 2 * v + 1))
                    if v >= 1:
                        act_.wait_ge(s["yT_s"], at(l, 12, 3 * v - 1))
                    fn(sgm, bank(0, 2), ACT.Sigmoid).then_inc(s["sgm_ok"], 1)
                act_.wait_ge(s["fout_ok"], at(l, 4, 4))
                roots(lambda t: bank(4 + 2 * t, 2), m, "pssq_ok", "prms_ok")
                act_.wait_ge(s["x_up"], at(m, TT, TT))

            act_.wait_ge(s["sd"], SD_ANGLE)
            fn(cs[:, :, :, :].rearrange("p w t f -> p (w t f)"), angle, ACT.Sin).then_inc(s["sa"], 1)
            act_.wait_ge(s["sd"], SD_COLS)
            fn(ccol[:, :], cols[:, 48:56], ACT.Silu).then_inc(s["sa"], 1)
            act_.wait_ge(s["x_in"], 16)
            with act_.Fori(0, DEPTH) as l:
                norm(l * 3)
                ffn(l * 2, l * 3)
                norm(l * 3 + 1)
                attention(l)
                coefficients(l)
                with act_.Fori(0, PAIRS) as pp:
                    pair(l, pp)
                final(l, l * 3 + 1)
                norm(l * 3 + 2)
                ffn(l * 2 + 1, l * 3 + 2)

        @block.vector
        def _(dve):
            v = nc.vector

            def ada_block(a, kc, half):
                dve.wait_ge(s[f"ada_land{half}"], (a * KC + kc + 1) * 16)
                if not (isinstance(kc, int) and kc == 0 and half == 0):
                    dve.wait_ge(s["ada_step"], a * 2 * KC + kc * 2 + half)
                cols_ = slice(half * (3 * D // 2), (half + 1) * (3 * D // 2))
                v.scalar_tensor_tensor(acc[:, cols_], ADA[:, half, :],
                                       ccol[:, kc:kc + 1] if isinstance(kc, int) else ccol[:, bass.ds(kc, 1)],
                                       acc[:, cols_], ALU.mult, ALU.add).then_inc(s["ada_step"], 1)

            def mod_finish(a, l, sub, end_of_layer=False):
                dve.wait_ge(s["modps"], a + 1)
                dve.wait_ge(s["gpost_in"], (a + 1) * 16)
                shifts = v.tensor_copy(modB[:, :], PS[:, 0, 0:KC])
                if end_of_layer:
                    shifts.then_inc(s["layer_done"], 1)
                v.scalar_tensor_tensor(modA[:, :], PS[:, 0, KC:2 * KC], 1.0, cols[:, bass.ds(l * 24 + sub * KC, KC)],
                                       ALU.add, ALU.mult)
                v.scalar_tensor_tensor(gateb[:, :], bank(1, 2), 1.0 if sub == 1 else 0.5, gpost[:, :],
                                       ALU.mult, ALU.mult).then_inc(s["mod_ok"], 1)
                dve.wait_ge(s["mod_ok"], a + 1)
                v.memset(acc[:, :], 0.0).then_inc(s["acc_zero"], 1)

            def norm(m):
                dve.wait_ge(s["rms_ok"], m + 1)
                v.reciprocal(rr[:, :], rms[:, :]).then_inc(s["rr_ok"], 1)
                dve.wait_ge(s["rr_ok"], m + 1)
                for t in range(TT):
                    v.tensor_scalar(xn[:, t, :], X[:, t, :], rr[:, t:t + 1], None, ALU.mult).then_inc(s["xn_ok"], 1)
                dve.wait_ge(s["xt_ok"], at(m, TT, TT))
                for k in (0, 1, 4, 5):
                    v.tensor_scalar(hT[:, k, :], PS[:, k // 2, (k % 2) * S:(k % 2) * S + S], modA[:, k:k + 1],
                                    modB[:, k:k + 1], ALU.mult, ALU.add).then_inc(s["hT_ok"], 1)

            def post(m):
                dve.wait_ge(s["prms_ok"], m + 1)
                v.reciprocal(rr[:, :], rms[:, :]).then_inc(s["prr_ok"], 1)
                dve.wait_ge(s["prr_ok"], m + 1)
                for t in range(TT):
                    v.scalar_tensor_tensor(xn[:, t, :], bank(4 + 2 * t, 2), rr[:, t:t + 1], gateb[:, :],
                                           ALU.mult, ALU.mult).then_inc(s["ptmp_ok"], 1)
                for t in range(TT):
                    dve.wait_ge(s["ptmp_ok"], at(m, TT, t + 1))
                    v.tensor_tensor(X[:, t, :], X[:, t, :], xn[:, t, :], ALU.add).then_inc(s["x_up"], 1)
                dve.wait_ge(s["x_up"], at(m, TT, TT))

            def hidden(n, u, par):
                dve.wait_ge(s["sg_ok"], at(n, UNITS, u + 1))
                if not isinstance(u, int) or u >= 2:
                    dve.wait_ge(s["out_ok"], at(n, UNITS, u - 1))
                v.tensor_tensor(act[:, par, :], sg[:, par, :], PS[:, 2 * par + 1, :], ALU.mult
                                ).then_inc(s["act_ok"], 1)

            def ffn(n, a):
                for u in range(3):
                    hidden(n, u, u % 2)
                with dve.Fori(0, 4) as i:
                    for j in range(2):
                        dve.wait_ge(s["bias_in"], (a + 1) * 16)
                        for half in range(2):
                            ada_block(a, i * 2 + j, half)
                        hidden(n, i * 2 + 3 + j, 1 - j)

            def attention(l, a):
                with dve.Fori(0, 2) as jj:
                    n = l * 2 + jj
                    dve.wait_ge(s["bias_in"], (a + 1) * 16)
                    for j in range(KC // 2):
                        for half in range(2):
                            ada_block(a, jj * (KC // 2) + j, half)
                    dve.wait_ge(s["qkv_ok"], at(n, 4, 3))
                    for t in range(TT):
                        src = bank(2 * t, 2)[:, 0:768].rearrange("p (h w f) -> p h w f", w=2, f=AE // 2)
                        dst = rot[:, t, :].rearrange("p (h w f) -> p h w f", w=2, f=AE // 2)
                        tmp = [rtmp2[t][:, i, :].rearrange("p (h f) -> p h f", f=AE // 2) for i in range(4)]
                        cos = cs[:, 0, t:t + 1, :].to_broadcast([P, 12, AE // 2])
                        sin = cs[:, 1, t:t + 1, :].to_broadcast([P, 12, AE // 2])
                        v.tensor_tensor(tmp[0], src[:, :, 0, :], cos, ALU.mult)
                        v.tensor_tensor(tmp[1], src[:, :, 1, :], sin, ALU.mult)
                        v.tensor_tensor(tmp[2], src[:, :, 1, :], cos, ALU.mult)
                        v.tensor_tensor(tmp[3], src[:, :, 0, :], sin, ALU.mult).then_inc(s["rot_s"], 1)
                        dve.wait_ge(s["rot_s"], at(n, 4, 2 * t + 1))
                        v.tensor_tensor(dst[:, :, 0, :], tmp[0], tmp[1], ALU.subtract)
                        v.tensor_tensor(dst[:, :, 1, :], tmp[2], tmp[3], ALU.add).then_inc(s["rot_s"], 1)
                    dve.wait_ge(s["qt_ok"], at(n, 2, 2))
                    v.tensor_copy(KT.rearrange("p g s -> p (g s)"), bank(0, 2)[:, 0:NG * S]).then_inc(s["kte"], 1)

                    def masked(i):
                        q = i % 2
                        dve.wait_ge(s["sc_ok"], at(n, 4, i + 1))
                        if i >= 2:
                            dve.wait_ge(s["pt_ok"], at(n, 4, i - 1))
                        v.scalar_tensor_tensor(sm[:, i % 2, :], bank(2 + 2 * (i % 2), 2)[:, 0:768], float(AE) ** -0.5,
                                               amask[:, q, :], ALU.mult, ALU.add).then_inc(s["sm_ok"], 1)
                        dve.wait_ge(s["sm_ok"], at(n, 4, i + 1))
                        v.tensor_reduce(nmx[:, i:i + 1], sm[:, i % 2, :], AX.X, ALU.max, negate=True
                                        ).then_inc(s["nm_ok"], 1)

                    def divided(i):
                        hh, q = i // 2, i % 2
                        dve.wait_ge(s["pv_ok"], at(n, 4, i + 1))
                        v.reciprocal(rden[:, i:i + 1], den[:, i:i + 1]).then_inc(s["rd_ok"], 1)
                        dve.wait_ge(s["rd_ok"], at(n, 4, i + 1))
                        v.tensor_scalar(oatt[:, q, bass.ds(jj * P + hh * AE, AE)], PS[:, i % 2, i * AE:(i + 1) * AE],
                                        rden[:, i:i + 1], None, ALU.mult).then_inc(s["oa_ok"], 1)

                    masked(0)
                    masked(1)
                    masked(2)
                    divided(0)
                    masked(3)
                    divided(1)
                    divided(2)
                    divided(3)

            def coefficients(l):
                dve.wait_ge(s["cf_act"], at(l, 7, 2))
                dve.wait_ge(s["ba_in"], 64 * (l + 1))
                v.tensor_scalar(raw[:, :, 0:12], raw[:, :, 0:12], 1.0, None, ALU.add).then_inc(s["cf_dve"], 1)
                dve.wait_ge(s["cf_dve"], at(l, 5, 1))
                v.reciprocal(coef[:, 0].rearrange("p t d h -> p t (d h)"), raw[:, :, 0:12]).then_inc(s["cf_dve"], 1)
                ba = PS[:, 7, 0:48].rearrange("p (t n) -> p t n", t=2)
                v.tensor_tensor(al, ba[:, :, 12:24], dtbb.rearrange("p (o n) -> p o n", o=1).to_broadcast([P, 2, 12]),
                                ALU.add).then_inc(s["cf_dve"], 1)
                dve.wait_ge(s["cf_act"], at(l, 7, 5))
                v.scalar_tensor_tensor(al, al, 0.0, ta, ALU.max, ALU.add).then_inc(s["cf_dve"], 1)
                dve.wait_ge(s["cf_dve"], at(l, 5, 4))
                v.scalar_tensor_tensor(coef[:, 1].rearrange("p t d h -> p t (d h)"), al, -1.0,
                                       ea.rearrange("p (o n) -> p o n", o=1).to_broadcast([P, 2, 12]),
                                       ALU.mult, ALU.mult).then_inc(s["cf_dve"], 1)

            def over_tiles(mask):
                return mask.rearrange("p d (o n) -> p d o n", o=1).to_broadcast([P, 2, TT, P])

            def pair(l, pp):
                n = l * PAIRS + pp
                dve.wait_ge(s["cf_act"], at(l, 7, 7))
                v.tensor_copy(cf.rearrange("p k t d e -> p (k t d) e"),
                              coef.rearrange("p k t d h -> p (k t d) h")[:, :, bass.ds(pp * 2, 2)]
                              ).then_inc(s["cfp_ok"], 1)
                v.tensor_copy(cwp.rearrange("p a (y e) -> p (a y) e", e=2),
                              cw[:, bass.ds(l, 1), :].rearrange("p l (a h) -> p (l a) h", h=DH)[:, :, bass.ds(pp * 2, 2)]
                              ).then_inc(s["cfp_ok"], 1)
                dve.wait_ge(s["cb_ok"], at(n, 3, 1))
                v.memset(cb[:, :, 0:2], 0.0)
                v.memset(cb[:, :, S + 2:S + 4], 0.0).then_inc(s["pad_ok"], 1)
                dve.wait_ge(s["pad_ok"], n + 1)
                dve.wait_ge(s["cfp_ok"], at(n, 2, 2))
                for y in range(3):
                    dve.wait_ge(s["cb_ok"], at(n, 3, y + 1))
                    for a in range(TAPS):
                        for e in range(2):
                            i = 2 * y + e
                            if a == 0:
                                v.tensor_scalar(qs[:, i, :], cb[:, i, 0:S], cwp[:, 0, i:i + 1], None, ALU.mult
                                                ).then_inc(s["cv_s"], 1)
                                continue
                            dve.wait_ge(s["cv_s"], at(n, 30, 10 * y + 2 * (a - 1) + e + 1))
                            v.scalar_tensor_tensor(qs[:, i, :], cb[:, i, a:a + S], cwp[:, a, i:i + 1], qs[:, i, :],
                                                   ALU.mult, ALU.add).then_inc(s["cv_s"], 1)
                dve.wait_ge(s["rs_ok"], n + 1)
                v.reciprocal(rs, rs).then_inc(s["rq_ok"], 1)
                dve.wait_ge(s["rq_ok"], n + 1)
                for i in range(4):
                    e, w = i % 2, 1 - i // 2
                    v.scalar_tensor_tensor(kqn[:, e, :, w, :], qs[:, i, :].rearrange("p (t n) -> p t n", t=TT),
                                           float(DE) ** -0.5 if w else 1.0,
                                           rs[:, i * S:(i + 1) * S].rearrange("p (t n) -> p t n", t=TT),
                                           ALU.mult, ALU.mult).then_inc(s["kqn_ok"], 1)
                dve.wait_ge(s["tk_ok"], n + 1)
                v.tensor_copy(vtok.rearrange("p e t n -> p (e t n)"), PS[:, 7, :]).then_inc(s["vtok_ok"], 1)
                for e in range(2):
                    dve.wait_ge(s["kk_ok"], at(n, 2, e + 1))
                    dve.wait_ge(s["etm_ok"], at(n, 4, 2 * e + 2))
                    for d in range(2):
                        for t in range(TT):
                            v.scalar_tensor_tensor(NB[:, e, d, t, :], PS[:, 4 + e, t * 256:t * 256 + P],
                                                   cf[:, 0, t, d, e:e + 1], ET[:, e, d, t, :], ALU.mult, ALU.mult
                                                   ).then_inc(s["nb_ok"], 1)
                for e in range(2):
                    kq = PS[:, 4 + e, :].rearrange("p (t w n) -> p t w n", t=TT, w=2)[:, :, 1, :]
                    for d in range(2):
                        v.tensor_tensor(AT[:, e, d], kq, ET[:, e, d], ALU.mult).then_inc(s["at_ok"], 1)
                dve.wait_ge(s["nb_ok"], at(n, 8, 8))
                for e in range(2):
                    dve.wait_ge(s["nbT_ok"], at(n, 2, e + 1))
                    v.tensor_tensor(A[:, e], PS[:, 2 + e, :].rearrange("p (d t n) -> p d t n", d=2, t=TT),
                                    over_tiles(level[:, 0]), ALU.mult).then_inc(s["d1_s"], 1)
                    for d in range(2):
                        last = v.tensor_tensor(DT[:, e, d], NB[:, e, d],
                                               level[:, 0, 1 - d:2 - d, :].to_broadcast([P, TT, P]), ALU.mult)
                    last.then_inc(s["d1_s"], 1)
                    eye = ident.rearrange("p (o n) -> p o n", o=1).to_broadcast([P, 4, P])
                    dve.wait_ge(s["d1_s"], at(n, 6, 3 * e + 2))
                    v.tensor_tensor(Dm[:, e].rearrange("p d t n -> p (d t) n"), A[:, e].rearrange("p d t n -> p (d t) n"),
                                    eye, ALU.add).then_inc(s["l_D"], 1)
                    v.tensor_tensor(DT[:, e].rearrange("p d t n -> p (d t) n"), DT[:, e].rearrange("p d t n -> p (d t) n"),
                                    eye, ALU.add).then_inc(s["d1_s"], 1)
                dve.wait_ge(s["ktok_ok"], n + 1)
                for e in range(2):
                    for d in range(2):
                        t = SECOND[d]
                        v.tensor_scalar(kg[:, 2 * e + d, :], ktok[:, e, t, :], cf[:, 2, t, d, e:e + 1], -1.0,
                                        ALU.mult, ALU.mult).then_inc(s["kg_ok"], 1)
                        t = FIRST[d]
                        v.tensor_scalar(kd[:, e, d, :], ktok[:, e, t, :], cf[:, 3, t, d, e:e + 1], None,
                                        ALU.mult).then_inc(s["kd_ok"], 1)

                def level_up(w):
                    k = n * 2 * (LEVELS - 1) + 2 * w
                    for e in range(2):
                        dve.wait_ge(s["l_a"], k + e + 1)
                        m = level[:, w + 1] if isinstance(w, int) else \
                            level[:, bass.ds(w + 1, 1)].rearrange("p v d n -> p (v d) n")
                        v.tensor_tensor(A[:, e], PS[:, 2 + e, :].rearrange("p (d t n) -> p d t n", d=2, t=TT),
                                        over_tiles(m), ALU.mult).then_inc(s["l_A"], 1)
                    for e in range(2):
                        dve.wait_ge(s["l_b"], k + e + 1)
                        v.tensor_tensor(DT[:, e].rearrange("p d t n -> p (d t n)"),
                                        DT[:, e].rearrange("p d t n -> p (d t n)"), PS[:, 4 + e, :], ALU.add
                                        ).then_inc(s["l_DT"], 1)

                with dve.Fori(0, LEVELS - 2) as w:
                    level_up(w)
                level_up(LEVELS - 2)
                dve.wait_ge(s["wu_ok"], at(n, 2, 1))
                for e in range(2):
                    for d in range(2):
                        t = FIRST[d]
                        v.tensor_scalar(vn[:, e, d, t, :], PS[:, 3, (2 * e + d) * P:(2 * e + d + 1) * P],
                                        cf[:, 0, t, d, e:e + 1], None, ALU.mult).then_inc(s["vn1_ok"], 1)
                dve.wait_ge(s["v2_ok"], n + 1)
                for e in range(2):
                    for d in range(2):
                        t = SECOND[d]
                        v.tensor_scalar(vn[:, e, d, t, :], PS[:, 5, (2 * e + d) * P:(2 * e + d + 1) * P],
                                        cf[:, 0, t, d, e:e + 1], None, ALU.mult).then_inc(s["vn2_ok"], 1)
                dve.wait_ge(s["o_ok"], n + 1)
                dve.wait_ge(s["qSs_ok"], n + 1)
                v.tensor_tensor(ob.rearrange("p j n -> p (j n)"), PS[:, 7, :], qS.rearrange("p j n -> p (j n)"),
                                ALU.add).then_inc(s["ob_ok"], 1)
                dve.wait_ge(s["orms_ok"], n + 1)
                v.reciprocal(orr, orms).then_inc(s["orr_ok"], 1)
                dve.wait_ge(s["orr_ok"], n + 1)
                dve.wait_ge(s["ob_ok"], n + 1)
                for j in range(4):
                    v.scalar_tensor_tensor(og[:, j, :], ob[:, j, :], orr[:, j:j + 1], nw, ALU.mult, ALU.mult
                                           ).then_inc(s["on_ok"], 1)
                dve.wait_ge(s["on_ok"], at(n, 4, 4))
                dve.wait_ge(s["z_ok"], n + 1)
                v.tensor_tensor(og.rearrange("p (e t) n -> p e t n", e=2), og.rearrange("p (e t) n -> p e t n", e=2),
                                zs.rearrange("p t (e n) -> p e t n", e=2), ALU.mult).then_inc(s["og_ok"], 1)

            def final(l):
                for u in range(4):
                    dve.wait_ge(s["sgm_ok"], at(l, 4, u + 1))
                    dve.wait_ge(s["fin_ok"], at(l, 8, 2 * u + 2))
                    if u >= 1:
                        dve.wait_ge(s["yT_s"], at(l, 12, 3 * u))
                    v.tensor_tensor(m1, sgm[:, 0:512], PS[:, 2, :], ALU.mult).then_inc(s["yT_s"], 1)
                    v.tensor_tensor(m2, sgm[:, 512:1024], PS[:, 3, :], ALU.mult).then_inc(s["yT_s"], 1)
                    dve.wait_ge(s["yT_s"], at(l, 12, 3 * u + 2))
                    if u >= 2:
                        dve.wait_ge(s["fout_ok"], at(l, 4, u - 1))
                    v.tensor_tensor(yT[:, u % 2].rearrange("p c s -> p (c s)"), m1, m2, ALU.add
                                    ).then_inc(s["yT_s"], 1)

            made = [0]

            def link(instruction):
                made[0] += 1
                instruction.then_inc(s["sd"], 1)
                dve.wait_ge(s["sd"], made[0])

            v.memset(ones[:, :], 1.0).then_inc(s["layer_done"], 1)
            v.memset(acc[:, :], 0.0).then_inc(s["acc_zero"], 1)
            v.memset(eps[:, :], EPS).then_inc(s["setup_dve"], 1)
            dve.wait_ge(s["setup_dve"], 1)
            dve.wait_ge(s["pos_in"], 16)
            dve.wait_ge(s["table_in"], 16)
            link(v.tensor_copy(posf[:, :], posi[:, :]))
            for t in range(TT):
                link(v.tensor_scalar(ang[:, t, :], freq, posf[:, t:t + 1], None, ALU.mult))
            angf = ang.rearrange("p t f -> p (t f)")
            W = TT * AE // 2
            for k, quarter in ((0, 0.25), (1, 0.0)):
                turns, a = turn_[:, k * W:(k + 1) * W], angle[:, k * W:(k + 1) * W]
                link(v.tensor_scalar(turns, angf, 1.0 / TWO_PI, quarter, ALU.mult, ALU.add))
                link(v.tensor_scalar(turns, turns, ROUND, None, ALU.add))
                link(v.tensor_scalar(turns, turns, -ROUND, None, ALU.add))
                link(v.scalar_tensor_tensor(a, turns, -PI1, angf, ALU.mult, ALU.add))
                link(v.scalar_tensor_tensor(a, turns, -PI2, a, ALU.mult, ALU.add))
                link(v.scalar_tensor_tensor(a, turns, -PI3, a, ALU.mult, ALU.add))
                link(v.tensor_scalar(a, a, quarter * TWO_PI, None, ALU.add))
                link(v.tensor_scalar(a, a, 3.1415925, -3.1415925, ALU.min, ALU.max))
            assert made[0] == SD_ANGLE
            dve.wait_ge(s["setup_pe"], 1)
            link(v.tensor_copy(cols[:, :], PS[:, 7, 0:56]))
            for l in range(DEPTH):
                link(v.tensor_copy(cw[:, l, :], PS[:, 7, 128 * (l + 1):128 * (l + 1) + 90]))
            assert made[0] == SD_COLS
            dve.wait_ge(s["sa"], 2)
            dve.wait_ge(s["bias_in"], 16)
            for kc in range(KC):
                for half in range(2):
                    ada_block(0, kc, half)
            mod_finish(0, 0, 0)
            dve.wait_ge(s["x_in"], 16)
            with dve.Fori(0, DEPTH) as l:
                norm(l * 3)
                ffn(l * 2, l * 3 + 1)
                post(l * 3)
                mod_finish(l * 3 + 1, l, 1)
                norm(l * 3 + 1)
                attention(l, l * 3 + 2)
                coefficients(l)
                with dve.Fori(0, PAIRS) as pp:
                    pair(l, pp)
                final(l)
                post(l * 3 + 1)
                mod_finish(l * 3 + 2, l, 2)
                norm(l * 3 + 2)
                ffn(l * 2 + 1, l * 3 + 3)
                post(l * 3 + 2)
                mod_finish(l * 3 + 3, l * -1 + 1, 0, end_of_layer=True)


_INS = ['x', 'c', 'positions', 'w_ada', 'b_ada', 'norm_pre', 'norm_post', 'ffn_w_in', 'ffn_w_out', 'w_in', 'conv_w',
        'a_log', 'dt_bias', 'dn_norm_w', 'w_branch_att', 'w_branch_dn', 'w_out']


def kernel(**inputs):
    import concourse.bacc as bacc
    from concourse.bass_utils import run_bass_kernel_spmd

    nc = bacc.Bacc("TRN2", target_bir_lowering=False, num_devices=1)
    arrays, args = {}, []
    given = [(name, np.ascontiguousarray(inputs[name])) for name in _INS] + [("table", constant_table())]
    for name, a in given:
        arrays[f"in_{name}"] = a
        args.append(nc.dram_tensor(f"in_{name}", a.shape, mybir.dt.from_np(a.dtype), kind="ExternalInput").ap())
    out = nc.dram_tensor("out_x", (1, S, D), F32, kind="ExternalOutput").ap()
    build(nc, *args, out)
    return run_bass_kernel_spmd(nc, [arrays], core_ids=[0]).results[0]["out_x"]
```

```python
from contextlib import ExitStack

import numpy as np

import concourse.bass as bass
from concourse import mybir

F32 = mybir.dt.float32
F32R = mybir.dt.float32r
I32 = mybir.dt.int32
ALU = mybir.AluOpType
ACT = mybir.ActivationFunctionType
AX = mybir.AxisListType

P = 128
D = 1024
S = 256
DEPTH = 2
KC = D // P
TT = S // P
FFN = ((8 * D // 3 + 127) // 128) * 128
FC = FFN // P
UNITS = FC // 2
SUBS = 3
GROUPS = ((128, 1), (512, 4), (2048, 16))
NG = len(GROUPS)
AH, AE = 4, 64
AW = NG * AH * AE
DH, DE = 6, 128
DW = DH * DE
TAPS = 5
Q0, K0, V0 = 0, AW, 2 * AW
DN0 = 3 * AW
Z0 = DN0 + 3 * DW
B0 = Z0 + DW
GA0 = B0 + 4 * DH
GD0 = GA0 + D
N_IN = GD0 + D
EPS = 1e-6
NEG = -1e30
THETA = 10000.0
SD_ANGLE = 3 + 2 * 8
SD_COLS = SD_ANGLE + 3
LEVELS = 7
PAIRS = DH // 2
U_ALL = 14400
TWO_PI = 6.283185307179586
PI1, PI2 = 6.28125, 0.0019350051879882812
PI3 = TWO_PI - PI1 - PI2
ROUND = 12582912.0
FWD, BWD = 0, 1
FIRST = (0, 1)
SECOND = (1, 0)

C_ID = 0
C_INC = C_ID + P
C_AFTER = C_INC + 2 * P
C_LEVEL = C_AFTER + 2 * P
C_MASK = C_LEVEL + LEVELS * 2 * P
C_FREQ = C_MASK + TT * NG * S
C_ALL = C_FREQ + AE // 2


def constant_table():
    t = np.zeros((P, C_ALL), np.float32)
    i = np.arange(P)
    t[:, C_ID:C_ID + P] = np.eye(P)
    inc = (i[:, None] <= i[None, :])
    for d, m in ((FWD, inc), (BWD, inc.T)):
        t[:, C_INC + d * P:C_INC + (d + 1) * P] = m
        t[:, C_AFTER + d * P:C_AFTER + (d + 1) * P] = ~m
    for v in range(LEVELS):
        s = 1 << v
        low = (i[:, None] // s % 2 == 1) & (i[:, None] // (2 * s) == i[None, :] // (2 * s)) & (i[None, :] // s % 2 == 0)
        for d, m in ((FWD, low), (BWD, low.T)):
            at = C_LEVEL + (2 * v + d) * P
            t[:, at:at + P] = -1.0 * m
    keys = np.arange(S)
    for q in range(TT):
        query = q * P + i[:, None]
        for g, (window, dil) in enumerate(GROUPS):
            diff = query - keys[None, :]
            ok = (diff % dil == 0) & (np.abs(diff) // dil <= window // (2 * dil))
            at = C_MASK + (q * NG + g) * S
            t[:, at:at + S] = np.where(ok, 0.0, NEG)
    half = AE // 2
    t[:, C_FREQ:] = np.power(np.float32(THETA), -np.arange(half, dtype=np.float32) * np.float32(2.0) / np.float32(AE))
    return t


GRAN = 1024
RAW_SLOTS, SPLIT_SLOTS = 6, 3
STEP = 6
Q_FFN = (0, 141)
N_FFN = STEP * UNITS
Q_ATT = N_FFN
N_ATT = 9
Q_BA = Q_ATT + 2 * N_ATT
Q_DN = Q_BA + 1
N_DN = 12
Q_FIN = Q_DN + PAIRS * N_DN
N_FIN = 4 + 2 * KC
NQ = Q_FIN + N_FIN + N_FFN
assert Q_FFN[1] == Q_FIN + N_FIN and N_DN % RAW_SLOTS == 0 and NQ % SPLIT_SLOTS == 0


def q_into(u):
    return 0 if isinstance(u, int) and u == 0 else STEP * u - 2


def q_out(u):
    return N_FFN - 2 if u == UNITS - 1 else STEP * u + STEP + 2


def q_hidden(l, f):
    return l * (2 * UNITS + KC) + f * (UNITS + KC)


def q_branch(dc):
    return Q_FIN + 4 + (0 if dc == 0 else 2 * dc - 1)


def q_rows(dc):
    return Q_FIN + 4 + (15 if dc == KC - 1 else 2 * dc + 2)


def raw_places():
    slot, loads = [0] * NQ, [1] * NQ
    for q in range(NQ):
        if q < Q_ATT:
            slot[q] = q % RAW_SLOTS
        elif q < Q_BA:
            k = (q - Q_ATT) % N_ATT
            slot[q], loads[q] = k % RAW_SLOTS, 2 if k < 6 else 1
        elif q == Q_BA:
            slot[q] = 3
        elif q < Q_FIN:
            slot[q] = (q - Q_DN) % RAW_SLOTS
        elif q < Q_FFN[1]:
            slot[q] = (q - Q_FIN) % RAW_SLOTS
        else:
            slot[q] = (q - Q_FFN[1]) % RAW_SLOTS
    for dc in range(KC):
        loads[q_branch(dc)] = 2
    return slot, loads


SLOT, LOADS = raw_places()


def landed(q, l, i=0, per=0):
    same = [p for p in range(NQ) if SLOT[p] == SLOT[q]]
    layer = 16 * sum(LOADS[p] for p in same)
    upto = 16 * sum(LOADS[p] for p in same if p <= q)
    turn = 16 * sum(LOADS[p] for p in same if q < p <= q + per)
    return l * layer + upto + i * turn


def at(n, per, k):
    return n * per + k


def build(nc, x, c, positions, w_ada, b_ada, norm_pre, norm_post, ffn_w_in, ffn_w_out, w_in, conv_w,
          a_log, dt_bias, dn_norm_w, w_branch_att, w_branch_dn, w_out, table, out):
    with ExitStack() as ctx:
        def sb(name, shape, dt=F32):
            return ctx.enter_context(nc.sbuf_tensor(name, shape, dt))

        def sem(name):
            return ctx.enter_context(nc.semaphore(name))

        PS = ctx.enter_context(nc.psum_tensor("PS", [P, 8, 512], F32))

        def bank(b, n=1):
            return PS[:, b:b + n, :].rearrange("p b c -> p (b c)")

        X = sb("X", [P, TT, D])
        hTh = sb("hTh", [P, KC, S], F32R)
        hTl = sb("hTl", [P, KC, S], F32R)
        RAW = sb("RAW", [P, RAW_SLOTS, GRAN])
        HI = sb("HI", [P, SPLIT_SLOTS, GRAN], F32R)
        LO = sb("LO", [P, SPLIT_SLOTS, GRAN], F32R)
        ACh = sb("ACh", [P, 2, 512], F32R)
        ACl = sb("ACl", [P, 2, 512], F32R)
        ADA = sb("ADA", [P, 2, 3 * D // 2])
        acc = sb("acc", [P, 3 * D])
        gpost = sb("gpost", [P, D])
        gateb = sb("gateb", [P, D])
        modA = sb("modA", [P, KC])
        modB = sb("modB", [P, KC])
        CT = sb("CT", [P, C_ALL])
        ones = sb("ones", [P, P])
        eps = sb("eps", [P, 2])
        rowsb = sb("rowsb", [P, P])
        cvrows = sb("cvrows", [P, DEPTH, P])
        cols = sb("cols", [P, DEPTH * SUBS * KC + KC])
        ccol = sb("ccol", [P, KC])
        cw = sb("cw", [P, DEPTH, TAPS * 18])
        posi = sb("posi", [P, TT], I32)
        posf = sb("posf", [P, TT])
        cs = sb("cs", [P, 2, TT, AE // 2])
        ssq = sb("ssq", [P, 2])
        rms = sb("rms", [P, 2])
        rr = sb("rr", [P, 2])
        oTh = sb("oTh", [P, 2 + DH, S], F32R)
        oTl = sb("oTl", [P, 2 + DH, S], F32R)
        small = sb("small", [P, 2 * 12 + P])
        alogb, dtbb, nw = small[:, 0:12], small[:, 12:24], small[:, 24:24 + P]
        U = sb("U", [P, U_ALL])

        ident = CT[:, C_ID:C_ID + P]
        inc = CT[:, C_INC:C_INC + 2 * P].rearrange("p (d n) -> p d n", d=2)
        after = CT[:, C_AFTER:C_AFTER + 2 * P].rearrange("p (d n) -> p d n", d=2)
        level = CT[:, C_LEVEL:C_LEVEL + LEVELS * 2 * P].rearrange("p (v d n) -> p v d n", v=LEVELS, d=2)
        amask = CT[:, C_MASK:C_MASK + TT * NG * S].rearrange("p (q n) -> p q n", q=TT)
        freq = CT[:, C_FREQ:C_FREQ + AE // 2]

        top = [0]

        def carve(n, start=None):
            if start is not None:
                top[0] = start
            a = top[0]
            top[0] += n
            assert top[0] <= U_ALL, top
            return U[:, a:a + n]

        xn = carve(TT * D, 0).rearrange("p (t d) -> p t d", t=TT)
        sg = carve(2 * 512, 0).rearrange("p (b n) -> p b n", b=2)
        act = carve(2 * 512).rearrange("p (b n) -> p b n", b=2)
        m12 = carve(2 * 512, 0).rearrange("p (b n) -> p b n", b=2)
        yT = carve(2 * S).rearrange("p (b s) -> p b s", b=2)
        GS2 = carve(2 * 512).rearrange("p (c n) -> p c n", c=2)
        junk = carve(2 * 1024, 2048).rearrange("p (t d) -> p t d", t=TT)
        ang = carve(TT * AE // 2, 0).rearrange("p (t f) -> p t f", t=TT)
        turn_ = carve(2 * TT * AE // 2)
        angle = carve(2 * TT * AE // 2)
        hsum = carve(KC * S, 12288).rearrange("p (k s) -> p k s", k=KC)
        rot = carve(TT * 768, 4096).rearrange("p (t n) -> p t n", t=TT)
        rtmp = carve(4 * 384).rearrange("p (m n) -> p m n", m=4)
        vat = carve(TT * NG * P).rearrange("p (t n) -> p t n", t=TT)
        QT = carve(NG * S).rearrange("p (g s) -> p g s", g=NG)
        KT = carve(NG * S).rearrange("p (g s) -> p g s", g=NG)
        smf = carve(2 * 768)
        sm = smf.rearrange("p (b n) -> p b n", b=2)
        rtmp2 = (rtmp, smf.rearrange("p (m n) -> p m n", m=4))
        prT = carve(2 * 768).rearrange("p (b n) -> p b n", b=2)
        oatT = carve(2 * S, 2048).rearrange("p (c s) -> p c s", c=2)
        oatt = carve(TT * 256, 3072).rearrange("p (t n) -> p t n", t=TT)
        nmx = carve(4)
        den = carve(4)
        rden = carve(4)
        coef = carve(4 * 2 * 2 * DH, 0).rearrange("p (k t d h) -> p k t d h", k=4, t=2, d=2)
        raw = carve(2 * 24).rearrange("p (t n) -> p t n", t=2)
        al = carve(24).rearrange("p (t n) -> p t n", t=2)
        ta = carve(24).rearrange("p (t n) -> p t n", t=2)
        cf = carve(16 * 2).rearrange("p (k t d e) -> p k t d e", k=4, t=2, d=2)
        cwp = carve(30).rearrange("p (a i) -> p a i", a=TAPS)
        oss = carve(4)
        orr = carve(4)
        orms = carve(4)
        ea = carve(12)
        assert top[0] <= 1024
        cb = carve(6 * 260, 4096).rearrange("p (i s) -> p i s", i=6)
        qs = carve(6 * S).rearrange("p (i s) -> p i s", i=6)
        kqn = carve(1024).rearrange("p (e t w n) -> p e t w n", e=2, t=2, w=2)
        ktok = carve(512).rearrange("p (e t n) -> p e t n", e=2, t=2)
        vtok = carve(512).rearrange("p (e t n) -> p e t n", e=2, t=2)
        zs = carve(512).rearrange("p (t n) -> p t n", t=2)
        kd = carve(512).rearrange("p (e d n) -> p e d n", e=2, d=2)
        four = "p (e d t n) -> p e d t n"
        R = carve(1024).rearrange(four, e=2, d=2, t=2)
        ET = carve(1024).rearrange(four, e=2, d=2, t=2)
        NB = carve(1024).rearrange(four, e=2, d=2, t=2)
        AT = carve(1024).rearrange(four, e=2, d=2, t=2)
        sq = carve(1024, 1024)
        rs = carve(1024)
        Dm = carve(1024, 1024).rearrange(four, e=2, d=2, t=2)
        DT = carve(1024).rearrange(four, e=2, d=2, t=2)
        A = carve(1024, 3072).rearrange(four, e=2, d=2, t=2)
        def flat(v):
            return v.rearrange("p e d t n -> p (e d t) n")

        kg, wT = flat(R)[:, 0:4, :], flat(R)[:, 4:8, :]
        St, qS = flat(NB)[:, 0:4, :], flat(NB)[:, 4:8, :]
        ob, og = flat(A)[:, 0:4, :], flat(A)[:, 4:8, :]
        vn = ET
        odT = qs[:, 0:2, :]
        GS = ADA[:, :, :].rearrange("p a n -> p (a n)").rearrange("p (c n) -> p c n", c=6)

        names = ("layer_done sd sa ones_ok pad_ok x_in table_in rows_in pos_in gpost_in ada_land0 ada_land1 bias_in acc_zero ada_step hi_ok lo_ok used "
                 "land0 land1 land2 land3 land4 land5 tmp_ok ach_ok acl_ok m12_ok y_ok hs_ok hsa_ok hh_ok hl_ok oh_ok ol_ok gt_ok gs_ok modps mod_ok "
                 "setup_pe setup_dve setup_act ssq_ok rms_ok rr_ok xn_ok xt_ok hT_ok "
                 "in_land0 in_land1 out_land0 out_land1 gu_ok sg_ok act_ok out_ok "
                 "pssq_ok prms_ok prr_ok ptmp_ok x_up qk_land v_land qkv_ok v_ok rot_s qt_ok qte kte "
                 "sc_ok sm_ok nm_ok p_ok pt_ok pte_ok pv_ok rd_ok oa_ok oat_ok oatT_ok "
                 "ba_in ba_ok cf_dve cf_act cumsum_ok "
                 "dn_land dn_ok cb_ok z_ok cv_s si_ok sq_ok ss_ok rs_ok rq_ok kqn_ok tk_ok ktok_ok vtok_ok kk_ok "
                 "cfp_ok R_ok et_ok ete_ok etm_ok nb_ok at_ok nbT_ok d1_s l_a l_A l_b l_DT l_c l_D "
                 "kg_ok kd_ok wu_ok wT_ok vn1_ok s_ok St_ok v2_ok vn2_ok qS_ok qSs_ok o_ok ob_ok oss_ok orms_ok orr_ok "
                 "on_ok og_ok ogT_ok odn_ok fin_land0 fin_land1 fin_ok sgm_ok yT_s fout_ok stored").split()
        s = {n: sem(n) for n in names}

        block = ctx.enter_context(nc.Block())

        @block.sync
        def _(sp):
            def load(q, l, src, dst=None, i=0, lag=RAW_SLOTS, per=0, first=True):
                if first and q - lag >= 0:
                    sp.wait_ge(s["lo_ok"], l * NQ + q - lag + 1 + i * per)
                raw = RAW[:, SLOT[q], :]
                sp.dma_start(raw if dst is None else dst(raw), src).then_inc(s[f"land{SLOT[q]}"], 16)

            def wide(k):
                return lambda raw: raw.rearrange("p (k n) -> p k n", k=k)

            def into_hidden(l, f, u, i=0, lag=RAW_SLOTS):
                q0 = Q_FFN[f] + q_into(u)
                for j in range(4):
                    half, kh = j // 2, j % 2
                    w = ffn_w_in[l, f][kh * 512:(kh + 1) * 512, bass.ds(i * 512 + u * 256 + half * FFN, 256)] \
                        if not isinstance(i, int) else \
                        ffn_w_in[l, f][kh * 512:(kh + 1) * 512, u * 256 + half * FFN:u * 256 + half * FFN + 256]
                    load(q0 + j, l, w.rearrange("(k p) n -> p k n", p=P), wide(4), i, lag, 2 * STEP)

            def out_of_hidden(l, f, u, i=0):
                q0 = Q_FFN[f] + q_out(u)
                for c in range(2):
                    rows = bass.ds(i * 512 + u * 256 + c * P, P) if not isinstance(i, int) else \
                        slice(u * 256 + c * P, u * 256 + (c + 1) * P)
                    load(q0 + c, l, ffn_w_out[l, f][rows, :], None, i, RAW_SLOTS, 2 * STEP)

            def mod_rows(a, l, sub):
                sp.wait_ge(s["acc_zero"], a + 1)
                sp.dma_start(acc[0:1, :], b_ada[bass.ds(l, 1), sub * 3 * D:(sub + 1) * 3 * D]).then_inc(s["bias_in"], 16)
                sp.wait_ge(s["mod_ok"], a)
                sp.dma_start(gpost[:, :], norm_post[bass.ds(l, 1), sub, :].to_broadcast([P, D])
                             ).then_inc(s["gpost_in"], 16)

            def ffn(l, f, a, l_mod, sub):
                into_hidden(l, f, 0, lag=2 if f else RAW_SLOTS)
                into_hidden(l, f, 1, lag=2 if f else RAW_SLOTS)
                out_of_hidden(l, f, 0)
                mod_rows(a, l_mod, sub)
                into_hidden(l, f, 2)
                out_of_hidden(l, f, 1)
                with sp.Fori(0, 4) as i:
                    for u in (3, 4):
                        into_hidden(l, f, u, i)
                        out_of_hidden(l, f, u - 1, i)
                out_of_hidden(l, f, UNITS - 1)

            def kview(w, rows, n0, n):
                return w[rows, n0 if isinstance(n0, slice) else bass.ds(n0, n)].rearrange("(k p) n -> p k n", p=P)

            def attention(l):
                with sp.Fori(0, 2) as jj:
                    for k in range(6):
                        g, kh = k // 2, k % 2
                        for w, off in ((0, Q0), (1, K0)):
                            load(Q_ATT + k, l, kview(w_in[l], slice(kh * 512, (kh + 1) * 512),
                                                     jj * P + off + g * AH * AE, P),
                                 lambda raw: raw.rearrange("p (k w n) -> p k w n", k=4, w=2)[:, :, w, :],
                                 jj, 3, N_ATT, first=(w == 0))
                    for g in range(NG):
                        load(Q_ATT + 6 + g, l, kview(w_in[l], slice(0, D), jj * P + V0 + g * AH * AE, P), wide(KC),
                             jj, 3, N_ATT)

            def small_weights(l):
                load(Q_BA, l, kview(w_in[l], slice(0, D), slice(B0, B0 + 24), 24),
                     lambda raw: raw[:, 0:KC * 24].rearrange("p (k n) -> p k n", k=KC), lag=3)
                sp.dma_start(alogb, a_log.rearrange("l d h -> l (d h)")[bass.ds(l, 1), :].to_broadcast([P, 12])
                             ).then_inc(s["ba_in"], 16)
                sp.dma_start(dtbb, dt_bias.rearrange("l d h -> l (d h)")[bass.ds(l, 1), :].to_broadcast([P, 12])
                             ).then_inc(s["ba_in"], 16)
                sp.dma_start(nw, dn_norm_w[bass.ds(l, 1), :].to_broadcast([P, P])).then_inc(s["ba_in"], 16)

            def delta(l):
                with sp.Fori(0, PAIRS) as pp:
                    for y in range(4):
                        for kh in range(2):
                            load(Q_DN + 2 * y + kh, l, kview(w_in[l], slice(kh * 512, (kh + 1) * 512),
                                                             pp * 256 + DN0 + y * DW, 256), wide(4), pp, 4, N_DN)
                    for j in range(4):
                        load(Q_DN + 8 + j, l, kview(w_in[l], slice(0, D), pp * 256 + (GA0, GD0)[j % 2] + j // 2 * P, P),
                             wide(KC), pp, 4, N_DN)

            def final(l):
                for j in range(4):
                    n0 = (GA0, GD0)[j % 2] + (6 + j // 2) * P
                    load(Q_FIN + j, l, kview(w_in[l], slice(0, D), slice(n0, n0 + P), P), wide(KC))

                def branch(dc):
                    q, cols_ = q_branch(dc), slice(dc * P, (dc + 1) * P)
                    load(q, l, kview(w_branch_att[l], slice(0, 2 * P), cols_, P),
                         lambda raw: raw.rearrange("p (k n) -> p k n", k=KC)[:, 0:2, :])
                    load(q, l, kview(w_branch_dn[l], slice(0, DW), cols_, P),
                         lambda raw: raw.rearrange("p (k n) -> p k n", k=KC)[:, 2:8, :], first=False)

                branch(0)
                for dc in range(KC):
                    if dc + 1 < KC:
                        branch(dc + 1)
                    load(q_rows(dc), l, w_out[l][dc * P:(dc + 1) * P, :])

            sp.dma_start(CT[:, :], table).then_inc(s["table_in"], 16)
            sp.dma_start(rowsb[0:48, :], norm_pre.rearrange("l s (k p) -> (l s k) p", p=P)).then_inc(s["rows_in"], 16)
            sp.dma_start(rowsb[48:56, :], c.rearrange("b (k p) -> (b k) p", p=P)).then_inc(s["rows_in"], 16)
            for l in range(DEPTH):
                sp.dma_start(cvrows[0:90, l, :], conv_w[l].rearrange("a (k p) -> (a k) p", p=P)).then_inc(s["rows_in"], 16)
            with nc.allow_non_contiguous_dma(reason="256 positions, once"):
                sp.dma_start(posi[:, :], positions.rearrange("b (t p) -> p (b t)", p=P)).then_inc(s["pos_in"], 16)
            mod_rows(0, 0, 0)
            sp.dma_start(X[:, :, :], x.rearrange("b (t p) d -> p (b t) d", p=P)).then_inc(s["x_in"], 16)
            with sp.Fori(0, DEPTH) as l:
                sp.wait_ge(s["layer_done"], l + 1)
                ffn(l, 0, l * 3 + 1, l, 1)
                mod_rows(l * 3 + 2, l, 2)
                attention(l)
                small_weights(l)
                delta(l)
                final(l)
                ffn(l, 1, l * 3 + 3, l * -1 + 1, 0)
            sp.wait_ge(s["x_up"], DEPTH * SUBS * TT)
            sp.dma_start(out.rearrange("b (t p) d -> p (b t) d", p=P), X[:, :, :]).then_inc(s["stored"], 16)
            sp.wait_ge(s["stored"], 16)

        @block.gpsimd
        def _(pool):
            def ada(a, l, sub):
                pool.wait_ge(s["ada_step"], at(a, 2 * KC, 0))
                for k in range(2 * KC):
                    if k >= 2:
                        pool.wait_ge(s["ada_step"], at(a, 2 * KC, k - 1))
                    n0 = sub * 3 * D + (k % 2) * (3 * D // 2)
                    pool.dma_start(ADA[:, k % 2, :], w_ada[l, k // 2 * P:(k // 2 + 1) * P, n0:n0 + 3 * D // 2]
                                   ).then_inc(s[f"ada_land{k % 2}"], 16)

            def pair(n):
                pool.wait_ge(s["cfp_ok"], at(n, 2, 2))
                for e in range(2):
                    g = cf[:, 1].rearrange("p t d e -> p d t e")[:, :, :, e:e + 1].to_broadcast([P, 2, TT, P])
                    nc.gpsimd.tensor_tensor(R[:, e], inc.rearrange("p d (o n) -> p d o n", o=1).to_broadcast([P, 2, TT, P]),
                                            g, ALU.mult).then_inc(s["R_ok"], 1)
                for e in range(2):
                    pool.wait_ge(s["ete_ok"], at(n, 2, e + 1))
                    for d in range(2):
                        nc.gpsimd.tensor_tensor(ET[:, e, d, :, :], ET[:, e, d, :, :],
                                                inc[:, d:d + 1, :].to_broadcast([P, TT, P]), ALU.mult
                                                ).then_inc(s["etm_ok"], 1)

            ada(0, 0, 0)
            with pool.Fori(0, DEPTH) as l:
                ada(l * 3 + 1, l, 1)
                ada(l * 3 + 2, l, 2)
                with pool.Fori(0, PAIRS) as pp:
                    pair(l * PAIRS + pp)
                pool.wait_ge(s["m12_ok"], at(l, KC, KC))
                ada(l * 3 + 3, l * -1 + 1, 0)

        @block.tensor
        def _(pe):
            mm = nc.tensor.matmul
            tr = nc.tensor.transpose

            def triple(o, left, right, start, stop):
                mm(o, left[0], right[0], start=start, stop=False, skip_group_check=True)
                mm(o, left[0], right[1], start=False, stop=False, skip_group_check=True)
                return mm(o, left[1], right[0], start=False, stop=stop, skip_group_check=True)

            def halves(q, l, i=0, per=0, k=1):
                pe.wait_ge(s["lo_ok"], l * NQ + q + 1 + i * per)
                return [w[:, q % SPLIT_SLOTS, :].rearrange("p (k n) -> p k n", k=k) for w in (HI, LO)]

            def x_rows(kc, t=None):
                cols_ = slice(None) if t is None else slice(t * P, (t + 1) * P)
                return [h[:, kc, cols_] for h in (hTh, hTl)]

            def part(w, kc, a, b):
                return [h[:, kc, a:b] for h in w]

            def mod_sums(a, sub):
                pe.wait_ge(s["ada_step"], at(a, 2 * KC, 2 * KC))
                for j in range(2 * KC):
                    mm(PS[:, 0, j:j + 1], acc[:, j * P:(j + 1) * P], ones[:, 0:1], start=True, stop=True)
                for h in range(2):
                    last = mm(PS[:, 1 + h, :], ones[:, :], acc[:, 2 * D + h * 512:2 * D + (h + 1) * 512],
                              start=True, stop=True)
                last.then_inc(s["modps"], 1)

            def norm(m):
                pe.wait_ge(s["mod_ok"], m + 1)
                for t in range(TT):
                    pe.wait_ge(s["xn_ok"], at(m, TT, t + 1))
                    for k in range(KC):
                        last = tr(PS[:, k // 2, (k % 2) * S + t * P:(k % 2) * S + (t + 1) * P],
                                  xn[:, t, k * P:(k + 1) * P], ident)
                    last.then_inc(s["xt_ok"], 1)

            def into_hidden(l, n, u, i=0):
                par, q0 = u % 2, Q_FFN[n[1]] + q_into(u)
                if u >= 2:
                    pe.wait_ge(s["tmp_ok"], at(n[0], UNITS, u - 1) + i * 2)
                for j in range(4):
                    half, kh = j // 2, j % 2
                    w = halves(q0 + j, l, i, 2 * STEP, 4)
                    if u == 0 and j < 2:
                        pe.wait_ge(s["hl_ok"], at(n[2], 2, kh + 1))
                    for c in range(2):
                        for k in range(4):
                            last = triple(PS[:, 2 * par + half, c * S:(c + 1) * S], part(w, k, c * P, (c + 1) * P),
                                          x_rows(4 * kh + k), j % 2 == 0 and c == 0 and k == 0, j % 2 == 1 and k == 3)
                    last.then_inc(s["used"], 1)

            def out_of_hidden(l, n, u, i=0, first=False, final=False):
                par, q0 = u % 2, Q_FFN[n[1]] + q_out(u)
                pe.wait_ge(s["ach_ok"], n[3] + u + 1 + i * 2)
                pe.wait_ge(s["acl_ok"], n[3] + u + 1 + i * 2)
                for c in range(2):
                    w = halves(q0 + c, l, i, 2 * STEP, 1)
                    for t in range(TT):
                        a = [h[:, par, c * S + t * P:c * S + (t + 1) * P] for h in (ACh, ACl)]
                        for h in range(2):
                            last = triple(PS[:, 4 + 2 * t + h, :], a, part(w, 0, h * 512, (h + 1) * 512),
                                          first and c == 0, final and c == 1)
                    last.then_inc(s["used"], 1)

            def ffn(l, f, m):
                n = (l * 2 + f, f, m, q_hidden(l, f))
                into_hidden(l, n, 0)
                into_hidden(l, n, 1)
                out_of_hidden(l, n, 0, first=True)
                into_hidden(l, n, 2)
                out_of_hidden(l, n, 1)
                with pe.Fori(0, 4) as i:
                    for u in (3, 4):
                        into_hidden(l, n, u, i)
                        out_of_hidden(l, n, u - 1, i)
                out_of_hidden(l, n, UNITS - 1, final=True)

            def attention(l):
                with pe.Fori(0, 2) as jj:
                    n = l * 2 + jj
                    pe.wait_ge(s["hl_ok"], at(l * 3 + 1, 2, 2))
                    for k in range(6):
                        g, kh = k // 2, k % 2
                        w = halves(Q_ATT + k, l, jj, N_ATT, 4)
                        for t in range(TT):
                            for kc in range(4):
                                last = triple(PS[:, 2 * t + g // 2, (g % 2) * 256:(g % 2) * 256 + 256],
                                              x_rows(4 * kh + kc, t), part(w, kc, 0, 256),
                                              kh == 0 and kc == 0, kh == 1 and kc == 3)
                        last.then_inc(s["used"], 1)
                    for g in range(NG):
                        w = halves(Q_ATT + 6 + g, l, jj, N_ATT, KC)
                        for t in range(TT):
                            for kc in range(KC):
                                last = triple(PS[:, 4 + t, g * P:(g + 1) * P], x_rows(kc, t), part(w, kc, 0, P),
                                              kc == 0, kc == KC - 1)
                        last.then_inc(s["used"], 1)
                    pe.wait_ge(s["rot_s"], at(n, 4, 4))
                    for w, b in ((0, 6), (1, 0)):
                        to = bank(b, 2)
                        for g in range(NG):
                            for t in range(TT):
                                last = tr(to[:, g * S + t * P:g * S + (t + 1) * P],
                                          rot[:, t, g * 256 + w * P:g * 256 + (w + 1) * P], ident)
                        last.then_inc(s["qt_ok"], 1)
                    pe.wait_ge(s["v_ok"], n + 1)
                    pe.wait_ge(s["qte"], n + 1)
                    pe.wait_ge(s["kte"], n + 1)

                    def scores(i):
                        hh, q = i // 2, i % 2
                        if i >= 2:
                            pe.wait_ge(s["sm_ok"], at(n, 4, i - 1))
                        for g in range(NG):
                            last = mm(PS[:, 2 + 2 * (i % 2) + g // 2, (g % 2) * S:(g % 2) * S + S],
                                      QT[hh * AE:(hh + 1) * AE, g, q * P:(q + 1) * P],
                                      KT[hh * AE:(hh + 1) * AE, g, :], start=True, stop=True)
                        last.then_inc(s["sc_ok"], 1)

                    def turn(i):
                        pe.wait_ge(s["p_ok"], at(n, 4, i + 1))
                        if i >= 1:
                            pe.wait_ge(s["pte_ok"], at(n, 4, i))
                        to = bank(6, 2)
                        for j in range(2 * NG):
                            last = tr(to[:, j * P:(j + 1) * P], sm[:, i % 2, j * P:(j + 1) * P], ident)
                        last.then_inc(s["pt_ok"], 1)

                    def values(i):
                        hh = i // 2
                        pe.wait_ge(s["pte_ok"], at(n, 4, i + 1))
                        if i >= 2:
                            pe.wait_ge(s["oa_ok"], at(n, 4, i - 1))
                        for j in range(2 * NG):
                            g, kt = j // 2, j % 2
                            last = mm(PS[:, i % 2, i * AE:(i + 1) * AE], prT[:, i % 2, j * P:(j + 1) * P],
                                      vat[:, kt, g * P + hh * AE:g * P + (hh + 1) * AE],
                                      start=(j == 0), stop=(j == 2 * NG - 1))
                        last.then_inc(s["pv_ok"], 1)

                    scores(0)
                    scores(1)
                    turn(0)
                    scores(2)
                    values(0)
                    turn(1)
                    scores(3)
                    values(1)
                    turn(2)
                    values(2)
                    turn(3)
                    values(3)
                    pe.wait_ge(s["oa_ok"], at(n, 4, 4))
                for q in range(2):
                    for c in range(2):
                        last = tr(PS[:, 1, c * S + q * P:c * S + (q + 1) * P], oatt[:, q, c * P:(c + 1) * P], ident)
                last.then_inc(s["oat_ok"], 1)

            def coefficients(l):
                w = [h[:, Q_BA % SPLIT_SLOTS, 0:KC * 24].rearrange("p (k n) -> p k n", k=KC) for h in (HI, LO)]
                pe.wait_ge(s["lo_ok"], l * NQ + Q_BA + 1)
                for t in range(TT):
                    for kc in range(KC):
                        last = triple(PS[:, 7, t * 24:(t + 1) * 24], x_rows(kc, t), part(w, kc, 0, 24),
                                      kc == 0, kc == KC - 1)
                last.then_inc(s["used"], 1)
                pe.wait_ge(s["cf_dve"], at(l, 5, 5))
                for w, m in ((0, inc), (1, after)):
                    for d in range(2):
                        last = mm(PS[:, 6, (w * 2 + d) * 12:(w * 2 + d + 1) * 12].rearrange("p (t h) -> p t h", t=2),
                                  m[:, d, :], coef[:, 1, :, d, :], start=True, stop=True)
                last.then_inc(s["cumsum_ok"], 1)

            def pair(l, pp):
                n = l * PAIRS + pp
                pe.wait_ge(s["cf_act"], at(l, 7, 7))
                pe.wait_ge(s["oh_ok"], at(l, 1 + PAIRS, 1 + pp))
                for y in range(3):
                    for kh in range(2):
                        w = halves(Q_DN + 2 * y + kh, l, pp, N_DN, 4)
                        for e in range(2):
                            for k in range(4):
                                last = triple(PS[:, y, e * S:(e + 1) * S], part(w, k, e * P, (e + 1) * P),
                                              x_rows(4 * kh + k), kh == 0 and e == 0 and k == 0, kh == 1 and k == 3)
                        last.then_inc(s["used"], 1)
                for kh in range(2):
                    w = halves(Q_DN + 6 + kh, l, pp, N_DN, 4)
                    for t in range(TT):
                        for k in range(4):
                            last = triple(PS[:, 3, t * S:(t + 1) * S], x_rows(4 * kh + k, t), part(w, k, 0, 256),
                                          kh == 0 and t == 0 and k == 0, kh == 1 and k == 3)
                    last.then_inc(s["used"], 1)

                def gates(j0, b):
                    for j in range(2):
                        w = halves(Q_DN + 8 + j0 + j, l, pp, N_DN, KC)
                        for k in range(KC):
                            last = triple(PS[:, b, j * S:(j + 1) * S], part(w, k, 0, P), x_rows(k), k == 0, k == KC - 1)
                        last.then_inc(s["used"], 1)

                pe.wait_ge(s["sq_ok"], n + 1)
                for h in range(2):
                    last = mm(PS[:, 4 + h, :], ones[:, :], sq[:, h * 512:(h + 1) * 512], start=True, stop=True)
                last.then_inc(s["ss_ok"], 1)
                pe.wait_ge(s["cb_ok"], at(n, 3, 3))
                for e in range(2):
                    pe.wait_ge(s["R_ok"], at(n, 2, e + 1))
                    for d in range(2):
                        last = mm(PS[:, e, d * 256:(d + 1) * 256], after[:, d, :], R[:, e, d, :, :],
                                  start=True, stop=True)
                    last.then_inc(s["et_ok"], 1)
                gates(0, 2)
                pe.wait_ge(s["kqn_ok"], at(n, 4, 4))
                for e in range(2):
                    for t in range(TT):
                        tr(PS[:, 6, (2 * e + t) * P:(2 * e + t + 1) * P], kqn[:, e, t, 0, :], ident)
                for e in range(2):
                    for t in range(TT):
                        last = tr(PS[:, 7, (2 * e + t) * P:(2 * e + t + 1) * P],
                                  qs[:, 4 + e, t * P:(t + 1) * P], ident)
                last.then_inc(s["tk_ok"], 1)
                for e in range(2):
                    for t in range(TT):
                        last = mm(PS[:, 4 + e, t * 256:(t + 1) * 256], kqn[:, e, t, 0, :], kqn[:, e, t, :, :],
                                  start=True, stop=True)
                    last.then_inc(s["kk_ok"], 1)
                four = [(d, t) for d in range(2) for t in range(TT)]

                pe.wait_ge(s["gs_ok"], at(n, 2, 1))

                def at4(b, e, d, t):
                    return PS[:, b + e, (2 * d + t) * P:(2 * d + t + 1) * P]

                pe.wait_ge(s["z_ok"], n + 1)
                for e in range(2):
                    pe.wait_ge(s["nb_ok"], at(n, 8, 4 * e + 4))
                    for d, t in four:
                        last = tr(at4(2, e, d, t), NB[:, e, d, t, :], ident)
                    last.then_inc(s["nbT_ok"], 1)
                pe.wait_ge(s["ete_ok"], at(n, 2, 1))
                gates(2, 0)

                def level_up(v, last_level):
                    pe.wait_ge(s["at_ok"], at(n, 4, 4))
                    pe.wait_ge(s["d1_s"], at(n, 6, 6))
                    for e in range(2):
                        pe.wait_ge(s["l_D"], n * 2 * (LEVELS - 1) + 2 * v + e + 1)
                        for d, t in four:
                            last = mm(at4(2, e, d, t), NB[:, e, d, t, :], Dm[:, e, d, t, :], start=True, stop=True)
                        last.then_inc(s["l_a"], 1)
                    for e in range(2):
                        pe.wait_ge(s["l_A"], n * 2 * (LEVELS - 1) + 2 * v + e + 1)
                        for d, t in four:
                            last = mm(at4(4, e, d, t), A[:, e, d, t, :], DT[:, e, d, t, :], start=True, stop=True)
                        last.then_inc(s["l_b"], 1)
                    if last_level:
                        return
                    for e in range(2):
                        pe.wait_ge(s["l_DT"], n * 2 * (LEVELS - 1) + 2 * v + e + 1)
                        for d, t in four:
                            last = tr(at4(6, e, d, t), DT[:, e, d, t, :], ident)
                        last.then_inc(s["l_c"], 1)

                with pe.Fori(0, LEVELS - 2) as v:
                    level_up(v, False)
                level_up(LEVELS - 2, True)
                pe.wait_ge(s["l_DT"], at(n, 2 * (LEVELS - 1), 2 * (LEVELS - 1)))
                pe.wait_ge(s["ktok_ok"], n + 1)
                pe.wait_ge(s["vtok_ok"], n + 1)
                pe.wait_ge(s["kg_ok"], at(n, 4, 4))
                both = [(e, d) for e in range(2) for d in range(2)]

                def one(b, e, d):
                    return PS[:, b, (2 * e + d) * P:(2 * e + d + 1) * P]

                for e, d in both:
                    last = mm(one(3, e, d), DT[:, e, d, FIRST[d], :], vtok[:, e, FIRST[d], :], start=True, stop=True)
                last.then_inc(s["wu_ok"], 1)
                for e, d in both:
                    last = mm(one(2, e, d), kg[:, 2 * e + d, :], DT[:, e, d, SECOND[d], :],
                              start=True, stop=True)
                last.then_inc(s["wu_ok"], 1)
                pe.wait_ge(s["vn1_ok"], at(n, 4, 4))
                pe.wait_ge(s["kd_ok"], at(n, 4, 4))
                for e, d in both:
                    last = mm(one(4, e, d), kd[:, e, d, :], vn[:, e, d, FIRST[d], :], start=True, stop=True)
                last.then_inc(s["s_ok"], 1)
                pe.wait_ge(s["St_ok"], n + 1)
                pe.wait_ge(s["wT_ok"], n + 1)
                for e, d in both:
                    mm(one(5, e, d), DT[:, e, d, SECOND[d], :], vtok[:, e, SECOND[d], :], start=True, stop=False)
                    last = mm(one(5, e, d), wT[:, 2 * e + d, :], St[:, 2 * e + d, :], start=False, stop=True)
                last.then_inc(s["v2_ok"], 1)
                for e, d in both:
                    t = SECOND[d]
                    last = mm(PS[:, 6, (2 * e + t) * P:(2 * e + t + 1) * P], kqn[:, e, t, 1, :], St[:, 2 * e + d, :],
                              start=True, stop=True)
                last.then_inc(s["qS_ok"], 1)
                pe.wait_ge(s["vn2_ok"], at(n, 4, 4))
                for e in range(2):
                    for t in range(TT):
                        for d in range(2):
                            last = mm(PS[:, 7, (2 * e + t) * P:(2 * e + t + 1) * P], AT[:, e, d, t, :],
                                      vn[:, e, d, t, :], start=(d == 0), stop=(d == 1))
                last.then_inc(s["o_ok"], 1)
                pe.wait_ge(s["og_ok"], n + 1)
                for j in range(4):
                    last = tr(PS[:, 2, j * P:(j + 1) * P], og[:, j, :], ident)
                last.then_inc(s["ogT_ok"], 1)

            def final(l):
                pe.wait_ge(s["oh_ok"], at(l, 1 + PAIRS, 1 + PAIRS))
                for j in range(4):
                    w = halves(Q_FIN + j, l, k=KC)
                    for k in range(KC):
                        last = triple(PS[:, 2 + j // 2, (j % 2) * S:(j % 2 + 1) * S], part(w, k, 0, P), x_rows(k),
                                      k == 0, k == KC - 1)
                    last.then_inc(s["used"], 1)
                pe.wait_ge(s["ol_ok"], at(l, 1 + PAIRS, 1 + PAIRS))
                pe.wait_ge(s["gs_ok"], at(l, 2 * PAIRS, 2 * PAIRS))

                def branch(dc):
                    w = halves(q_branch(dc), l, k=KC)
                    if dc >= 2:
                        pe.wait_ge(s["m12_ok"], at(l, KC, dc - 1))
                    for k in range(2 + DH):
                        o = PS[:, dc % 2, 0:S] if k < 2 else PS[:, dc % 2, S:2 * S]
                        last = triple(o, part(w, k, 0, P), [h[:, k, :] for h in (oTh, oTl)],
                                      k in (0, 2), k in (1, 1 + DH))
                    last.then_inc(s["used"], 1)

                def rows(dc):
                    w = halves(q_rows(dc), l)
                    pe.wait_ge(s["ach_ok"], q_hidden(l, 0) + UNITS + dc + 1)
                    pe.wait_ge(s["acl_ok"], q_hidden(l, 0) + UNITS + dc + 1)
                    for t in range(TT):
                        a = [h[:, dc % 2, t * P:(t + 1) * P] for h in (ACh, ACl)]
                        for h in range(2):
                            last = triple(PS[:, 4 + 2 * t + h, :], a, part(w, 0, h * 512, (h + 1) * 512),
                                          dc == 0, dc == KC - 1)
                    last.then_inc(s["used"], 1)

                branch(0)
                for dc in range(KC):
                    if dc + 1 < KC:
                        branch(dc + 1)
                    rows(dc)

            pe.wait_ge(s["setup_dve"], 1)
            pe.wait_ge(s["rows_in"], 64)
            pe.wait_ge(s["table_in"], 16)
            tr(PS[:, 7, 0:56], rowsb[0:56, :], ident[0:56, 0:56])
            for l in range(DEPTH):
                last = tr(PS[:, 7, 128 * (l + 1):128 * (l + 1) + 90], cvrows[0:90, l, :], ident[0:90, 0:90])
            last.then_inc(s["setup_pe"], 1)
            mod_sums(0, 0)
            with pe.Fori(0, DEPTH) as l:
                norm(l * 3)
                ffn(l, 0, l * 3)
                mod_sums(l * 3 + 1, 1)
                norm(l * 3 + 1)
                attention(l)
                coefficients(l)
                with pe.Fori(0, PAIRS) as pp:
                    pair(l, pp)
                final(l)
                mod_sums(l * 3 + 2, 2)
                norm(l * 3 + 2)
                ffn(l, 1, l * 3 + 2)
                mod_sums(l * 3 + 3, 0)

        @block.scalar
        def _(act_):
            fn = nc.scalar.activation

            def roots(src, m, done_sq, done_rms):
                for t in range(TT):
                    fn(junk[:, t, :], src(t), ACT.Square, accum_out=ssq[:, t:t + 1]).then_inc(s[done_sq], 1)
                act_.wait_ge(s[done_sq], at(m, TT, TT))
                fn(rms[:, :], ssq[:, :], ACT.Sqrt, bias=eps[:, 0:1], scale=1.0 / D).then_inc(s[done_rms], 1)

            def high(q, l, i=0, per=0, n=GRAN):
                act_.wait_ge(s[f"land{SLOT[q]}"], landed(q, l, i, per))
                if q >= SPLIT_SLOTS:
                    act_.wait_ge(s["used"], l * NQ + q - SPLIT_SLOTS + 1 + i * per)
                fn(HI[:, q % SPLIT_SLOTS, 0:n], RAW[:, SLOT[q], 0:n], ACT.Copy).then_inc(s["hi_ok"], 1)

            def norm(m, l, q):
                roots(lambda t: X[:, t, :], m, "ssq_ok", "rms_ok")
                if q is not None:
                    for k in range(SPLIT_SLOTS):
                        high(q + k, l)
                act_.wait_ge(s["xt_ok"], at(m, TT, TT))
                for kh in range(2):
                    for k in (4 * kh + 2, 4 * kh + 3):
                        fn(hsum[:, k, :], PS[:, k // 2, (k % 2) * S:(k % 2) * S + S], ACT.Identity,
                           bias=modB[:, k:k + 1], scale=modA[:, k:k + 1]).then_inc(s["hsa_ok"], 1)
                    act_.wait_ge(s["hsa_ok"], at(m, 4, 2 * kh + 2))
                    act_.wait_ge(s["hs_ok"], at(m, 4, 2 * kh + 2))
                    fn(hTh[:, 4 * kh:4 * kh + 4, :], hsum[:, 4 * kh:4 * kh + 4, :], ACT.Copy).then_inc(s["hh_ok"], 1)

            def silu_unit(l, n, u, i=0):
                par = u % 2
                act_.wait_ge(s["used"], l * NQ + Q_FFN[n[1]] + q_into(u) + 4 + i * 2 * STEP)
                if u >= 2:
                    act_.wait_ge(s["tmp_ok"], at(n[0], UNITS, u - 1) + i * 2)
                fn(sg[:, par, :], PS[:, 2 * par, :], ACT.Silu).then_inc(s["sg_ok"], 1)

            def high_hidden(l, n, u, i=0):
                par = u % 2
                act_.wait_ge(s["tmp_ok"], at(n[0], UNITS, u + 1) + i * 2)
                if u >= 2:
                    act_.wait_ge(s["used"], l * NQ + Q_FFN[n[1]] + q_out(u - 2) + 2 + i * 2 * STEP)
                fn(ACh[:, par, :], act[:, par, :], ACT.Copy).then_inc(s["ach_ok"], 1)

            def ffn(l, f, m):
                n, q0 = (l * 2 + f, f), Q_FFN[f]

                def step(u, i=0):
                    q = q0 + q_into(u)
                    high(q, l, i, 2 * STEP)
                    high(q + 1, l, i, 2 * STEP)
                    silu_unit(l, n, u - 1, i)
                    high(q + 2, l, i, 2 * STEP)
                    high(q + 3, l, i, 2 * STEP)
                    high_hidden(l, n, u - 1, i)
                    high(q + 4, l, i, 2 * STEP)
                    high(q + 5, l, i, 2 * STEP)

                high(q0 + 3, l)
                step(1)
                step(2)
                with act_.Fori(0, 4) as i:
                    step(3, i)
                    step(4, i)
                silu_unit(l, n, UNITS - 1)
                high(q0 + N_FFN - 2, l)
                high_hidden(l, n, UNITS - 1)
                high(q0 + N_FFN - 1, l)
                act_.wait_ge(s["used"], l * NQ + q0 + N_FFN)
                roots(lambda t: bank(4 + 2 * t, 2), m, "pssq_ok", "prms_ok")
                act_.wait_ge(s["x_up"], at(m, TT, TT))

            def attention(l):
                with act_.Fori(0, 2) as jj:
                    n = l * 2 + jj
                    for k in range(N_ATT):
                        high(Q_ATT + k, l, jj, N_ATT)
                    act_.wait_ge(s["used"], l * NQ + Q_ATT + N_ATT + jj * N_ATT)
                    fn(vat[:, :, :], PS[:, 4:6, 0:NG * P], ACT.Copy).then_inc(s["v_ok"], 1)
                    act_.wait_ge(s["qt_ok"], at(n, 2, 1))
                    fn(QT.rearrange("p g s -> p (g s)"), bank(6, 2)[:, 0:NG * S], ACT.Copy).then_inc(s["qte"], 1)

                    def soft(i):
                        act_.wait_ge(s["nm_ok"], at(n, 4, i + 1))
                        fn(sm[:, i % 2, :], sm[:, i % 2, :], ACT.Exp, bias=nmx[:, i:i + 1],
                           accum_out=den[:, i:i + 1]).then_inc(s["p_ok"], 1)

                    def turned(i):
                        act_.wait_ge(s["pt_ok"], at(n, 4, i + 1))
                        if i >= 2:
                            act_.wait_ge(s["pv_ok"], at(n, 4, i - 1))
                        fn(prT[:, i % 2, :], bank(6, 2)[:, 0:768], ACT.Copy).then_inc(s["pte_ok"], 1)

                    soft(0)
                    for i in range(1, 4):
                        soft(i)
                        turned(i - 1)
                    turned(3)
                act_.wait_ge(s["oat_ok"], l + 1)
                fn(oTh[:, 0:2, :], PS[:, 1, :].rearrange("p (c s) -> p c s", c=2), ACT.Copy)
                fn(oatT, PS[:, 1, :].rearrange("p (c s) -> p c s", c=2), ACT.Copy).then_inc(s["oh_ok"], 1)

            def coefficients(l):
                high(Q_BA, l, n=KC * 24)
                high(Q_DN, l)
                high(Q_DN + 1, l)
                act_.wait_ge(s["used"], l * NQ + Q_BA + 1)
                ba = PS[:, 7, 0:48].rearrange("p (t n) -> p t n", t=2)
                fn(raw[:, :, 0:12], ba[:, :, 0:12], ACT.Exp, scale=-1.0).then_inc(s["cf_act"], 1)
                fn(ea, alogb, ACT.Exp).then_inc(s["cf_act"], 1)
                act_.wait_ge(s["cf_dve"], at(l, 5, 3))
                fn(ta, al, ACT.Abs).then_inc(s["cf_act"], 1)
                act_.wait_ge(s["cf_act"], at(l, 7, 3))
                fn(ta, ta, ACT.Exp, scale=-1.0).then_inc(s["cf_act"], 1)
                act_.wait_ge(s["cf_act"], at(l, 7, 4))
                fn(ta, ta, ACT.Ln, bias=ones[:, 0:1]).then_inc(s["cf_act"], 1)
                high(Q_DN + 2, l)
                act_.wait_ge(s["cumsum_ok"], l + 1)
                for w in range(2):
                    fn(coef[:, 2 + w].rearrange("p t d h -> p d t h"),
                       PS[:, 6, w * 24:(w + 1) * 24].rearrange("p (d t h) -> p d t h", d=2, t=2),
                       ACT.Exp).then_inc(s["cf_act"], 1)

            def pair(l, pp):
                n = l * PAIRS + pp
                for ahead, y in ((3, None), (4, 0), (5, None), (6, 1), (7, None), (8, 2), (9, None), (10, None)):
                    high(Q_DN + ahead, l, pp, N_DN)
                    if y is not None:
                        act_.wait_ge(s["used"], l * NQ + Q_DN + 2 * y + 2 + pp * N_DN)
                        fn(cb[:, 2 * y:2 * y + 2, 2:2 + S], PS[:, y, :].rearrange("p (e s) -> p e s", e=2),
                           ACT.Copy).then_inc(s["cb_ok"], 1)
                act_.wait_ge(s["used"], l * NQ + Q_DN + 8 + pp * N_DN)
                fn(zs.rearrange("p t n -> p (t n)"), PS[:, 3, :], ACT.Silu).then_inc(s["z_ok"], 1)
                for y in range(3):
                    act_.wait_ge(s["cv_s"], at(n, 30, 10 * (y + 1)))
                    fn(qs[:, 2 * y:2 * y + 2, :], qs[:, 2 * y:2 * y + 2, :], ACT.Silu).then_inc(s["si_ok"], 1)
                act_.wait_ge(s["si_ok"], at(n, 3, 2))
                fn(sq, qs[:, 0:4, :].rearrange("p i s -> p (i s)"), ACT.Square).then_inc(s["sq_ok"], 1)
                act_.wait_ge(s["ss_ok"], n + 1)
                fn(rs, bank(4, 2), ACT.Ln, bias=eps[:, 0:1]).then_inc(s["rs_ok"], 1)
                act_.wait_ge(s["rs_ok"], at(n, 2, 1))
                fn(rs, rs, ACT.Exp, scale=-0.5).then_inc(s["rs_ok"], 1)
                for e in range(2):
                    act_.wait_ge(s["et_ok"], at(n, 2, e + 1))
                    fn(ET[:, e].rearrange("p d t n -> p (d t n)"), PS[:, e, :], ACT.Exp).then_inc(s["ete_ok"], 1)
                high(Q_DN + 11, l, pp, N_DN)
                act_.wait_ge(s["used"], l * NQ + Q_DN + 10 + pp * N_DN)
                fn(GS[:, bass.ds(pp * 2, 1), :], PS[:, 2:3, :], ACT.Sigmoid).then_inc(s["gs_ok"], 1)
                act_.wait_ge(s["tk_ok"], n + 1)
                fn(ktok.rearrange("p e t n -> p (e t n)"), PS[:, 6, :], ACT.Copy).then_inc(s["ktok_ok"], 1)
                act_.wait_ge(s["used"], l * NQ + Q_DN + 12 + pp * N_DN)
                fn(GS[:, bass.ds(pp * 2 + 1, 1), :], PS[:, 0:1, :], ACT.Sigmoid).then_inc(s["gs_ok"], 1)
                for k in range(3):
                    high(Q_DN + N_DN + k, l, pp, N_DN)
                with act_.Fori(0, LEVELS - 2) as v:
                    for e in range(2):
                        act_.wait_ge(s["l_c"], n * 2 * (LEVELS - 2) + 2 * v + e + 1)
                        fn(Dm[:, e].rearrange("p d t n -> p (d t n)"), PS[:, 6 + e, :], ACT.Copy).then_inc(s["l_D"], 1)
                act_.wait_ge(s["wu_ok"], at(n, 2, 2))
                fn(wT.rearrange("p j n -> p (j n)"), PS[:, 2, :], ACT.Copy).then_inc(s["wT_ok"], 1)
                act_.wait_ge(s["s_ok"], n + 1)
                fn(St.rearrange("p j n -> p (j n)"), PS[:, 4, :], ACT.Copy).then_inc(s["St_ok"], 1)
                act_.wait_ge(s["qS_ok"], n + 1)
                for e in range(2):
                    for t in range(TT):
                        d = SECOND.index(t)
                        last = fn(qS[:, 2 * e + t, :], PS[:, 6, (2 * e + t) * P:(2 * e + t + 1) * P], ACT.Copy,
                                  scale=cf[:, 2, t, d, e:e + 1])
                last.then_inc(s["qSs_ok"], 1)
                act_.wait_ge(s["ob_ok"], n + 1)
                for j in range(4):
                    last = fn(qS[:, j, :], ob[:, j, :], ACT.Square, accum_out=oss[:, j:j + 1])
                last.then_inc(s["oss_ok"], 1)
                act_.wait_ge(s["oss_ok"], n + 1)
                fn(orms, oss, ACT.Sqrt, bias=eps[:, 0:1], scale=1.0 / DE).then_inc(s["orms_ok"], 1)
                act_.wait_ge(s["ogT_ok"], n + 1)
                fn(oTh[:, bass.ds(pp * 2 + 2, 2), :], PS[:, 2, :].rearrange("p (e s) -> p e s", e=2), ACT.Copy)
                fn(odT, PS[:, 2, :].rearrange("p (e s) -> p e s", e=2), ACT.Copy).then_inc(s["oh_ok"], 1)

            def final(l, m):
                high(Q_FIN + 3, l)
                high(Q_FIN + 4, l)
                act_.wait_ge(s["used"], l * NQ + Q_FIN + 2)
                fn(GS2[:, 0, :], PS[:, 2, :], ACT.Sigmoid).then_inc(s["gt_ok"], 1)
                high(Q_FIN + 5, l)
                act_.wait_ge(s["used"], l * NQ + Q_FIN + 4)
                fn(GS2[:, 1, :], PS[:, 3, :], ACT.Sigmoid).then_inc(s["gt_ok"], 1)
                high(Q_FIN + 6, l)
                for dc in range(KC):
                    act_.wait_ge(s["y_ok"], at(l, KC, dc + 1))
                    if dc >= 2:
                        act_.wait_ge(s["used"], l * NQ + q_rows(dc - 2) + 1)
                    fn(ACh[:, dc % 2, 0:S], yT[:, dc % 2, :], ACT.Copy).then_inc(s["ach_ok"], 1)
                    for q in (Q_FIN + 7 + 2 * dc, Q_FIN + 8 + 2 * dc):
                        if q < Q_FFN[1]:
                            high(q, l)
                act_.wait_ge(s["used"], l * NQ + Q_FFN[1])
                roots(lambda t: bank(4 + 2 * t, 2), m, "pssq_ok", "prms_ok")
                act_.wait_ge(s["x_up"], at(m, TT, TT))

            act_.wait_ge(s["sd"], SD_ANGLE)
            fn(cs[:, :, :, :].rearrange("p w t f -> p (w t f)"), angle, ACT.Sin).then_inc(s["sa"], 1)
            act_.wait_ge(s["sd"], SD_COLS)
            fn(ccol[:, :], cols[:, 48:56], ACT.Silu).then_inc(s["sa"], 1)
            act_.wait_ge(s["x_in"], 16)
            with act_.Fori(0, DEPTH) as l:
                norm(l * 3, l, Q_FFN[0])
                ffn(l, 0, l * 3)
                norm(l * 3 + 1, l, None)
                attention(l)
                coefficients(l)
                with act_.Fori(0, PAIRS) as pp:
                    pair(l, pp)
                final(l, l * 3 + 1)
                norm(l * 3 + 2, l, Q_FFN[1])
                ffn(l, 1, l * 3 + 2)

        @block.vector
        def _(dve):
            v = nc.vector

            def ada_block(a, kc, half):
                dve.wait_ge(s[f"ada_land{half}"], (a * KC + kc + 1) * 16)
                if not (isinstance(kc, int) and kc == 0 and half == 0):
                    dve.wait_ge(s["ada_step"], a * 2 * KC + kc * 2 + half)
                cols_ = slice(half * (3 * D // 2), (half + 1) * (3 * D // 2))
                v.scalar_tensor_tensor(acc[:, cols_], ADA[:, half, :],
                                       ccol[:, kc:kc + 1] if isinstance(kc, int) else ccol[:, bass.ds(kc, 1)],
                                       acc[:, cols_], ALU.mult, ALU.add).then_inc(s["ada_step"], 1)

            def mod_finish(a, l, sub, end_of_layer=False):
                dve.wait_ge(s["modps"], a + 1)
                dve.wait_ge(s["gpost_in"], (a + 1) * 16)
                shifts = v.tensor_copy(modB[:, :], PS[:, 0, 0:KC])
                if end_of_layer:
                    shifts.then_inc(s["layer_done"], 1)
                v.scalar_tensor_tensor(modA[:, :], PS[:, 0, KC:2 * KC], 1.0, cols[:, bass.ds(l * 24 + sub * KC, KC)],
                                       ALU.add, ALU.mult)
                v.scalar_tensor_tensor(gateb[:, :], bank(1, 2), 1.0 if sub == 1 else 0.5, gpost[:, :],
                                       ALU.mult, ALU.mult).then_inc(s["mod_ok"], 1)
                dve.wait_ge(s["mod_ok"], a + 1)
                v.memset(acc[:, :], 0.0).then_inc(s["acc_zero"], 1)

            def low(q, l, i=0, per=0, n=GRAN):
                dve.wait_ge(s["hi_ok"], l * NQ + q + 1 + i * per)
                slot = q % SPLIT_SLOTS
                v.tensor_tensor(LO[:, slot, 0:n], RAW[:, SLOT[q], 0:n], HI[:, slot, 0:n].bitcast(F32), ALU.subtract
                                ).then_inc(s["lo_ok"], 1)

            def norm(m, l, q):
                dve.wait_ge(s["rms_ok"], m + 1)
                v.reciprocal(rr[:, :], rms[:, :]).then_inc(s["rr_ok"], 1)
                dve.wait_ge(s["rr_ok"], m + 1)
                for t in range(TT):
                    v.tensor_scalar(xn[:, t, :], X[:, t, :], rr[:, t:t + 1], None, ALU.mult).then_inc(s["xn_ok"], 1)
                if q is not None:
                    low(q, l)
                dve.wait_ge(s["xt_ok"], at(m, TT, TT))
                for k in (0, 1, 4, 5):
                    v.tensor_scalar(hsum[:, k, :], PS[:, k // 2, (k % 2) * S:(k % 2) * S + S], modA[:, k:k + 1],
                                    modB[:, k:k + 1], ALU.mult, ALU.add).then_inc(s["hs_ok"], 1)
                dve.wait_ge(s["hs_ok"], at(m, 4, 4))
                for kh in range(2):
                    dve.wait_ge(s["hh_ok"], at(m, 2, kh + 1))
                    rows_ = slice(4 * kh, 4 * kh + 4)
                    v.tensor_tensor(hTl[:, rows_, :], hsum[:, rows_, :], hTh[:, rows_, :].bitcast(F32), ALU.subtract
                                    ).then_inc(s["hl_ok"], 1)

            def post(m):
                dve.wait_ge(s["prms_ok"], m + 1)
                v.reciprocal(rr[:, :], rms[:, :]).then_inc(s["prr_ok"], 1)
                dve.wait_ge(s["prr_ok"], m + 1)
                for t in range(TT):
                    v.scalar_tensor_tensor(xn[:, t, :], bank(4 + 2 * t, 2), rr[:, t:t + 1], gateb[:, :],
                                           ALU.mult, ALU.mult).then_inc(s["ptmp_ok"], 1)
                for t in range(TT):
                    dve.wait_ge(s["ptmp_ok"], at(m, TT, t + 1))
                    v.tensor_tensor(X[:, t, :], X[:, t, :], xn[:, t, :], ALU.add).then_inc(s["x_up"], 1)
                dve.wait_ge(s["x_up"], at(m, TT, TT))

            def hidden(l, n, u, i=0):
                par = u % 2
                dve.wait_ge(s["sg_ok"], at(n[0], UNITS, u + 1) + i * 2)
                if u >= 2:
                    dve.wait_ge(s["ach_ok"], n[2] + u - 1 + i * 2)
                    dve.wait_ge(s["acl_ok"], n[2] + u - 1 + i * 2)
                v.tensor_tensor(act[:, par, :], sg[:, par, :], PS[:, 2 * par + 1, :], ALU.mult
                                ).then_inc(s["tmp_ok"], 1)

            def low_hidden(n, u, i=0):
                par = u % 2
                dve.wait_ge(s["ach_ok"], n[2] + u + 1 + i * 2)
                dve.wait_ge(s["tmp_ok"], at(n[0], UNITS, u + 1) + i * 2)
                v.tensor_tensor(ACl[:, par, :], act[:, par, :], ACh[:, par, :].bitcast(F32), ALU.subtract
                                ).then_inc(s["acl_ok"], 1)

            def ffn(l, f, a):
                n, q0 = (l * 2 + f, f, q_hidden(l, f)), Q_FFN[f]

                def step(u, i=0):
                    q = q0 + q_into(u)
                    low(q, l, i, 2 * STEP)
                    low(q + 1, l, i, 2 * STEP)
                    hidden(l, n, u - 1, i)
                    low(q + 2, l, i, 2 * STEP)
                    low(q + 3, l, i, 2 * STEP)
                    low_hidden(n, u - 1, i)
                    low(q + 4, l, i, 2 * STEP)
                    low(q + 5, l, i, 2 * STEP)

                for k in range(1, 4):
                    low(q0 + k, l)
                step(1)
                step(2)
                with dve.Fori(0, 4) as i:
                    for j in range(2):
                        step(3 + j, i)
                        dve.wait_ge(s["bias_in"], (a + 1) * 16)
                        for half in range(2):
                            ada_block(a, i * 2 + j, half)
                hidden(l, n, UNITS - 1)
                low(q0 + N_FFN - 2, l)
                low_hidden(n, UNITS - 1)
                low(q0 + N_FFN - 1, l)

            def attention(l, a):
                with dve.Fori(0, 2) as jj:
                    n = l * 2 + jj
                    for k in range(N_ATT):
                        low(Q_ATT + k, l, jj, N_ATT)
                        if k < KC:
                            dve.wait_ge(s["bias_in"], (a + 1) * 16)
                            ada_block(a, jj * (KC // 2) + k // 2, k % 2)
                    dve.wait_ge(s["used"], l * NQ + Q_ATT + 6 + jj * N_ATT)
                    for t in range(TT):
                        src = bank(2 * t, 2)[:, 0:768].rearrange("p (h w f) -> p h w f", w=2, f=AE // 2)
                        dst = rot[:, t, :].rearrange("p (h w f) -> p h w f", w=2, f=AE // 2)
                        tmp = [rtmp2[t][:, i, :].rearrange("p (h f) -> p h f", f=AE // 2) for i in range(4)]
                        cos = cs[:, 0, t:t + 1, :].to_broadcast([P, 12, AE // 2])
                        sin = cs[:, 1, t:t + 1, :].to_broadcast([P, 12, AE // 2])
                        v.tensor_tensor(tmp[0], src[:, :, 0, :], cos, ALU.mult)
                        v.tensor_tensor(tmp[1], src[:, :, 1, :], sin, ALU.mult)
                        v.tensor_tensor(tmp[2], src[:, :, 1, :], cos, ALU.mult)
                        v.tensor_tensor(tmp[3], src[:, :, 0, :], sin, ALU.mult).then_inc(s["rot_s"], 1)
                        dve.wait_ge(s["rot_s"], at(n, 4, 2 * t + 1))
                        v.tensor_tensor(dst[:, :, 0, :], tmp[0], tmp[1], ALU.subtract)
                        v.tensor_tensor(dst[:, :, 1, :], tmp[2], tmp[3], ALU.add).then_inc(s["rot_s"], 1)
                    dve.wait_ge(s["qt_ok"], at(n, 2, 2))
                    v.tensor_copy(KT.rearrange("p g s -> p (g s)"), bank(0, 2)[:, 0:NG * S]).then_inc(s["kte"], 1)

                    def masked(i):
                        q = i % 2
                        dve.wait_ge(s["sc_ok"], at(n, 4, i + 1))
                        if i >= 2:
                            dve.wait_ge(s["pt_ok"], at(n, 4, i - 1))
                        v.scalar_tensor_tensor(sm[:, i % 2, :], bank(2 + 2 * (i % 2), 2)[:, 0:768], float(AE) ** -0.5,
                                               amask[:, q, :], ALU.mult, ALU.add).then_inc(s["sm_ok"], 1)
                        dve.wait_ge(s["sm_ok"], at(n, 4, i + 1))
                        v.tensor_reduce(nmx[:, i:i + 1], sm[:, i % 2, :], AX.X, ALU.max, negate=True
                                        ).then_inc(s["nm_ok"], 1)

                    def divided(i):
                        hh, q = i // 2, i % 2
                        dve.wait_ge(s["pv_ok"], at(n, 4, i + 1))
                        v.reciprocal(rden[:, i:i + 1], den[:, i:i + 1]).then_inc(s["rd_ok"], 1)
                        dve.wait_ge(s["rd_ok"], at(n, 4, i + 1))
                        v.tensor_scalar(oatt[:, q, bass.ds(jj * P + hh * AE, AE)], PS[:, i % 2, i * AE:(i + 1) * AE],
                                        rden[:, i:i + 1], None, ALU.mult).then_inc(s["oa_ok"], 1)

                    masked(0)
                    masked(1)
                    masked(2)
                    divided(0)
                    masked(3)
                    divided(1)
                    divided(2)
                    divided(3)

                dve.wait_ge(s["oh_ok"], at(l, 1 + PAIRS, 1))
                v.tensor_tensor(oTl[:, 0:2, :], oatT, oTh[:, 0:2, :].bitcast(F32), ALU.subtract).then_inc(s["ol_ok"], 1)

            def coefficients(l):
                low(Q_BA, l, n=KC * 24)
                low(Q_DN, l)
                low(Q_DN + 1, l)
                dve.wait_ge(s["cf_act"], at(l, 7, 2))
                dve.wait_ge(s["ba_in"], 48 * (l + 1))
                v.tensor_scalar(raw[:, :, 0:12], raw[:, :, 0:12], 1.0, None, ALU.add).then_inc(s["cf_dve"], 1)
                dve.wait_ge(s["cf_dve"], at(l, 5, 1))
                v.reciprocal(coef[:, 0].rearrange("p t d h -> p t (d h)"), raw[:, :, 0:12]).then_inc(s["cf_dve"], 1)
                ba = PS[:, 7, 0:48].rearrange("p (t n) -> p t n", t=2)
                v.tensor_tensor(al, ba[:, :, 12:24], dtbb.rearrange("p (o n) -> p o n", o=1).to_broadcast([P, 2, 12]),
                                ALU.add).then_inc(s["cf_dve"], 1)
                dve.wait_ge(s["cf_act"], at(l, 7, 5))
                v.scalar_tensor_tensor(al, al, 0.0, ta, ALU.max, ALU.add).then_inc(s["cf_dve"], 1)
                dve.wait_ge(s["cf_dve"], at(l, 5, 4))
                v.scalar_tensor_tensor(coef[:, 1].rearrange("p t d h -> p t (d h)"), al, -1.0,
                                       ea.rearrange("p (o n) -> p o n", o=1).to_broadcast([P, 2, 12]),
                                       ALU.mult, ALU.mult).then_inc(s["cf_dve"], 1)
                low(Q_DN + 2, l)

            def over_tiles(mask):
                return mask.rearrange("p d (o n) -> p d o n", o=1).to_broadcast([P, 2, TT, P])

            def pair(l, pp):
                n = l * PAIRS + pp
                dve.wait_ge(s["cf_act"], at(l, 7, 7))
                v.tensor_copy(cf.rearrange("p k t d e -> p (k t d) e"),
                              coef.rearrange("p k t d h -> p (k t d) h")[:, :, bass.ds(pp * 2, 2)]
                              ).then_inc(s["cfp_ok"], 1)
                v.tensor_copy(cwp.rearrange("p a (y e) -> p (a y) e", e=2),
                              cw[:, bass.ds(l, 1), :].rearrange("p l (a h) -> p (l a) h", h=DH)[:, :, bass.ds(pp * 2, 2)]
                              ).then_inc(s["cfp_ok"], 1)
                low(Q_DN + 3, l, pp, N_DN)
                low(Q_DN + 4, l, pp, N_DN)
                dve.wait_ge(s["cb_ok"], at(n, 3, 1))
                v.memset(cb[:, :, 0:2], 0.0)
                v.memset(cb[:, :, S + 2:S + 4], 0.0).then_inc(s["pad_ok"], 1)
                dve.wait_ge(s["pad_ok"], n + 1)
                dve.wait_ge(s["cfp_ok"], at(n, 2, 2))
                for y in range(3):
                    dve.wait_ge(s["cb_ok"], at(n, 3, y + 1))
                    for a in range(TAPS):
                        for e in range(2):
                            i = 2 * y + e
                            if a == 0:
                                v.tensor_scalar(qs[:, i, :], cb[:, i, 0:S], cwp[:, 0, i:i + 1], None, ALU.mult
                                                ).then_inc(s["cv_s"], 1)
                                continue
                            dve.wait_ge(s["cv_s"], at(n, 30, 10 * y + 2 * (a - 1) + e + 1))
                            v.scalar_tensor_tensor(qs[:, i, :], cb[:, i, a:a + S], cwp[:, a, i:i + 1], qs[:, i, :],
                                                   ALU.mult, ALU.add).then_inc(s["cv_s"], 1)
                    if y < 2:
                        low(Q_DN + 5 + 2 * y, l, pp, N_DN)
                        low(Q_DN + 6 + 2 * y, l, pp, N_DN)
                low(Q_DN + 9, l, pp, N_DN)
                low(Q_DN + 10, l, pp, N_DN)
                dve.wait_ge(s["rs_ok"], at(n, 2, 2))
                for i in range(4):
                    e, w = i % 2, 1 - i // 2
                    v.scalar_tensor_tensor(kqn[:, e, :, w, :], qs[:, i, :].rearrange("p (t n) -> p t n", t=TT),
                                           float(DE) ** -0.5 if w else 1.0,
                                           rs[:, i * S:(i + 1) * S].rearrange("p (t n) -> p t n", t=TT),
                                           ALU.mult, ALU.mult).then_inc(s["kqn_ok"], 1)
                low(Q_DN + 11, l, pp, N_DN)
                dve.wait_ge(s["tk_ok"], n + 1)
                v.tensor_copy(vtok.rearrange("p e t n -> p (e t n)"), PS[:, 7, :]).then_inc(s["vtok_ok"], 1)
                for e in range(2):
                    dve.wait_ge(s["kk_ok"], at(n, 2, e + 1))
                    dve.wait_ge(s["etm_ok"], at(n, 4, 2 * e + 2))
                    for d in range(2):
                        for t in range(TT):
                            v.scalar_tensor_tensor(NB[:, e, d, t, :], PS[:, 4 + e, t * 256:t * 256 + P],
                                                   cf[:, 0, t, d, e:e + 1], ET[:, e, d, t, :], ALU.mult, ALU.mult
                                                   ).then_inc(s["nb_ok"], 1)
                for e in range(2):
                    kq = PS[:, 4 + e, :].rearrange("p (t w n) -> p t w n", t=TT, w=2)[:, :, 1, :]
                    for d in range(2):
                        v.tensor_tensor(AT[:, e, d], kq, ET[:, e, d], ALU.mult).then_inc(s["at_ok"], 1)
                dve.wait_ge(s["nb_ok"], at(n, 8, 8))
                for e in range(2):
                    dve.wait_ge(s["nbT_ok"], at(n, 2, e + 1))
                    v.tensor_tensor(A[:, e], PS[:, 2 + e, :].rearrange("p (d t n) -> p d t n", d=2, t=TT),
                                    over_tiles(level[:, 0]), ALU.mult).then_inc(s["d1_s"], 1)
                    for d in range(2):
                        last = v.tensor_tensor(DT[:, e, d], NB[:, e, d],
                                               level[:, 0, 1 - d:2 - d, :].to_broadcast([P, TT, P]), ALU.mult)
                    last.then_inc(s["d1_s"], 1)
                    eye = ident.rearrange("p (o n) -> p o n", o=1).to_broadcast([P, 4, P])
                    dve.wait_ge(s["d1_s"], at(n, 6, 3 * e + 2))
                    v.tensor_tensor(Dm[:, e].rearrange("p d t n -> p (d t) n"), A[:, e].rearrange("p d t n -> p (d t) n"),
                                    eye, ALU.add).then_inc(s["l_D"], 1)
                    v.tensor_tensor(DT[:, e].rearrange("p d t n -> p (d t) n"), DT[:, e].rearrange("p d t n -> p (d t) n"),
                                    eye, ALU.add).then_inc(s["d1_s"], 1)
                for k in range(3):
                    low(Q_DN + N_DN + k, l, pp, N_DN)
                dve.wait_ge(s["ktok_ok"], n + 1)
                for e in range(2):
                    for d in range(2):
                        t = SECOND[d]
                        v.tensor_scalar(kg[:, 2 * e + d, :], ktok[:, e, t, :], cf[:, 2, t, d, e:e + 1], -1.0,
                                        ALU.mult, ALU.mult).then_inc(s["kg_ok"], 1)
                        t = FIRST[d]
                        v.tensor_scalar(kd[:, e, d, :], ktok[:, e, t, :], cf[:, 3, t, d, e:e + 1], None,
                                        ALU.mult).then_inc(s["kd_ok"], 1)

                def level_up(w):
                    k = n * 2 * (LEVELS - 1) + 2 * w
                    for e in range(2):
                        dve.wait_ge(s["l_a"], k + e + 1)
                        m = level[:, w + 1] if isinstance(w, int) else \
                            level[:, bass.ds(w + 1, 1)].rearrange("p v d n -> p (v d) n")
                        v.tensor_tensor(A[:, e], PS[:, 2 + e, :].rearrange("p (d t n) -> p d t n", d=2, t=TT),
                                        over_tiles(m), ALU.mult).then_inc(s["l_A"], 1)
                    for e in range(2):
                        dve.wait_ge(s["l_b"], k + e + 1)
                        v.tensor_tensor(DT[:, e].rearrange("p d t n -> p (d t n)"),
                                        DT[:, e].rearrange("p d t n -> p (d t n)"), PS[:, 4 + e, :], ALU.add
                                        ).then_inc(s["l_DT"], 1)

                with dve.Fori(0, LEVELS - 2) as w:
                    level_up(w)
                level_up(LEVELS - 2)
                dve.wait_ge(s["wu_ok"], at(n, 2, 1))
                for e in range(2):
                    for d in range(2):
                        t = FIRST[d]
                        v.tensor_scalar(vn[:, e, d, t, :], PS[:, 3, (2 * e + d) * P:(2 * e + d + 1) * P],
                                        cf[:, 0, t, d, e:e + 1], None, ALU.mult).then_inc(s["vn1_ok"], 1)
                dve.wait_ge(s["v2_ok"], n + 1)
                for e in range(2):
                    for d in range(2):
                        t = SECOND[d]
                        v.tensor_scalar(vn[:, e, d, t, :], PS[:, 5, (2 * e + d) * P:(2 * e + d + 1) * P],
                                        cf[:, 0, t, d, e:e + 1], None, ALU.mult).then_inc(s["vn2_ok"], 1)
                dve.wait_ge(s["o_ok"], n + 1)
                dve.wait_ge(s["qSs_ok"], n + 1)
                v.tensor_tensor(ob.rearrange("p j n -> p (j n)"), PS[:, 7, :], qS.rearrange("p j n -> p (j n)"),
                                ALU.add).then_inc(s["ob_ok"], 1)
                dve.wait_ge(s["orms_ok"], n + 1)
                v.reciprocal(orr, orms).then_inc(s["orr_ok"], 1)
                dve.wait_ge(s["orr_ok"], n + 1)
                dve.wait_ge(s["ob_ok"], n + 1)
                for j in range(4):
                    v.scalar_tensor_tensor(og[:, j, :], ob[:, j, :], orr[:, j:j + 1], nw, ALU.mult, ALU.mult
                                           ).then_inc(s["on_ok"], 1)
                dve.wait_ge(s["on_ok"], at(n, 4, 4))
                dve.wait_ge(s["z_ok"], n + 1)
                v.tensor_tensor(og.rearrange("p (e t) n -> p e t n", e=2), og.rearrange("p (e t) n -> p e t n", e=2),
                                zs.rearrange("p t (e n) -> p e t n", e=2), ALU.mult).then_inc(s["og_ok"], 1)
                dve.wait_ge(s["oh_ok"], at(l, 1 + PAIRS, 2 + pp))
                v.tensor_tensor(oTl[:, bass.ds(pp * 2 + 2, 2), :], odT, oTh[:, bass.ds(pp * 2 + 2, 2), :].bitcast(F32),
                                ALU.subtract).then_inc(s["ol_ok"], 1)

            def final(l):
                for k in range(3, 7):
                    low(Q_FIN + k, l)
                for dc in range(KC):
                    par = dc % 2
                    dve.wait_ge(s["used"], l * NQ + q_branch(dc) + 1)
                    dve.wait_ge(s["gs_ok"], at(l, 2 * PAIRS, 2 * PAIRS))
                    dve.wait_ge(s["gt_ok"], at(l, 2, 2))
                    if dc >= 2:
                        dve.wait_ge(s["y_ok"], at(l, KC, dc - 1))
                    gate = GS[:, dc, :] if dc < 6 else GS2[:, dc - 6, :]
                    v.tensor_tensor(m12[:, par, :], gate, PS[:, par, :], ALU.mult).then_inc(s["m12_ok"], 1)
                    dve.wait_ge(s["m12_ok"], at(l, KC, dc + 1))
                    if dc >= 2:
                        dve.wait_ge(s["ach_ok"], q_hidden(l, 0) + UNITS + dc - 1)
                        dve.wait_ge(s["acl_ok"], q_hidden(l, 0) + UNITS + dc - 1)
                    v.tensor_tensor(yT[:, par, :], m12[:, par, 0:S], m12[:, par, S:2 * S], ALU.add
                                    ).then_inc(s["y_ok"], 1)
                    dve.wait_ge(s["y_ok"], at(l, KC, dc + 1))
                    dve.wait_ge(s["ach_ok"], q_hidden(l, 0) + UNITS + dc + 1)
                    v.tensor_tensor(ACl[:, par, 0:S], yT[:, par, :], ACh[:, par, 0:S].bitcast(F32), ALU.subtract
                                    ).then_inc(s["acl_ok"], 1)
                    for q in (Q_FIN + 7 + 2 * dc, Q_FIN + 8 + 2 * dc):
                        if q < Q_FFN[1]:
                            low(q, l)

            made = [0]

            def link(instruction):
                made[0] += 1
                instruction.then_inc(s["sd"], 1)
                dve.wait_ge(s["sd"], made[0])

            v.memset(ones[:, :], 1.0).then_inc(s["layer_done"], 1)
            v.memset(acc[:, :], 0.0).then_inc(s["acc_zero"], 1)
            v.memset(eps[:, :], EPS).then_inc(s["setup_dve"], 1)
            dve.wait_ge(s["setup_dve"], 1)
            dve.wait_ge(s["pos_in"], 16)
            dve.wait_ge(s["table_in"], 16)
            link(v.tensor_copy(posf[:, :], posi[:, :]))
            for t in range(TT):
                link(v.tensor_scalar(ang[:, t, :], freq, posf[:, t:t + 1], None, ALU.mult))
            angf = ang.rearrange("p t f -> p (t f)")
            W = TT * AE // 2
            for k, quarter in ((0, 0.25), (1, 0.0)):
                turns, a = turn_[:, k * W:(k + 1) * W], angle[:, k * W:(k + 1) * W]
                link(v.tensor_scalar(turns, angf, 1.0 / TWO_PI, quarter, ALU.mult, ALU.add))
                link(v.tensor_scalar(turns, turns, ROUND, None, ALU.add))
                link(v.tensor_scalar(turns, turns, -ROUND, None, ALU.add))
                link(v.scalar_tensor_tensor(a, turns, -PI1, angf, ALU.mult, ALU.add))
                link(v.scalar_tensor_tensor(a, turns, -PI2, a, ALU.mult, ALU.add))
                link(v.scalar_tensor_tensor(a, turns, -PI3, a, ALU.mult, ALU.add))
                link(v.tensor_scalar(a, a, quarter * TWO_PI, None, ALU.add))
                link(v.tensor_scalar(a, a, 3.1415925, -3.1415925, ALU.min, ALU.max))
            assert made[0] == SD_ANGLE
            dve.wait_ge(s["setup_pe"], 1)
            link(v.tensor_copy(cols[:, :], PS[:, 7, 0:56]))
            for l in range(DEPTH):
                link(v.tensor_copy(cw[:, l, :], PS[:, 7, 128 * (l + 1):128 * (l + 1) + 90]))
            assert made[0] == SD_COLS
            dve.wait_ge(s["sa"], 2)
            dve.wait_ge(s["bias_in"], 16)
            for kc in range(KC):
                for half in range(2):
                    ada_block(0, kc, half)
            mod_finish(0, 0, 0)
            dve.wait_ge(s["x_in"], 16)
            with dve.Fori(0, DEPTH) as l:
                norm(l * 3, l, Q_FFN[0])
                ffn(l, 0, l * 3 + 1)
                post(l * 3)
                mod_finish(l * 3 + 1, l, 1)
                norm(l * 3 + 1, l, None)
                attention(l, l * 3 + 2)
                coefficients(l)
                with dve.Fori(0, PAIRS) as pp:
                    pair(l, pp)
                final(l)
                post(l * 3 + 1)
                mod_finish(l * 3 + 2, l, 2)
                norm(l * 3 + 2, l, Q_FFN[1])
                ffn(l, 1, l * 3 + 3)
                post(l * 3 + 2)
                mod_finish(l * 3 + 3, l * -1 + 1, 0, end_of_layer=True)


_INS = ['x', 'c', 'positions', 'w_ada', 'b_ada', 'norm_pre', 'norm_post', 'ffn_w_in', 'ffn_w_out', 'w_in', 'conv_w',
        'a_log', 'dt_bias', 'dn_norm_w', 'w_branch_att', 'w_branch_dn', 'w_out']


def kernel(**inputs):
    import concourse.bacc as bacc
    from concourse.bass_utils import run_bass_kernel_spmd

    nc = bacc.Bacc("TRN2", target_bir_lowering=False, num_devices=1)
    arrays, args = {}, []
    given = [(name, np.ascontiguousarray(inputs[name])) for name in _INS] + [("table", constant_table())]
    for name, a in given:
        arrays[f"in_{name}"] = a
        args.append(nc.dram_tensor(f"in_{name}", a.shape, mybir.dt.from_np(a.dtype), kind="ExternalInput").ap())
    out = nc.dram_tensor("out_x", (1, S, D), F32, kind="ExternalOutput").ap()
    build(nc, *args, out)
    return run_bass_kernel_spmd(nc, [arrays], core_ids=[0]).results[0]["out_x"]
```

```python
from contextlib import ExitStack

import numpy as np

import concourse.bass as bass
from concourse import mybir

F32 = mybir.dt.float32
F32R = mybir.dt.float32r
I32 = mybir.dt.int32
ALU = mybir.AluOpType
ACT = mybir.ActivationFunctionType
AX = mybir.AxisListType

P = 128
D = 1024
S = 256
DEPTH = 2
KC = D // P
TT = S // P
FFN = ((8 * D // 3 + 127) // 128) * 128
FC = FFN // P
UNITS = FC // 2
SUBS = 3
GROUPS = ((128, 1), (512, 4), (2048, 16))
NG = len(GROUPS)
AH, AE = 4, 64
AW = NG * AH * AE
DH, DE = 6, 128
DW = DH * DE
TAPS = 5
Q0, K0, V0 = 0, AW, 2 * AW
DN0 = 3 * AW
Z0 = DN0 + 3 * DW
B0 = Z0 + DW
GA0 = B0 + 4 * DH
GD0 = GA0 + D
EPS = 1e-6
NEG = -1e30
THETA = 10000.0
SD_ANGLE = 3 + 2 * 8
SD_COLS = SD_ANGLE + 3
LEVELS = 7
PAIRS = DH // 2
U_ALL = 14400
TWO_PI = 6.283185307179586
PI1, PI2 = 6.28125, 0.0019350051879882812
PI3 = TWO_PI - PI1 - PI2
ROUND = 12582912.0
FWD, BWD = 0, 1
FIRST = (0, 1)
SECOND = (1, 0)

C_ID = 0
C_INC = C_ID + P
C_AFTER = C_INC + 2 * P
C_LEVEL = C_AFTER + 2 * P
C_MASK = C_LEVEL + LEVELS * 2 * P
C_FREQ = C_MASK + TT * NG * S
C_ALL = C_FREQ + AE // 2


FIRST_MORE = 6


def constant_table():
    t = np.zeros((P, C_ALL), np.float32)
    i = np.arange(P)
    t[:, C_ID:C_ID + P] = np.eye(P)
    inc = (i[:, None] <= i[None, :])
    for d, m in ((FWD, inc), (BWD, inc.T)):
        t[:, C_INC + d * P:C_INC + (d + 1) * P] = m
        t[:, C_AFTER + d * P:C_AFTER + (d + 1) * P] = ~m
    for v in range(LEVELS):
        s = 1 << v
        low = (i[:, None] // s % 2 == 1) & (i[:, None] // (2 * s) == i[None, :] // (2 * s)) & (i[None, :] // s % 2 == 0)
        for d, m in ((FWD, low), (BWD, low.T)):
            at = C_LEVEL + (2 * v + d) * P
            t[:, at:at + P] = -1.0 * m
    keys = np.arange(S)
    for q in range(TT):
        query = q * P + i[:, None]
        for g, (window, dil) in enumerate(GROUPS):
            diff = query - keys[None, :]
            ok = (diff % dil == 0) & (np.abs(diff) // dil <= window // (2 * dil))
            at = C_MASK + (q * NG + g) * S
            t[:, at:at + S] = np.where(ok, 0.0, NEG)
    half = AE // 2
    t[:, C_FREQ:] = np.power(np.float32(THETA), -np.arange(half, dtype=np.float32) * np.float32(2.0) / np.float32(AE))
    return t


GRAN = 1024
RAW_SLOTS, SPLIT_SLOTS = 6, 3
STEP = 6
Q_FFN = (0, 141)
N_FFN = STEP * UNITS
Q_ATT = N_FFN
N_ATT = 9
Q_BA = Q_ATT + 2 * N_ATT
Q_DN = Q_BA + 1
N_DN = 12
Q_FIN = Q_DN + PAIRS * N_DN
N_FIN = 4 + 2 * KC
NQ = Q_FIN + N_FIN + N_FFN
assert Q_FFN[1] == Q_FIN + N_FIN and N_DN % RAW_SLOTS == 0 and NQ % SPLIT_SLOTS == 0


def q_into(u):
    return 0 if isinstance(u, int) and u == 0 else STEP * u - 2


def q_out(u):
    return N_FFN - 2 if u == UNITS - 1 else STEP * u + STEP + 2


def q_hidden(l, f):
    return l * (2 * UNITS + KC) + f * (UNITS + KC)


def q_branch(dc):
    return Q_FIN + 4 + (0 if dc == 0 else 2 * dc - 1)


def q_rows(dc):
    return Q_FIN + 4 + (15 if dc == KC - 1 else 2 * dc + 2)


def raw_places():
    slot, loads = [0] * NQ, [1] * NQ
    for q in range(NQ):
        if q < Q_ATT:
            slot[q] = q % RAW_SLOTS
        elif q < Q_BA:
            k = (q - Q_ATT) % N_ATT
            slot[q], loads[q] = k % RAW_SLOTS, 2 if k < 6 else 1
        else:
            slot[q] = (q - Q_BA) % RAW_SLOTS
    for dc in range(KC):
        loads[q_branch(dc)] = 2
    return slot, loads


SLOT, LOADS = raw_places()


def landed(q, l, i=0, per=0):
    same = [p for p in range(NQ) if SLOT[p] == SLOT[q]]
    layer = 16 * sum(LOADS[p] for p in same)
    upto = 16 * sum(LOADS[p] for p in same if p <= q)
    turn = 16 * sum(LOADS[p] for p in same if q < p <= q + per)
    return l * layer + upto + i * turn


def at(n, per, k):
    return n * per + k


def build(nc, x, c, positions, w_ada, b_ada, norm_pre, norm_post, ffn_w_in, ffn_w_out, w_in, conv_w,
          a_log, dt_bias, dn_norm_w, w_branch_att, w_branch_dn, w_out, table, out):
    with ExitStack() as ctx:
        def sb(name, shape, dt=F32):
            return ctx.enter_context(nc.sbuf_tensor(name, shape, dt))

        def sem(name):
            return ctx.enter_context(nc.semaphore(name))

        PS = ctx.enter_context(nc.psum_tensor("PS", [P, 8, 512], F32))

        def bank(b, n=1):
            return PS[:, b:b + n, :].rearrange("p b c -> p (b c)")

        X = sb("X", [P, TT, D])
        hTh = sb("hTh", [P, KC, S], F32R)
        hTl = sb("hTl", [P, KC, S], F32R)
        RAW = sb("RAW", [P, RAW_SLOTS, GRAN])
        HI = sb("HI", [P, SPLIT_SLOTS, GRAN], F32R)
        LO = sb("LO", [P, SPLIT_SLOTS, GRAN], F32R)
        ACh = sb("ACh", [P, 2, 512], F32R)
        ACl = sb("ACl", [P, 2, 512], F32R)
        ADA = sb("ADA", [P, 2, 3 * D // 2])
        acc = sb("acc", [P, 3 * D])
        gpost = sb("gpost", [P, D])
        gateb = sb("gateb", [P, D])
        modA = sb("modA", [P, KC])
        modB = sb("modB", [P, KC])
        CT = sb("CT", [P, C_ALL])
        ones = sb("ones", [P, P])
        eps = sb("eps", [P, 2])
        spare = sb("spare", [P, 2])
        rowsb = sb("rowsb", [P, P])
        cvrows = sb("cvrows", [P, DEPTH, P])
        cols = sb("cols", [P, DEPTH * SUBS * KC + KC])
        ccol = sb("ccol", [P, KC])
        cw = sb("cw", [P, DEPTH, TAPS * 18])
        posi = sb("posi", [P, TT], I32)
        posf = sb("posf", [P, TT])
        cs = sb("cs", [P, 2, TT, AE // 2])
        ssq = sb("ssq", [P, 2])
        rms = sb("rms", [P, 2])
        rr = sb("rr", [P, 2])
        oTh = sb("oTh", [P, 2 + DH, S], F32R)
        oTl = sb("oTl", [P, 2 + DH, S], F32R)
        small = sb("small", [P, 2 * 12 + P])
        alogb, dtbb, nw = small[:, 0:12], small[:, 12:24], small[:, 24:24 + P]
        U = sb("U", [P, U_ALL])

        ident = CT[:, C_ID:C_ID + P]
        inc = CT[:, C_INC:C_INC + 2 * P].rearrange("p (d n) -> p d n", d=2)
        after = CT[:, C_AFTER:C_AFTER + 2 * P].rearrange("p (d n) -> p d n", d=2)
        level = CT[:, C_LEVEL:C_LEVEL + LEVELS * 2 * P].rearrange("p (v d n) -> p v d n", v=LEVELS, d=2)
        amask = CT[:, C_MASK:C_MASK + TT * NG * S].rearrange("p (q n) -> p q n", q=TT)
        freq = CT[:, C_FREQ:C_FREQ + AE // 2]

        top = [0]

        def carve(n, start=None):
            if start is not None:
                top[0] = start
            a = top[0]
            top[0] += n
            assert top[0] <= U_ALL, top
            return U[:, a:a + n]

        xn = carve(TT * D, 0).rearrange("p (t d) -> p t d", t=TT)
        sg = carve(2 * 512, 0).rearrange("p (b n) -> p b n", b=2)
        act = carve(2 * 512).rearrange("p (b n) -> p b n", b=2)
        m12 = carve(2 * 512, 0).rearrange("p (b n) -> p b n", b=2)
        yT = carve(2 * S).rearrange("p (b s) -> p b s", b=2)
        GS2 = carve(2 * 512).rearrange("p (c n) -> p c n", c=2)
        junk = carve(2 * 1024, 2048).rearrange("p (t d) -> p t d", t=TT)
        ang = carve(TT * AE // 2, 0).rearrange("p (t f) -> p t f", t=TT)
        turn_ = carve(2 * TT * AE // 2)
        angle = carve(2 * TT * AE // 2)
        hsum = carve(KC * S, 12288).rearrange("p (k s) -> p k s", k=KC)
        first_blocks = carve(FIRST_MORE * (3 * D // 2), 4096).rearrange("p (b n) -> p b n", b=FIRST_MORE)
        rot = carve(TT * 768, 4096).rearrange("p (t n) -> p t n", t=TT)
        rtmp = carve(4 * 384).rearrange("p (m n) -> p m n", m=4)
        vat = carve(TT * NG * P).rearrange("p (t n) -> p t n", t=TT)
        QT = carve(NG * S).rearrange("p (g s) -> p g s", g=NG)
        KT = carve(NG * S).rearrange("p (g s) -> p g s", g=NG)
        smf = carve(2 * 768)
        sm = smf.rearrange("p (b n) -> p b n", b=2)
        rtmp2 = (rtmp, smf.rearrange("p (m n) -> p m n", m=4))
        prT = carve(2 * 768).rearrange("p (b n) -> p b n", b=2)
        oatT = carve(2 * S, 2048).rearrange("p (c s) -> p c s", c=2)
        oatt = carve(TT * 256, 3072).rearrange("p (t n) -> p t n", t=TT)
        nmx = carve(4)
        den = carve(4)
        rden = carve(4)
        coef = carve(4 * 2 * 2 * DH, 0).rearrange("p (k t d h) -> p k t d h", k=4, t=2, d=2)
        raw = carve(2 * 24).rearrange("p (t n) -> p t n", t=2)
        al = carve(24).rearrange("p (t n) -> p t n", t=2)
        ta = carve(24).rearrange("p (t n) -> p t n", t=2)
        cf = carve(16 * 2).rearrange("p (k t d e) -> p k t d e", k=4, t=2, d=2)
        cwp = carve(30).rearrange("p (a i) -> p a i", a=TAPS)
        oss = carve(4)
        orr = carve(4)
        orms = carve(4)
        ea = carve(12)
        assert top[0] <= 1024
        cb = carve(6 * 260, 4096).rearrange("p (i s) -> p i s", i=6)
        qs = carve(6 * S).rearrange("p (i s) -> p i s", i=6)
        kqn = carve(1024).rearrange("p (e t w n) -> p e t w n", e=2, t=2, w=2)
        ktok = carve(512).rearrange("p (e t n) -> p e t n", e=2, t=2)
        vtok = carve(512).rearrange("p (e t n) -> p e t n", e=2, t=2)
        zs = carve(512).rearrange("p (t n) -> p t n", t=2)
        kd = carve(512).rearrange("p (e d n) -> p e d n", e=2, d=2)
        four = "p (e d t n) -> p e d t n"
        R = carve(1024).rearrange(four, e=2, d=2, t=2)
        ET = carve(1024).rearrange(four, e=2, d=2, t=2)
        NB = carve(1024).rearrange(four, e=2, d=2, t=2)
        AT = carve(1024).rearrange(four, e=2, d=2, t=2)
        sq = carve(1024, 1024)
        rs = carve(1024)
        Dm = carve(1024, 1024).rearrange(four, e=2, d=2, t=2)
        DT = carve(1024).rearrange(four, e=2, d=2, t=2)
        A = carve(1024, 3072).rearrange(four, e=2, d=2, t=2)
        def flat(v):
            return v.rearrange("p e d t n -> p (e d t) n")

        kg, wT = flat(R)[:, 0:4, :], flat(R)[:, 4:8, :]
        St, qS = flat(NB)[:, 0:4, :], flat(NB)[:, 4:8, :]
        ob, og = flat(A)[:, 0:4, :], flat(A)[:, 4:8, :]
        vn = ET
        odT = qs[:, 0:2, :]
        GS = ADA[:, :, :].rearrange("p a n -> p (a n)").rearrange("p (c n) -> p c n", c=6)

        names = (
            "layer_done sd sa pad_ok x_in table_in rows_in pos_in gpost_in ada_land0 ada_land1 ada_land2 "
            "ada_land3 ada_land4 ada_land5 ada_land6 ada_land7 bias_in acc_zero ada_step hi_ok lo_ok used land0 "
            "land1 land2 land3 land4 land5 tmp_ok ach_ok acl_ok m12_ok y_ok hs_ok hsa_ok hh_ok hl_ok oh_ok "
            "ol_ok gt_ok gs_ok modps mod_ok setup_pe setup_dve modc_ok gateps ssq_ok rms_ok rr_ok xn_ok xt_ok "
            "sg_ok pssq_ok prms_ok prr_ok ptmp_ok x_up v_ok rot_s qt_ok qte kte sc_ok sm_ok nm_ok p_ok pt_ok "
            "pte_ok pv_ok rd_ok oa_ok oat_ok ba_in cf_dve cf_act cumsum_ok cb_ok z_ok cv_s si_ok sq_ok ss_ok "
            "rs_ok kqn_ok tk_ok ktok_ok vtok_ok kk_ok cfp_ok R_ok et_ok ete_ok etm_ok nb_ok at_ok nbT_ok d1_s "
            "l_a l_A l_b l_DT l_c l_D kg_ok kd_ok wu_ok wT_ok vn1_ok s_ok St_ok v2_ok vn2_ok qS_ok qSs_ok o_ok "
            "ob_ok oss_ok orms_ok orr_ok on_ok og_ok ogT_ok stored").split()
        s = {n: sem(n) for n in names}

        block = ctx.enter_context(nc.Block())

        @block.sync
        def _(sp):
            def load(q, l, src, dst=None, i=0, lag=RAW_SLOTS, per=0, first=True):
                if first and q - lag >= 0:
                    sp.wait_ge(s["lo_ok"], l * NQ + q - lag + 1 + i * per)
                raw = RAW[:, SLOT[q], :]
                sp.dma_start(raw if dst is None else dst(raw), src).then_inc(s[f"land{SLOT[q]}"], 16)

            def wide(k):
                return lambda raw: raw.rearrange("p (k n) -> p k n", k=k)

            def into_hidden(l, f, u, i=0, lag=RAW_SLOTS):
                q0 = Q_FFN[f] + q_into(u)
                for j in range(4):
                    half, kh = j // 2, j % 2
                    w = ffn_w_in[l, f][kh * 512:(kh + 1) * 512, bass.ds(i * 512 + u * 256 + half * FFN, 256)] \
                        if not isinstance(i, int) else \
                        ffn_w_in[l, f][kh * 512:(kh + 1) * 512, u * 256 + half * FFN:u * 256 + half * FFN + 256]
                    load(q0 + j, l, w.rearrange("(k p) n -> p k n", p=P), wide(4), i, lag, 2 * STEP)

            def out_of_hidden(l, f, u, i=0):
                q0 = Q_FFN[f] + q_out(u)
                for c in range(2):
                    rows = bass.ds(i * 512 + u * 256 + c * P, P) if not isinstance(i, int) else \
                        slice(u * 256 + c * P, u * 256 + (c + 1) * P)
                    load(q0 + c, l, ffn_w_out[l, f][rows, :], None, i, RAW_SLOTS, 2 * STEP)

            def ffn(l, f):
                into_hidden(l, f, 0)
                into_hidden(l, f, 1)
                out_of_hidden(l, f, 0)
                into_hidden(l, f, 2)
                out_of_hidden(l, f, 1)
                with sp.Fori(0, 4) as i:
                    for u in (3, 4):
                        into_hidden(l, f, u, i)
                        out_of_hidden(l, f, u - 1, i)
                out_of_hidden(l, f, UNITS - 1)

            def kview(w, rows, n0, n):
                return w[rows, n0 if isinstance(n0, slice) else bass.ds(n0, n)].rearrange("(k p) n -> p k n", p=P)

            def attention(l):
                with sp.Fori(0, 2) as jj:
                    for k in range(6):
                        g, kh = k // 2, k % 2
                        for w, off in ((0, Q0), (1, K0)):
                            load(Q_ATT + k, l, kview(w_in[l], slice(kh * 512, (kh + 1) * 512),
                                                     jj * P + off + g * AH * AE, P),
                                 lambda raw: raw.rearrange("p (k w n) -> p k w n", k=4, w=2)[:, :, w, :],
                                 jj, 3 if k < 3 else RAW_SLOTS, N_ATT, first=(w == 0))
                    for g in range(NG):
                        load(Q_ATT + 6 + g, l, kview(w_in[l], slice(0, D), jj * P + V0 + g * AH * AE, P), wide(KC),
                             jj, RAW_SLOTS, N_ATT)

            def small_weights(l):
                load(Q_BA, l, kview(w_in[l], slice(0, D), slice(B0, B0 + 24), 24),
                     lambda raw: raw[:, 0:KC * 24].rearrange("p (k n) -> p k n", k=KC), lag=3)
                sp.dma_start(alogb, a_log.rearrange("l d h -> l (d h)")[bass.ds(l, 1), :].to_broadcast([P, 12])
                             ).then_inc(s["ba_in"], 16)
                sp.dma_start(dtbb, dt_bias.rearrange("l d h -> l (d h)")[bass.ds(l, 1), :].to_broadcast([P, 12])
                             ).then_inc(s["ba_in"], 16)
                sp.dma_start(nw, dn_norm_w[bass.ds(l, 1), :].to_broadcast([P, P])).then_inc(s["ba_in"], 16)

            def delta(l):
                with sp.Fori(0, PAIRS) as pp:
                    for y in range(3):
                        for e in range(2):
                            load(Q_DN + 2 * y + e, l, kview(w_in[l], slice(0, D), pp * 256 + DN0 + y * DW + e * P, P),
                                 wide(KC), pp, 3 if y == 0 else RAW_SLOTS, N_DN)
                    for kh in range(2):
                        load(Q_DN + 6 + kh, l, kview(w_in[l], slice(kh * 512, (kh + 1) * 512),
                                                     pp * 256 + Z0, 256), wide(4), pp, RAW_SLOTS, N_DN)
                    for j in range(4):
                        load(Q_DN + 8 + j, l, kview(w_in[l], slice(0, D), pp * 256 + (GA0, GD0)[j % 2] + j // 2 * P, P),
                             wide(KC), pp, RAW_SLOTS, N_DN)

            def final(l):
                for j in range(4):
                    n0 = (GA0, GD0)[j % 2] + (6 + j // 2) * P
                    load(Q_FIN + j, l, kview(w_in[l], slice(0, D), slice(n0, n0 + P), P), wide(KC))

                def branch(dc):
                    q, cols_ = q_branch(dc), slice(dc * P, (dc + 1) * P)
                    load(q, l, kview(w_branch_att[l], slice(0, 2 * P), cols_, P),
                         lambda raw: raw.rearrange("p (k n) -> p k n", k=KC)[:, 0:2, :])
                    load(q, l, kview(w_branch_dn[l], slice(0, DW), cols_, P),
                         lambda raw: raw.rearrange("p (k n) -> p k n", k=KC)[:, 2:8, :], first=False)

                branch(0)
                for dc in range(KC):
                    if dc + 1 < KC:
                        branch(dc + 1)
                    load(q_rows(dc), l, w_out[l][dc * P:(dc + 1) * P, :])

            sp.dma_start(CT[:, :], table).then_inc(s["table_in"], 16)
            sp.dma_start(rowsb[0:48, :], norm_pre.rearrange("l s (k p) -> (l s k) p", p=P)).then_inc(s["rows_in"], 16)
            sp.dma_start(rowsb[48:56, :], c.rearrange("b (k p) -> (b k) p", p=P)).then_inc(s["rows_in"], 16)
            for l in range(DEPTH):
                sp.dma_start(cvrows[0:90, l, :], conv_w[l].rearrange("a (k p) -> (a k) p", p=P)).then_inc(s["rows_in"], 16)
            with nc.allow_non_contiguous_dma(reason="256 positions, once"):
                sp.dma_start(posi[:, :], positions.rearrange("b (t p) -> p (b t)", p=P)).then_inc(s["pos_in"], 16)
            sp.dma_start(X[:, :, :], x.rearrange("b (t p) d -> p (b t) d", p=P)).then_inc(s["x_in"], 16)
            with sp.Fori(0, DEPTH) as l:
                sp.wait_ge(s["layer_done"], l + 1)
                ffn(l, 0)
                attention(l)
                small_weights(l)
                delta(l)
                final(l)
                ffn(l, 1)
            sp.wait_ge(s["x_up"], DEPTH * SUBS * TT)
            sp.dma_start(out.rearrange("b (t p) d -> p (b t) d", p=P), X[:, :, :]).then_inc(s["stored"], 16)
            sp.wait_ge(s["stored"], 16)

        @block.gpsimd
        def _(pool):
            def mod_rows(a, l, sub):
                pool.wait_ge(s["acc_zero"], a + 1)
                pool.dma_start(acc[0:1, :], b_ada[bass.ds(l, 1), sub * 3 * D:(sub + 1) * 3 * D]
                               ).then_inc(s["bias_in"], 16)
                if not isinstance(a, int):
                    pool.wait_ge(s["mod_ok"], a)
                pool.dma_start(gpost[:, :], norm_post[bass.ds(l, 1), sub, :].to_broadcast([P, D])
                                ).then_inc(s["gpost_in"], 16)

            def ada(a, l, sub):
                pool.wait_ge(s["ada_step"], at(a, 2 * KC, 0))
                for k in range(2 * KC):
                    if k >= 2:
                        pool.wait_ge(s["ada_step"], at(a, 2 * KC, k - 1))
                    n0 = sub * 3 * D + (k % 2) * (3 * D // 2)
                    pool.dma_start(ADA[:, k % 2, :], w_ada[l, k // 2 * P:(k // 2 + 1) * P, n0:n0 + 3 * D // 2]
                                   ).then_inc(s[f"ada_land{k % 2}"], 16)
                    if k == 1:
                        mod_rows(a, l, sub)

            def pair(n):
                pool.wait_ge(s["cfp_ok"], at(n, 2, 2))
                for e in range(2):
                    g = cf[:, 1].rearrange("p t d e -> p d t e")[:, :, :, e:e + 1].to_broadcast([P, 2, TT, P])
                    nc.gpsimd.tensor_tensor(R[:, e], inc.rearrange("p d (o n) -> p d o n", o=1).to_broadcast([P, 2, TT, P]),
                                            g, ALU.mult).then_inc(s["R_ok"], 1)
                for e in range(2):
                    pool.wait_ge(s["ete_ok"], at(n, 2, e + 1))
                    for d in range(2):
                        nc.gpsimd.tensor_tensor(ET[:, e, d, :, :], ET[:, e, d, :, :],
                                                inc[:, d:d + 1, :].to_broadcast([P, TT, P]), ALU.mult
                                                ).then_inc(s["etm_ok"], 1)

            for j in range(2 * KC):
                k = j % (2 + FIRST_MORE)
                if j >= 2 + FIRST_MORE:
                    pool.wait_ge(s["ada_step"], j - (2 + FIRST_MORE) + 1)
                n0 = (j % 2) * (3 * D // 2)
                pool.dma_start(ADA[:, k, :] if k < 2 else first_blocks[:, k - 2, :],
                               w_ada[0, j // 2 * P:(j // 2 + 1) * P, n0:n0 + 3 * D // 2]
                               ).then_inc(s[f"ada_land{k}"], 16)
                if j == 1:
                    mod_rows(0, 0, 0)
            with pool.Fori(0, DEPTH) as l:
                ada(l * 3 + 1, l, 1)
                ada(l * 3 + 2, l, 2)
                with pool.Fori(0, PAIRS) as pp:
                    pair(l * PAIRS + pp)
                pool.wait_ge(s["m12_ok"], at(l, KC, KC))
                ada(l * 3 + 3, l * -1 + 1, 0)

        @block.tensor
        def _(pe):
            mm = nc.tensor.matmul
            tr = nc.tensor.transpose

            def triple(o, left, right, start, stop):
                mm(o, left[0], right[0], start=start, stop=False, skip_group_check=True)
                mm(o, left[0], right[1], start=False, stop=False, skip_group_check=True)
                return mm(o, left[1], right[0], start=False, stop=stop, skip_group_check=True)

            def halves(q, l, i=0, per=0, k=1):
                pe.wait_ge(s["lo_ok"], l * NQ + q + 1 + i * per)
                return [w[:, q % SPLIT_SLOTS, :].rearrange("p (k n) -> p k n", k=k) for w in (HI, LO)]

            def x_rows(kc, t=None):
                cols_ = slice(None) if t is None else slice(t * P, (t + 1) * P)
                return [h[:, kc, cols_] for h in (hTh, hTl)]

            def part(w, kc, a, b):
                return [h[:, kc, a:b] for h in w]

            def mod_columns(a):
                pe.wait_ge(s["ada_step"], at(a, 2 * KC, 2 * KC))
                for j in range(2 * KC):
                    last = mm(PS[:, 2, j:j + 1], acc[:, j * P:(j + 1) * P], ones[:, 0:1], start=True, stop=True)
                last.then_inc(s["modps"], 1)

            def mod_gate():
                for h in range(2):
                    last = mm(PS[:, 4 + h, :], ones[:, :], acc[:, 2 * D + h * 512:2 * D + (h + 1) * 512],
                              start=True, stop=True)
                last.then_inc(s["gateps"], 1)

            def norm(m):
                pe.wait_ge(s["modc_ok"], m + 1)
                for t in range(TT):
                    pe.wait_ge(s["xn_ok"], at(m, TT, t + 1))
                    for k in range(KC):
                        last = tr(PS[:, k // 2, (k % 2) * S + t * P:(k % 2) * S + (t + 1) * P],
                                  xn[:, t, k * P:(k + 1) * P], ident)
                    last.then_inc(s["xt_ok"], 1)

            def into_hidden(l, n, u, i=0):
                par, q0 = u % 2, Q_FFN[n[1]] + q_into(u)
                if u >= 2:
                    pe.wait_ge(s["tmp_ok"], at(n[0], UNITS, u - 1) + i * 2)
                for j in range(4):
                    half, kh = j // 2, j % 2
                    w = halves(q0 + j, l, i, 2 * STEP, 4)
                    if u == 0 and j < 2:
                        pe.wait_ge(s["hl_ok"], at(n[2], 2, kh + 1))
                    for c in range(2):
                        for k in range(4):
                            last = triple(PS[:, 2 * par + half, c * S:(c + 1) * S], part(w, k, c * P, (c + 1) * P),
                                          x_rows(4 * kh + k), j % 2 == 0 and c == 0 and k == 0, j % 2 == 1 and k == 3)
                    last.then_inc(s["used"], 1)

            def out_of_hidden(l, n, u, i=0, first=False, final=False):
                par, q0 = u % 2, Q_FFN[n[1]] + q_out(u)
                pe.wait_ge(s["ach_ok"], n[3] + u + 1 + i * 2)
                pe.wait_ge(s["acl_ok"], n[3] + u + 1 + i * 2)
                for c in range(2):
                    w = halves(q0 + c, l, i, 2 * STEP, 1)
                    for t in range(TT):
                        a = [h[:, par, c * S + t * P:c * S + (t + 1) * P] for h in (ACh, ACl)]
                        for h in range(2):
                            last = triple(PS[:, 4 + 2 * t + h, :], a, part(w, 0, h * 512, (h + 1) * 512),
                                          first and c == 0, final and c == 1)
                    last.then_inc(s["used"], 1)

            def ffn(l, f, m):
                n = (l * 2 + f, f, m, q_hidden(l, f))
                into_hidden(l, n, 0)
                into_hidden(l, n, 1)
                pe.wait_ge(s["mod_ok"], m + 1)
                out_of_hidden(l, n, 0, first=True)
                into_hidden(l, n, 2)
                out_of_hidden(l, n, 1)
                with pe.Fori(0, 4) as i:
                    for u in (3, 4):
                        into_hidden(l, n, u, i)
                        out_of_hidden(l, n, u - 1, i)
                mod_columns(m + 1)
                out_of_hidden(l, n, UNITS - 1, final=True)
                pe.wait_ge(s["ptmp_ok"], at(m, TT, 1))
                mod_gate()

            def attention(l):
                with pe.Fori(0, 2) as jj:
                    n = l * 2 + jj
                    pe.wait_ge(s["hl_ok"], at(l * 3 + 1, 2, 2))
                    for k in range(6):
                        g, kh = k // 2, k % 2
                        w = halves(Q_ATT + k, l, jj, N_ATT, 4)
                        for t in range(TT):
                            for kc in range(4):
                                last = triple(PS[:, 2 * t + g // 2, (g % 2) * 256:(g % 2) * 256 + 256],
                                              x_rows(4 * kh + kc, t), part(w, kc, 0, 256),
                                              kh == 0 and kc == 0, kh == 1 and kc == 3)
                        last.then_inc(s["used"], 1)
                    pe.wait_ge(s["mod_ok"], l * 3 + 2)
                    for g in range(NG):
                        w = halves(Q_ATT + 6 + g, l, jj, N_ATT, KC)
                        for t in range(TT):
                            for kc in range(KC):
                                last = triple(PS[:, 4 + t, g * P:(g + 1) * P], x_rows(kc, t), part(w, kc, 0, P),
                                              kc == 0, kc == KC - 1)
                        last.then_inc(s["used"], 1)
                    pe.wait_ge(s["rot_s"], at(n, 4, 4))
                    for w, b in ((0, 6), (1, 0)):
                        to = bank(b, 2)
                        for g in range(NG):
                            for t in range(TT):
                                last = tr(to[:, g * S + t * P:g * S + (t + 1) * P],
                                          rot[:, t, g * 256 + w * P:g * 256 + (w + 1) * P], ident)
                        last.then_inc(s["qt_ok"], 1)
                    pe.wait_ge(s["v_ok"], n + 1)
                    pe.wait_ge(s["qte"], n + 1)
                    pe.wait_ge(s["kte"], n + 1)

                    def scores(i):
                        hh, q = i // 2, i % 2
                        if i >= 2:
                            pe.wait_ge(s["sm_ok"], at(n, 4, i - 1))
                        for g in range(NG):
                            last = mm(PS[:, 2 + 2 * (i % 2) + g // 2, (g % 2) * S:(g % 2) * S + S],
                                      QT[hh * AE:(hh + 1) * AE, g, q * P:(q + 1) * P],
                                      KT[hh * AE:(hh + 1) * AE, g, :], start=True, stop=True)
                        last.then_inc(s["sc_ok"], 1)

                    def turn(i):
                        pe.wait_ge(s["p_ok"], at(n, 4, i + 1))
                        if i >= 1:
                            pe.wait_ge(s["pte_ok"], at(n, 4, i))
                        to = bank(6, 2)
                        for j in range(2 * NG):
                            last = tr(to[:, j * P:(j + 1) * P], sm[:, i % 2, j * P:(j + 1) * P], ident)
                        last.then_inc(s["pt_ok"], 1)

                    def values(i):
                        hh = i // 2
                        pe.wait_ge(s["pte_ok"], at(n, 4, i + 1))
                        if i >= 2:
                            pe.wait_ge(s["oa_ok"], at(n, 4, i - 1))
                        for j in range(2 * NG):
                            g, kt = j // 2, j % 2
                            last = mm(PS[:, i % 2, i * AE:(i + 1) * AE], prT[:, i % 2, j * P:(j + 1) * P],
                                      vat[:, kt, g * P + hh * AE:g * P + (hh + 1) * AE],
                                      start=(j == 0), stop=(j == 2 * NG - 1))
                        last.then_inc(s["pv_ok"], 1)

                    scores(0)
                    scores(1)
                    turn(0)
                    scores(2)
                    values(0)
                    turn(1)
                    scores(3)
                    values(1)
                    turn(2)
                    values(2)
                    turn(3)
                    values(3)
                    pe.wait_ge(s["oa_ok"], at(n, 4, 4))
                for q in range(2):
                    for c in range(2):
                        last = tr(PS[:, 1, c * S + q * P:c * S + (q + 1) * P], oatt[:, q, c * P:(c + 1) * P], ident)
                last.then_inc(s["oat_ok"], 1)

            def two_chunks(q, b, l, i=0, per=0):
                for j in range(2):
                    w = halves(q + j, l, i, per, KC)
                    for k in range(KC):
                        last = triple(PS[:, b, j * S:(j + 1) * S], part(w, k, 0, P), x_rows(k), k == 0, k == KC - 1)
                    last.then_inc(s["used"], 1)

            def coefficients(l):
                w = [h[:, Q_BA % SPLIT_SLOTS, 0:KC * 24].rearrange("p (k n) -> p k n", k=KC) for h in (HI, LO)]
                pe.wait_ge(s["lo_ok"], l * NQ + Q_BA + 1)
                for t in range(TT):
                    for kc in range(KC):
                        last = triple(PS[:, 7, t * 24:(t + 1) * 24], x_rows(kc, t), part(w, kc, 0, 24),
                                      kc == 0, kc == KC - 1)
                last.then_inc(s["used"], 1)
                two_chunks(Q_DN, 0, l)
                pe.wait_ge(s["oh_ok"], at(l, 1 + PAIRS, 1))
                pe.wait_ge(s["cf_dve"], at(l, 5, 5))
                for w, m in ((0, inc), (1, after)):
                    for d in range(2):
                        last = mm(PS[:, 6, (w * 2 + d) * 12:(w * 2 + d + 1) * 12].rearrange("p (t h) -> p t h", t=2),
                                  m[:, d, :], coef[:, 1, :, d, :], start=True, stop=True)
                last.then_inc(s["cumsum_ok"], 1)

            def pair(l, pp):
                n = l * PAIRS + pp
                pe.wait_ge(s["cf_act"], at(l, 7, 7))
                for y in (1, 2):
                    two_chunks(Q_DN + 2 * y, y, l, pp, N_DN)
                for kh in range(2):
                    w = halves(Q_DN + 6 + kh, l, pp, N_DN, 4)
                    for t in range(TT):
                        for k in range(4):
                            last = triple(PS[:, 3, t * S:(t + 1) * S], x_rows(4 * kh + k, t), part(w, k, 0, 256),
                                          kh == 0 and t == 0 and k == 0, kh == 1 and k == 3)
                    last.then_inc(s["used"], 1)

                pe.wait_ge(s["oh_ok"], at(l, 1 + PAIRS, 1 + pp))
                pe.wait_ge(s["sq_ok"], n + 1)
                for h in range(2):
                    last = mm(PS[:, 4 + h, :], ones[:, :], sq[:, h * 512:(h + 1) * 512], start=True, stop=True)
                last.then_inc(s["ss_ok"], 1)
                pe.wait_ge(s["cb_ok"], at(n, 3, 3))
                for e in range(2):
                    pe.wait_ge(s["R_ok"], at(n, 2, e + 1))
                    for d in range(2):
                        last = mm(PS[:, e, d * 256:(d + 1) * 256], after[:, d, :], R[:, e, d, :, :],
                                  start=True, stop=True)
                    last.then_inc(s["et_ok"], 1)
                two_chunks(Q_DN + 8, 2, l, pp, N_DN)
                pe.wait_ge(s["kqn_ok"], at(n, 4, 4))
                for e in range(2):
                    for t in range(TT):
                        tr(PS[:, 6, (2 * e + t) * P:(2 * e + t + 1) * P], kqn[:, e, t, 0, :], ident)
                for e in range(2):
                    for t in range(TT):
                        last = tr(PS[:, 7, (2 * e + t) * P:(2 * e + t + 1) * P],
                                  qs[:, 4 + e, t * P:(t + 1) * P], ident)
                last.then_inc(s["tk_ok"], 1)
                for e in range(2):
                    for t in range(TT):
                        last = mm(PS[:, 4 + e, t * 256:(t + 1) * 256], kqn[:, e, t, 0, :], kqn[:, e, t, :, :],
                                  start=True, stop=True)
                    last.then_inc(s["kk_ok"], 1)
                four = [(d, t) for d in range(2) for t in range(TT)]

                pe.wait_ge(s["gs_ok"], at(n, 2, 1))

                def at4(b, e, d, t):
                    return PS[:, b + e, (2 * d + t) * P:(2 * d + t + 1) * P]

                pe.wait_ge(s["z_ok"], n + 1)
                for e in range(2):
                    pe.wait_ge(s["nb_ok"], at(n, 8, 4 * e + 4))
                    for d, t in four:
                        last = tr(at4(2, e, d, t), NB[:, e, d, t, :], ident)
                    last.then_inc(s["nbT_ok"], 1)
                pe.wait_ge(s["ete_ok"], at(n, 2, 1))
                two_chunks(Q_DN + 10, 0, l, pp, N_DN)

                def level_up(v, last_level):
                    pe.wait_ge(s["ktok_ok"], n + 1)
                    pe.wait_ge(s["vtok_ok"], n + 1)
                    pe.wait_ge(s["at_ok"], at(n, 4, 4))
                    pe.wait_ge(s["d1_s"], at(n, 6, 6))
                    for e in range(2):
                        pe.wait_ge(s["l_D"], n * 2 * (LEVELS - 1) + 2 * v + e + 1)
                        for d, t in four:
                            last = mm(at4(2, e, d, t), NB[:, e, d, t, :], Dm[:, e, d, t, :], start=True, stop=True)
                        last.then_inc(s["l_a"], 1)
                    for e in range(2):
                        pe.wait_ge(s["l_A"], n * 2 * (LEVELS - 1) + 2 * v + e + 1)
                        for d, t in four:
                            last = mm(at4(4, e, d, t), A[:, e, d, t, :], DT[:, e, d, t, :], start=True, stop=True)
                        last.then_inc(s["l_b"], 1)
                    if last_level:
                        return
                    for e in range(2):
                        pe.wait_ge(s["l_DT"], n * 2 * (LEVELS - 1) + 2 * v + e + 1)
                        for d, t in four:
                            last = tr(at4(6, e, d, t), DT[:, e, d, t, :], ident)
                        last.then_inc(s["l_c"], 1)

                with pe.Fori(0, LEVELS - 2) as v:
                    level_up(v, False)
                level_up(LEVELS - 2, True)
                pe.wait_ge(s["l_DT"], at(n, 2 * (LEVELS - 1), 2 * (LEVELS - 1)))
                pe.wait_ge(s["kg_ok"], at(n, 4, 4))
                both = [(e, d) for e in range(2) for d in range(2)]

                def one(b, e, d):
                    return PS[:, b, (2 * e + d) * P:(2 * e + d + 1) * P]

                for e, d in both:
                    last = mm(one(3, e, d), DT[:, e, d, FIRST[d], :], vtok[:, e, FIRST[d], :], start=True, stop=True)
                last.then_inc(s["wu_ok"], 1)
                for e, d in both:
                    last = mm(one(2, e, d), kg[:, 2 * e + d, :], DT[:, e, d, SECOND[d], :],
                              start=True, stop=True)
                last.then_inc(s["wu_ok"], 1)
                pe.wait_ge(s["vn1_ok"], at(n, 4, 4))
                pe.wait_ge(s["kd_ok"], at(n, 4, 4))
                for e, d in both:
                    last = mm(one(4, e, d), kd[:, e, d, :], vn[:, e, d, FIRST[d], :], start=True, stop=True)
                last.then_inc(s["s_ok"], 1)
                pe.wait_ge(s["St_ok"], n + 1)
                pe.wait_ge(s["wT_ok"], n + 1)
                for e, d in both:
                    mm(one(5, e, d), DT[:, e, d, SECOND[d], :], vtok[:, e, SECOND[d], :], start=True, stop=False)
                    last = mm(one(5, e, d), wT[:, 2 * e + d, :], St[:, 2 * e + d, :], start=False, stop=True)
                last.then_inc(s["v2_ok"], 1)
                for e, d in both:
                    t = SECOND[d]
                    last = mm(PS[:, 6, (2 * e + t) * P:(2 * e + t + 1) * P], kqn[:, e, t, 1, :], St[:, 2 * e + d, :],
                              start=True, stop=True)
                last.then_inc(s["qS_ok"], 1)
                pe.wait_ge(s["vn2_ok"], at(n, 4, 4))
                for e in range(2):
                    for t in range(TT):
                        for d in range(2):
                            last = mm(PS[:, 7, (2 * e + t) * P:(2 * e + t + 1) * P], AT[:, e, d, t, :],
                                      vn[:, e, d, t, :], start=(d == 0), stop=(d == 1))
                last.then_inc(s["o_ok"], 1)
                pe.wait_ge(s["gs_ok"], at(n, 2, 2))
                two_chunks(Q_DN + N_DN, 0, l, pp, N_DN)
                pe.wait_ge(s["og_ok"], n + 1)
                for j in range(4):
                    last = tr(PS[:, 4, j * P:(j + 1) * P], og[:, j, :], ident)
                last.then_inc(s["ogT_ok"], 1)

            def final(l, m):
                two_chunks(Q_FIN + 2, 3, l)
                pe.wait_ge(s["gt_ok"], at(l, 2, 1))
                pe.wait_ge(s["ol_ok"], at(l, 1 + PAIRS, 1 + PAIRS))
                pe.wait_ge(s["gs_ok"], at(l, 2 * PAIRS, 2 * PAIRS))

                def branch(dc):
                    w = halves(q_branch(dc), l, k=KC)
                    if dc >= 2:
                        pe.wait_ge(s["m12_ok"], at(l, KC, dc - 1))
                    for k in range(2 + DH):
                        o = PS[:, dc % 2, 0:S] if k < 2 else PS[:, dc % 2, S:2 * S]
                        last = triple(o, part(w, k, 0, P), [h[:, k, :] for h in (oTh, oTl)],
                                      k in (0, 2), k in (1, 1 + DH))
                    last.then_inc(s["used"], 1)

                def rows(dc):
                    w = halves(q_rows(dc), l)
                    pe.wait_ge(s["ach_ok"], q_hidden(l, 0) + UNITS + dc + 1)
                    pe.wait_ge(s["acl_ok"], q_hidden(l, 0) + UNITS + dc + 1)
                    for t in range(TT):
                        a = [h[:, dc % 2, t * P:(t + 1) * P] for h in (ACh, ACl)]
                        for h in range(2):
                            last = triple(PS[:, 4 + 2 * t + h, :], a, part(w, 0, h * 512, (h + 1) * 512),
                                          dc == 0, dc == KC - 1)
                    last.then_inc(s["used"], 1)

                branch(0)
                for dc in range(KC):
                    if dc + 1 < KC:
                        branch(dc + 1)
                    else:
                        mod_columns(m + 1)
                    rows(dc)
                pe.wait_ge(s["ptmp_ok"], at(m, TT, 1))
                mod_gate()

            pe.wait_ge(s["setup_dve"], 1)
            pe.wait_ge(s["rows_in"], 64)
            pe.wait_ge(s["table_in"], 16)
            tr(PS[:, 7, 0:56], rowsb[0:56, :], ident[0:56, 0:56])
            for l in range(DEPTH):
                last = tr(PS[:, 7, 128 * (l + 1):128 * (l + 1) + 90], cvrows[0:90, l, :], ident[0:90, 0:90])
            last.then_inc(s["setup_pe"], 1)
            mod_columns(0)
            mod_gate()
            with pe.Fori(0, DEPTH) as l:
                norm(l * 3)
                ffn(l, 0, l * 3)
                norm(l * 3 + 1)
                attention(l)
                coefficients(l)
                with pe.Fori(0, PAIRS) as pp:
                    pair(l, pp)
                final(l, l * 3 + 1)
                norm(l * 3 + 2)
                ffn(l, 1, l * 3 + 2)

        @block.scalar
        def _(act_):
            fn = nc.scalar.activation

            def roots(src, m, done_sq, done_rms, source=None, k=0):
                for t in range(TT):
                    if source is not None:
                        act_.wait_ge(s[source], k + t + 1)
                    fn(junk[:, t, :], src(t), ACT.Square, accum_out=ssq[:, t:t + 1]).then_inc(s[done_sq], 1)
                act_.wait_ge(s[done_sq], at(m, TT, TT))
                fn(rms[:, :], ssq[:, :], ACT.Sqrt, bias=eps[:, 0:1], scale=1.0 / D).then_inc(s[done_rms], 1)

            def high(q, l, i=0, per=0):
                act_.wait_ge(s[f"land{SLOT[q]}"], landed(q, l, i, per))
                if q >= SPLIT_SLOTS:
                    act_.wait_ge(s["used"], l * NQ + q - SPLIT_SLOTS + 1 + i * per)
                fn(HI[:, q % SPLIT_SLOTS, :], RAW[:, SLOT[q], :], ACT.Copy).then_inc(s["hi_ok"], 1)

            def norm(m, l, q):
                for k in range(SPLIT_SLOTS):
                    high(q + k, l)
                act_.wait_ge(s["xt_ok"], at(m, TT, TT))
                for kh in range(2):
                    for k in (4 * kh + 2, 4 * kh + 3):
                        fn(hsum[:, k, :], PS[:, k // 2, (k % 2) * S:(k % 2) * S + S], ACT.Identity,
                           bias=modB[:, k:k + 1], scale=modA[:, k:k + 1]).then_inc(s["hsa_ok"], 1)
                    act_.wait_ge(s["hsa_ok"], at(m, 4, 2 * kh + 2))
                    act_.wait_ge(s["hs_ok"], at(m, 4, 2 * kh + 2))
                    fn(hTh[:, 4 * kh:4 * kh + 4, :], hsum[:, 4 * kh:4 * kh + 4, :], ACT.Copy).then_inc(s["hh_ok"], 1)
                act_.wait_ge(s["mod_ok"], m + 1)
                fn(acc.rearrange("p (j n) -> p j n", n=P),
                   ones.rearrange("p (o n) -> p o n", o=1).to_broadcast([P, 3 * KC, P]), ACT.Copy, scale=0.0
                   ).then_inc(s["acc_zero"], 1)

            def silu_unit(l, n, u, i=0):
                par = u % 2
                act_.wait_ge(s["used"], l * NQ + Q_FFN[n[1]] + q_into(u) + 4 + i * 2 * STEP)
                if u >= 2:
                    act_.wait_ge(s["tmp_ok"], at(n[0], UNITS, u - 1) + i * 2)
                fn(sg[:, par, :], PS[:, 2 * par, :], ACT.Silu).then_inc(s["sg_ok"], 1)

            def high_hidden(l, n, u, i=0):
                par = u % 2
                act_.wait_ge(s["tmp_ok"], at(n[0], UNITS, u + 1) + i * 2)
                if u >= 2:
                    act_.wait_ge(s["used"], l * NQ + Q_FFN[n[1]] + q_out(u - 2) + 2 + i * 2 * STEP)
                fn(ACh[:, par, :], act[:, par, :], ACT.Copy).then_inc(s["ach_ok"], 1)

            def ffn(l, f, m):
                n, q0 = (l * 2 + f, f), Q_FFN[f]

                def step(u, i=0):
                    q = q0 + q_into(u)
                    high(q, l, i, 2 * STEP)
                    high(q + 1, l, i, 2 * STEP)
                    silu_unit(l, n, u - 1, i)
                    high(q + 2, l, i, 2 * STEP)
                    high(q + 3, l, i, 2 * STEP)
                    high_hidden(l, n, u - 1, i)
                    high(q + 4, l, i, 2 * STEP)
                    high(q + 5, l, i, 2 * STEP)

                high(q0 + 3, l)
                step(1)
                step(2)
                with act_.Fori(0, 4) as i:
                    step(3, i)
                    step(4, i)
                silu_unit(l, n, UNITS - 1)
                high(q0 + N_FFN - 2, l)
                high_hidden(l, n, UNITS - 1)
                high(q0 + N_FFN - 1, l)
                fn(spare[:, :], eps[:, :], ACT.Sqrt)
                act_.wait_ge(s["used"], l * NQ + q0 + N_FFN)
                roots(lambda t: bank(4 + 2 * t, 2), m, "pssq_ok", "prms_ok")
                roots(lambda t: X[:, t, :], m + 1, "ssq_ok", "rms_ok", "x_up", at(m, TT, 0))

            def attention(l):
                with act_.Fori(0, 2) as jj:
                    n = l * 2 + jj
                    for k in range(SPLIT_SLOTS, N_ATT):
                        high(Q_ATT + k, l, jj, N_ATT)
                    act_.wait_ge(s["used"], l * NQ + Q_ATT + N_ATT + jj * N_ATT)
                    fn(vat[:, :, :], PS[:, 4:6, 0:NG * P], ACT.Copy).then_inc(s["v_ok"], 1)
                    act_.wait_ge(s["qt_ok"], at(n, 2, 1))
                    fn(QT.rearrange("p g s -> p (g s)"), bank(6, 2)[:, 0:NG * S], ACT.Copy).then_inc(s["qte"], 1)
                    for k in range(SPLIT_SLOTS):
                        high(Q_ATT + N_ATT + k, l, jj, N_ATT)

                    def soft(i):
                        act_.wait_ge(s["nm_ok"], at(n, 4, i + 1))
                        fn(sm[:, i % 2, :], sm[:, i % 2, :], ACT.Exp, bias=nmx[:, i:i + 1],
                           accum_out=den[:, i:i + 1]).then_inc(s["p_ok"], 1)

                    def turned(i):
                        act_.wait_ge(s["pt_ok"], at(n, 4, i + 1))
                        if i >= 2:
                            act_.wait_ge(s["pv_ok"], at(n, 4, i - 1))
                        fn(prT[:, i % 2, :], bank(6, 2)[:, 0:768], ACT.Copy).then_inc(s["pte_ok"], 1)

                    soft(0)
                    for i in range(1, 4):
                        soft(i)
                        turned(i - 1)
                    turned(3)
                act_.wait_ge(s["oat_ok"], l + 1)
                fn(oTh[:, 0:2, :], PS[:, 1, :].rearrange("p (c s) -> p c s", c=2), ACT.Copy)
                fn(oatT, PS[:, 1, :].rearrange("p (c s) -> p c s", c=2), ACT.Copy).then_inc(s["oh_ok"], 1)

            def coefficients(l):
                act_.wait_ge(s["used"], l * NQ + Q_BA + 1)
                ba = PS[:, 7, 0:48].rearrange("p (t n) -> p t n", t=2)
                fn(raw[:, :, 0:12], ba[:, :, 0:12], ACT.Exp, scale=-1.0).then_inc(s["cf_act"], 1)
                fn(ea, alogb, ACT.Exp).then_inc(s["cf_act"], 1)
                act_.wait_ge(s["cf_dve"], at(l, 5, 3))
                fn(ta, al, ACT.Abs).then_inc(s["cf_act"], 1)
                act_.wait_ge(s["cf_act"], at(l, 7, 3))
                fn(ta, ta, ACT.Exp, scale=-1.0).then_inc(s["cf_act"], 1)
                act_.wait_ge(s["cf_act"], at(l, 7, 4))
                fn(ta, ta, ACT.Ln, bias=ones[:, 0:1]).then_inc(s["cf_act"], 1)
                high(Q_DN + 2, l)
                high(Q_DN + 3, l)
                act_.wait_ge(s["cumsum_ok"], l + 1)
                for w in range(2):
                    fn(coef[:, 2 + w].rearrange("p t d h -> p d t h"),
                       PS[:, 6, w * 24:(w + 1) * 24].rearrange("p (d t h) -> p d t h", d=2, t=2),
                       ACT.Exp).then_inc(s["cf_act"], 1)

            def pair(l, pp):
                n = l * PAIRS + pp
                for ahead, y in ((4, 0), (5, None), (6, 1), (7, None), (8, 2)):
                    high(Q_DN + ahead, l, pp, N_DN)
                    if y is not None:
                        act_.wait_ge(s["used"], l * NQ + Q_DN + 2 * y + 2 + pp * N_DN)
                        fn(cb[:, 2 * y:2 * y + 2, 2:2 + S], PS[:, y, :].rearrange("p (e s) -> p e s", e=2),
                           ACT.Copy).then_inc(s["cb_ok"], 1)
                def silu_of(y):
                    act_.wait_ge(s["cv_s"], at(n, 30, 10 * (y + 1)))
                    fn(qs[:, 2 * y:2 * y + 2, :], qs[:, 2 * y:2 * y + 2, :], ACT.Silu).then_inc(s["si_ok"], 1)

                silu_of(0)
                silu_of(1)
                act_.wait_ge(s["si_ok"], at(n, 3, 2))
                fn(sq, qs[:, 0:4, :].rearrange("p i s -> p (i s)"), ACT.Square).then_inc(s["sq_ok"], 1)
                high(Q_DN + 9, l, pp, N_DN)
                high(Q_DN + 10, l, pp, N_DN)
                act_.wait_ge(s["used"], l * NQ + Q_DN + 8 + pp * N_DN)
                fn(zs.rearrange("p t n -> p (t n)"), PS[:, 3, :], ACT.Silu).then_inc(s["z_ok"], 1)
                silu_of(2)
                act_.wait_ge(s["ss_ok"], n + 1)
                fn(rs, bank(4, 2), ACT.Ln, bias=eps[:, 0:1]).then_inc(s["rs_ok"], 1)
                act_.wait_ge(s["rs_ok"], at(n, 2, 1))
                fn(rs, rs, ACT.Exp, scale=-0.5).then_inc(s["rs_ok"], 1)
                for e in range(2):
                    act_.wait_ge(s["et_ok"], at(n, 2, e + 1))
                    fn(ET[:, e].rearrange("p d t n -> p (d t n)"), PS[:, e, :], ACT.Exp).then_inc(s["ete_ok"], 1)
                high(Q_DN + 11, l, pp, N_DN)
                act_.wait_ge(s["used"], l * NQ + Q_DN + 10 + pp * N_DN)
                fn(GS[:, bass.ds(pp * 2, 1), :], PS[:, 2:3, :], ACT.Sigmoid).then_inc(s["gs_ok"], 1)
                act_.wait_ge(s["tk_ok"], n + 1)
                fn(ktok.rearrange("p e t n -> p (e t n)"), PS[:, 6, :], ACT.Copy).then_inc(s["ktok_ok"], 1)
                act_.wait_ge(s["used"], l * NQ + Q_DN + 12 + pp * N_DN)
                fn(GS[:, bass.ds(pp * 2 + 1, 1), :], PS[:, 0:1, :], ACT.Sigmoid).then_inc(s["gs_ok"], 1)
                for k in range(3):
                    high(Q_DN + N_DN + k, l, pp, N_DN)
                with act_.Fori(0, LEVELS - 2) as v:
                    for e in range(2):
                        act_.wait_ge(s["l_c"], n * 2 * (LEVELS - 2) + 2 * v + e + 1)
                        fn(Dm[:, e].rearrange("p d t n -> p (d t n)"), PS[:, 6 + e, :], ACT.Copy).then_inc(s["l_D"], 1)
                act_.wait_ge(s["wu_ok"], at(n, 2, 2))
                fn(wT.rearrange("p j n -> p (j n)"), PS[:, 2, :], ACT.Copy).then_inc(s["wT_ok"], 1)
                act_.wait_ge(s["s_ok"], n + 1)
                fn(St.rearrange("p j n -> p (j n)"), PS[:, 4, :], ACT.Copy).then_inc(s["St_ok"], 1)
                act_.wait_ge(s["qS_ok"], n + 1)
                for e in range(2):
                    for t in range(TT):
                        d = SECOND.index(t)
                        last = fn(qS[:, 2 * e + t, :], PS[:, 6, (2 * e + t) * P:(2 * e + t + 1) * P], ACT.Copy,
                                  scale=cf[:, 2, t, d, e:e + 1])
                last.then_inc(s["qSs_ok"], 1)
                act_.wait_ge(s["ob_ok"], n + 1)
                for j in range(4):
                    last = fn(qS[:, j, :], ob[:, j, :], ACT.Square, accum_out=oss[:, j:j + 1])
                last.then_inc(s["oss_ok"], 1)
                act_.wait_ge(s["oss_ok"], n + 1)
                fn(orms, oss, ACT.Sqrt, bias=eps[:, 0:1], scale=1.0 / DE).then_inc(s["orms_ok"], 1)
                high(Q_DN + N_DN + 3, l, pp, N_DN)
                act_.wait_ge(s["ogT_ok"], n + 1)
                fn(oTh[:, bass.ds(pp * 2 + 2, 2), :], PS[:, 4, :].rearrange("p (e s) -> p e s", e=2), ACT.Copy)
                fn(odT, PS[:, 4, :].rearrange("p (e s) -> p e s", e=2), ACT.Copy).then_inc(s["oh_ok"], 1)

            def final(l, m):
                high(Q_FIN + 4, l)
                act_.wait_ge(s["used"], l * NQ + Q_FIN + 2)
                fn(GS2[:, 0, :], PS[:, 0, :], ACT.Sigmoid).then_inc(s["gt_ok"], 1)
                high(Q_FIN + 5, l)
                act_.wait_ge(s["used"], l * NQ + Q_FIN + 4)
                fn(GS2[:, 1, :], PS[:, 3, :], ACT.Sigmoid).then_inc(s["gt_ok"], 1)
                high(Q_FIN + 6, l)
                for dc in range(KC):
                    act_.wait_ge(s["y_ok"], at(l, KC, dc + 1))
                    if dc >= 2:
                        act_.wait_ge(s["used"], l * NQ + q_rows(dc - 2) + 1)
                    fn(ACh[:, dc % 2, 0:S], yT[:, dc % 2, :], ACT.Copy).then_inc(s["ach_ok"], 1)
                    for q in (Q_FIN + 7 + 2 * dc, Q_FIN + 8 + 2 * dc):
                        if q < Q_FFN[1]:
                            high(q, l)
                fn(spare[:, :], eps[:, :], ACT.Sqrt)
                act_.wait_ge(s["used"], l * NQ + Q_FFN[1])
                roots(lambda t: bank(4 + 2 * t, 2), m, "pssq_ok", "prms_ok")
                roots(lambda t: X[:, t, :], m + 1, "ssq_ok", "rms_ok", "x_up", at(m, TT, 0))

            act_.wait_ge(s["sd"], SD_ANGLE)
            fn(cs[:, :, :, :].rearrange("p w t f -> p (w t f)"), angle, ACT.Sin).then_inc(s["sa"], 1)
            act_.wait_ge(s["sd"], SD_COLS)
            fn(ccol[:, :], cols[:, 48:56], ACT.Silu).then_inc(s["sa"], 1)
            act_.wait_ge(s["x_in"], 16)
            roots(lambda t: X[:, t, :], 0, "ssq_ok", "rms_ok")
            with act_.Fori(0, DEPTH) as l:
                norm(l * 3, l, Q_FFN[0])
                ffn(l, 0, l * 3)
                norm(l * 3 + 1, l, Q_ATT)
                attention(l)
                coefficients(l)
                with act_.Fori(0, PAIRS) as pp:
                    pair(l, pp)
                final(l, l * 3 + 1)
                norm(l * 3 + 2, l, Q_FFN[1])
                ffn(l, 1, l * 3 + 2)

        @block.vector
        def _(dve):
            v = nc.vector

            def ada_block(a, kc, half):
                if isinstance(a, int):
                    j = 2 * kc + half
                    k = j % (2 + FIRST_MORE)
                    dve.wait_ge(s[f"ada_land{k}"], 16 * (j // (2 + FIRST_MORE) + 1))
                    block_ = ADA[:, k, :] if k < 2 else first_blocks[:, k - 2, :]
                else:
                    dve.wait_ge(s[f"ada_land{half}"], ((a - 1) * KC + 2 + kc + 1) * 16)
                    block_ = ADA[:, half, :]
                if not (isinstance(kc, int) and kc == 0 and half == 0):
                    dve.wait_ge(s["ada_step"], a * 2 * KC + kc * 2 + half)
                cols_ = slice(half * (3 * D // 2), (half + 1) * (3 * D // 2))
                v.scalar_tensor_tensor(acc[:, cols_], block_,
                                       ccol[:, kc:kc + 1] if isinstance(kc, int) else ccol[:, bass.ds(kc, 1)],
                                       acc[:, cols_], ALU.mult, ALU.add).then_inc(s["ada_step"], 1)

            def mod_columns(a, l, sub, end_of_layer=False):
                dve.wait_ge(s["modps"], a + 1)
                shifts = v.tensor_copy(modB[:, :], PS[:, 2, 0:KC])
                if end_of_layer:
                    shifts.then_inc(s["layer_done"], 1)
                v.scalar_tensor_tensor(modA[:, :], PS[:, 2, KC:2 * KC], 1.0, cols[:, bass.ds(l * 24 + sub * KC, KC)],
                                       ALU.add, ALU.mult).then_inc(s["modc_ok"], 1)

            def mod_gate(a, sub):
                dve.wait_ge(s["gateps"], a + 1)
                dve.wait_ge(s["gpost_in"], (a + 1) * 16)
                v.scalar_tensor_tensor(gateb[:, :], bank(4, 2), 1.0 if sub == 1 else 0.5, gpost[:, :],
                                       ALU.mult, ALU.mult).then_inc(s["mod_ok"], 1)

            def low(q, l, i=0, per=0):
                dve.wait_ge(s["hi_ok"], l * NQ + q + 1 + i * per)
                slot = q % SPLIT_SLOTS
                v.tensor_tensor(LO[:, slot, :], RAW[:, SLOT[q], :], HI[:, slot, :].bitcast(F32), ALU.subtract
                                ).then_inc(s["lo_ok"], 1)

            def norm(m, l, q, sub):
                dve.wait_ge(s["rms_ok"], m + 1)
                v.reciprocal(rr[:, :], rms[:, :]).then_inc(s["rr_ok"], 1)
                dve.wait_ge(s["rr_ok"], m + 1)
                for t in range(TT):
                    v.tensor_scalar(xn[:, t, :], X[:, t, :], rr[:, t:t + 1], None, ALU.mult).then_inc(s["xn_ok"], 1)
                mod_gate(m, sub)
                low(q, l)
                dve.wait_ge(s["xt_ok"], at(m, TT, TT))
                dve.wait_ge(s["modc_ok"], m + 1)
                for k in (0, 1, 4, 5):
                    v.tensor_scalar(hsum[:, k, :], PS[:, k // 2, (k % 2) * S:(k % 2) * S + S], modA[:, k:k + 1],
                                    modB[:, k:k + 1], ALU.mult, ALU.add).then_inc(s["hs_ok"], 1)
                dve.wait_ge(s["hs_ok"], at(m, 4, 4))
                for kh in range(2):
                    dve.wait_ge(s["hh_ok"], at(m, 2, kh + 1))
                    rows_ = slice(4 * kh, 4 * kh + 4)
                    v.tensor_tensor(hTl[:, rows_, :], hsum[:, rows_, :], hTh[:, rows_, :].bitcast(F32), ALU.subtract
                                    ).then_inc(s["hl_ok"], 1)

            def post(m):
                dve.wait_ge(s["prms_ok"], m + 1)
                v.reciprocal(rr[:, :], rms[:, :]).then_inc(s["prr_ok"], 1)
                dve.wait_ge(s["prr_ok"], m + 1)
                for t in range(TT):
                    v.scalar_tensor_tensor(xn[:, t, :], bank(4 + 2 * t, 2), rr[:, t:t + 1], gateb[:, :],
                                           ALU.mult, ALU.mult).then_inc(s["ptmp_ok"], 1)
                for t in range(TT):
                    dve.wait_ge(s["ptmp_ok"], at(m, TT, t + 1))
                    v.tensor_tensor(X[:, t, :], X[:, t, :], xn[:, t, :], ALU.add).then_inc(s["x_up"], 1)

            def hidden(l, n, u, i=0):
                par = u % 2
                dve.wait_ge(s["sg_ok"], at(n[0], UNITS, u + 1) + i * 2)
                if u >= 2:
                    dve.wait_ge(s["ach_ok"], n[2] + u - 1 + i * 2)
                    dve.wait_ge(s["acl_ok"], n[2] + u - 1 + i * 2)
                v.tensor_tensor(act[:, par, :], sg[:, par, :], PS[:, 2 * par + 1, :], ALU.mult
                                ).then_inc(s["tmp_ok"], 1)

            def low_hidden(n, u, i=0):
                par = u % 2
                dve.wait_ge(s["ach_ok"], n[2] + u + 1 + i * 2)
                dve.wait_ge(s["tmp_ok"], at(n[0], UNITS, u + 1) + i * 2)
                v.tensor_tensor(ACl[:, par, :], act[:, par, :], ACh[:, par, :].bitcast(F32), ALU.subtract
                                ).then_inc(s["acl_ok"], 1)

            def ffn(l, f, a):
                n, q0 = (l * 2 + f, f, q_hidden(l, f)), Q_FFN[f]

                def step(u, i=0):
                    q = q0 + q_into(u)
                    low(q, l, i, 2 * STEP)
                    low(q + 1, l, i, 2 * STEP)
                    hidden(l, n, u - 1, i)
                    low(q + 2, l, i, 2 * STEP)
                    low(q + 3, l, i, 2 * STEP)
                    low_hidden(n, u - 1, i)
                    low(q + 4, l, i, 2 * STEP)
                    low(q + 5, l, i, 2 * STEP)

                for k in range(1, 4):
                    low(q0 + k, l)
                step(1)
                step(2)
                with dve.Fori(0, 4) as i:
                    for j in range(2):
                        step(3 + j, i)
                        dve.wait_ge(s["bias_in"], (a + 1) * 16)
                        for half in range(2):
                            ada_block(a, i * 2 + j, half)
                hidden(l, n, UNITS - 1)
                low(q0 + N_FFN - 2, l)
                low_hidden(n, UNITS - 1)
                low(q0 + N_FFN - 1, l)

            def attention(l, a):
                low(Q_ATT + 1, l)
                low(Q_ATT + 2, l)
                with dve.Fori(0, 2) as jj:
                    n = l * 2 + jj

                    def ada(k):
                        ada_block(a, jj * (KC // 2) + k // 2, k % 2)

                    dve.wait_ge(s["bias_in"], (a + 1) * 16)
                    for k in range(SPLIT_SLOTS, N_ATT):
                        low(Q_ATT + k, l, jj, N_ATT)
                        if k % 3 < 2:
                            ada(k // 3 * 2 - 2 + k % 3)
                    dve.wait_ge(s["used"], l * NQ + Q_ATT + 6 + jj * N_ATT)
                    for t in range(TT):
                        src = bank(2 * t, 2)[:, 0:768].rearrange("p (h w f) -> p h w f", w=2, f=AE // 2)
                        dst = rot[:, t, :].rearrange("p (h w f) -> p h w f", w=2, f=AE // 2)
                        tmp = [rtmp2[t][:, i, :].rearrange("p (h f) -> p h f", f=AE // 2) for i in range(4)]
                        cos = cs[:, 0, t:t + 1, :].to_broadcast([P, 12, AE // 2])
                        sin = cs[:, 1, t:t + 1, :].to_broadcast([P, 12, AE // 2])
                        v.tensor_tensor(tmp[0], src[:, :, 0, :], cos, ALU.mult)
                        v.tensor_tensor(tmp[1], src[:, :, 1, :], sin, ALU.mult)
                        v.tensor_tensor(tmp[2], src[:, :, 1, :], cos, ALU.mult)
                        v.tensor_tensor(tmp[3], src[:, :, 0, :], sin, ALU.mult).then_inc(s["rot_s"], 1)
                        dve.wait_ge(s["rot_s"], at(n, 4, 2 * t + 1))
                        v.tensor_tensor(dst[:, :, 0, :], tmp[0], tmp[1], ALU.subtract)
                        v.tensor_tensor(dst[:, :, 1, :], tmp[2], tmp[3], ALU.add).then_inc(s["rot_s"], 1)
                    dve.wait_ge(s["qt_ok"], at(n, 2, 2))
                    v.tensor_copy(KT.rearrange("p g s -> p (g s)"), bank(0, 2)[:, 0:NG * S]).then_inc(s["kte"], 1)
                    low(Q_ATT + N_ATT, l, jj, N_ATT)

                    def masked(i):
                        q = i % 2
                        dve.wait_ge(s["sc_ok"], at(n, 4, i + 1))
                        if i >= 2:
                            dve.wait_ge(s["pt_ok"], at(n, 4, i - 1))
                        v.scalar_tensor_tensor(sm[:, i % 2, :], bank(2 + 2 * (i % 2), 2)[:, 0:768], float(AE) ** -0.5,
                                               amask[:, q, :], ALU.mult, ALU.add).then_inc(s["sm_ok"], 1)
                        dve.wait_ge(s["sm_ok"], at(n, 4, i + 1))
                        v.tensor_reduce(nmx[:, i:i + 1], sm[:, i % 2, :], AX.X, ALU.max, negate=True
                                        ).then_inc(s["nm_ok"], 1)

                    def divided(i):
                        hh, q = i // 2, i % 2
                        dve.wait_ge(s["pv_ok"], at(n, 4, i + 1))
                        v.reciprocal(rden[:, i:i + 1], den[:, i:i + 1]).then_inc(s["rd_ok"], 1)
                        dve.wait_ge(s["rd_ok"], at(n, 4, i + 1))
                        v.tensor_scalar(oatt[:, q, bass.ds(jj * P + hh * AE, AE)], PS[:, i % 2, i * AE:(i + 1) * AE],
                                        rden[:, i:i + 1], None, ALU.mult).then_inc(s["oa_ok"], 1)

                    masked(0)
                    masked(1)
                    ada(4)
                    masked(2)
                    divided(0)
                    ada(5)
                    masked(3)
                    divided(1)
                    ada(6)
                    low(Q_ATT + N_ATT + 1, l, jj, N_ATT)
                    divided(2)
                    ada(7)
                    low(Q_ATT + N_ATT + 2, l, jj, N_ATT)
                    divided(3)

                dve.wait_ge(s["oh_ok"], at(l, 1 + PAIRS, 1))
                v.tensor_tensor(oTl[:, 0:2, :], oatT, oTh[:, 0:2, :].bitcast(F32), ALU.subtract).then_inc(s["ol_ok"], 1)

            def coefficients(l):
                dve.wait_ge(s["cf_act"], at(l, 7, 2))
                dve.wait_ge(s["ba_in"], 48 * (l + 1))
                v.tensor_scalar(raw[:, :, 0:12], raw[:, :, 0:12], 1.0, None, ALU.add).then_inc(s["cf_dve"], 1)
                dve.wait_ge(s["cf_dve"], at(l, 5, 1))
                v.reciprocal(coef[:, 0].rearrange("p t d h -> p t (d h)"), raw[:, :, 0:12]).then_inc(s["cf_dve"], 1)
                ba = PS[:, 7, 0:48].rearrange("p (t n) -> p t n", t=2)
                v.tensor_tensor(al, ba[:, :, 12:24], dtbb.rearrange("p (o n) -> p o n", o=1).to_broadcast([P, 2, 12]),
                                ALU.add).then_inc(s["cf_dve"], 1)
                dve.wait_ge(s["cf_act"], at(l, 7, 5))
                v.scalar_tensor_tensor(al, al, 0.0, ta, ALU.max, ALU.add).then_inc(s["cf_dve"], 1)
                dve.wait_ge(s["cf_dve"], at(l, 5, 4))
                v.scalar_tensor_tensor(coef[:, 1].rearrange("p t d h -> p t (d h)"), al, -1.0,
                                       ea.rearrange("p (o n) -> p o n", o=1).to_broadcast([P, 2, 12]),
                                       ALU.mult, ALU.mult).then_inc(s["cf_dve"], 1)
                low(Q_DN + 2, l)
                low(Q_DN + 3, l)

            def over_tiles(mask):
                return mask.rearrange("p d (o n) -> p d o n", o=1).to_broadcast([P, 2, TT, P])

            def pair(l, pp):
                n = l * PAIRS + pp
                dve.wait_ge(s["cf_act"], at(l, 7, 7))
                v.tensor_copy(cf.rearrange("p k t d e -> p (k t d) e"),
                              coef.rearrange("p k t d h -> p (k t d) h")[:, :, bass.ds(pp * 2, 2)]
                              ).then_inc(s["cfp_ok"], 1)
                v.tensor_copy(cwp.rearrange("p a (y e) -> p (a y) e", e=2),
                              cw[:, bass.ds(l, 1), :].rearrange("p l (a h) -> p (l a) h", h=DH)[:, :, bass.ds(pp * 2, 2)]
                              ).then_inc(s["cfp_ok"], 1)
                low(Q_DN + 4, l, pp, N_DN)
                dve.wait_ge(s["cb_ok"], at(n, 3, 1))
                v.memset(cb[:, :, 0:2], 0.0)
                v.memset(cb[:, :, S + 2:S + 4], 0.0).then_inc(s["pad_ok"], 1)
                dve.wait_ge(s["pad_ok"], n + 1)
                dve.wait_ge(s["cfp_ok"], at(n, 2, 2))
                for y in range(3):
                    dve.wait_ge(s["cb_ok"], at(n, 3, y + 1))
                    for a in range(TAPS):
                        for e in range(2):
                            i = 2 * y + e
                            if a == 0:
                                v.tensor_scalar(qs[:, i, :], cb[:, i, 0:S], cwp[:, 0, i:i + 1], None, ALU.mult
                                                ).then_inc(s["cv_s"], 1)
                                continue
                            dve.wait_ge(s["cv_s"], at(n, 30, 10 * y + 2 * (a - 1) + e + 1))
                            v.scalar_tensor_tensor(qs[:, i, :], cb[:, i, a:a + S], cwp[:, a, i:i + 1], qs[:, i, :],
                                                   ALU.mult, ALU.add).then_inc(s["cv_s"], 1)
                    if y < 2:
                        low(Q_DN + 5 + 2 * y, l, pp, N_DN)
                        low(Q_DN + 6 + 2 * y, l, pp, N_DN)
                low(Q_DN + 9, l, pp, N_DN)
                low(Q_DN + 10, l, pp, N_DN)
                dve.wait_ge(s["rs_ok"], at(n, 2, 2))
                for i in range(4):
                    e, w = i % 2, 1 - i // 2
                    v.scalar_tensor_tensor(kqn[:, e, :, w, :], qs[:, i, :].rearrange("p (t n) -> p t n", t=TT),
                                           float(DE) ** -0.5 if w else 1.0,
                                           rs[:, i * S:(i + 1) * S].rearrange("p (t n) -> p t n", t=TT),
                                           ALU.mult, ALU.mult).then_inc(s["kqn_ok"], 1)
                low(Q_DN + 11, l, pp, N_DN)
                dve.wait_ge(s["tk_ok"], n + 1)
                v.tensor_copy(vtok.rearrange("p e t n -> p (e t n)"), PS[:, 7, :]).then_inc(s["vtok_ok"], 1)
                for e in range(2):
                    dve.wait_ge(s["kk_ok"], at(n, 2, e + 1))
                    dve.wait_ge(s["etm_ok"], at(n, 4, 2 * e + 2))
                    for d in range(2):
                        for t in range(TT):
                            v.scalar_tensor_tensor(NB[:, e, d, t, :], PS[:, 4 + e, t * 256:t * 256 + P],
                                                   cf[:, 0, t, d, e:e + 1], ET[:, e, d, t, :], ALU.mult, ALU.mult
                                                   ).then_inc(s["nb_ok"], 1)
                for e in range(2):
                    kq = PS[:, 4 + e, :].rearrange("p (t w n) -> p t w n", t=TT, w=2)[:, :, 1, :]
                    for d in range(2):
                        v.tensor_tensor(AT[:, e, d], kq, ET[:, e, d], ALU.mult).then_inc(s["at_ok"], 1)
                dve.wait_ge(s["nb_ok"], at(n, 8, 8))
                for e in range(2):
                    dve.wait_ge(s["nbT_ok"], at(n, 2, e + 1))
                    v.tensor_tensor(A[:, e], PS[:, 2 + e, :].rearrange("p (d t n) -> p d t n", d=2, t=TT),
                                    over_tiles(level[:, 0]), ALU.mult).then_inc(s["d1_s"], 1)
                    for d in range(2):
                        last = v.tensor_tensor(DT[:, e, d], NB[:, e, d],
                                               level[:, 0, 1 - d:2 - d, :].to_broadcast([P, TT, P]), ALU.mult)
                    last.then_inc(s["d1_s"], 1)
                    eye = ident.rearrange("p (o n) -> p o n", o=1).to_broadcast([P, 4, P])
                    dve.wait_ge(s["d1_s"], at(n, 6, 3 * e + 2))
                    v.tensor_tensor(Dm[:, e].rearrange("p d t n -> p (d t) n"), A[:, e].rearrange("p d t n -> p (d t) n"),
                                    eye, ALU.add).then_inc(s["l_D"], 1)
                    v.tensor_tensor(DT[:, e].rearrange("p d t n -> p (d t) n"), DT[:, e].rearrange("p d t n -> p (d t) n"),
                                    eye, ALU.add).then_inc(s["d1_s"], 1)
                def scaled_keys(e):
                    dve.wait_ge(s["ktok_ok"], n + 1)
                    for d in range(2):
                        t = SECOND[d]
                        v.tensor_scalar(kg[:, 2 * e + d, :], ktok[:, e, t, :], cf[:, 2, t, d, e:e + 1], -1.0,
                                        ALU.mult, ALU.mult).then_inc(s["kg_ok"], 1)
                        t = FIRST[d]
                        v.tensor_scalar(kd[:, e, d, :], ktok[:, e, t, :], cf[:, 3, t, d, e:e + 1], None,
                                        ALU.mult).then_inc(s["kd_ok"], 1)

                def level_up(w, i=0):
                    k = n * 2 * (LEVELS - 1) + 2 * w + 2 * i
                    for e in range(2):
                        dve.wait_ge(s["l_a"], k + e + 1)
                        m = level[:, w + 1] if isinstance(i, int) else \
                            level[:, bass.ds(i + (w + 1), 1)].rearrange("p v d n -> p (v d) n")
                        v.tensor_tensor(A[:, e], PS[:, 2 + e, :].rearrange("p (d t n) -> p d t n", d=2, t=TT),
                                        over_tiles(m), ALU.mult).then_inc(s["l_A"], 1)
                    for e in range(2):
                        dve.wait_ge(s["l_b"], k + e + 1)
                        v.tensor_tensor(DT[:, e].rearrange("p d t n -> p (d t n)"),
                                        DT[:, e].rearrange("p d t n -> p (d t n)"), PS[:, 4 + e, :], ALU.add
                                        ).then_inc(s["l_DT"], 1)

                for w in range(3):
                    level_up(w)
                    low(Q_DN + N_DN + w, l, pp, N_DN)
                    if w < 2:
                        scaled_keys(w)
                with dve.Fori(0, LEVELS - 5) as i:
                    level_up(3, i)
                level_up(LEVELS - 2)
                dve.wait_ge(s["wu_ok"], at(n, 2, 1))
                for e in range(2):
                    for d in range(2):
                        t = FIRST[d]
                        v.tensor_scalar(vn[:, e, d, t, :], PS[:, 3, (2 * e + d) * P:(2 * e + d + 1) * P],
                                        cf[:, 0, t, d, e:e + 1], None, ALU.mult).then_inc(s["vn1_ok"], 1)
                dve.wait_ge(s["v2_ok"], n + 1)
                for e in range(2):
                    for d in range(2):
                        t = SECOND[d]
                        v.tensor_scalar(vn[:, e, d, t, :], PS[:, 5, (2 * e + d) * P:(2 * e + d + 1) * P],
                                        cf[:, 0, t, d, e:e + 1], None, ALU.mult).then_inc(s["vn2_ok"], 1)
                dve.wait_ge(s["o_ok"], n + 1)
                dve.wait_ge(s["qSs_ok"], n + 1)
                v.tensor_tensor(ob.rearrange("p j n -> p (j n)"), PS[:, 7, :], qS.rearrange("p j n -> p (j n)"),
                                ALU.add).then_inc(s["ob_ok"], 1)
                dve.wait_ge(s["orms_ok"], n + 1)
                v.reciprocal(orr, orms).then_inc(s["orr_ok"], 1)
                dve.wait_ge(s["orr_ok"], n + 1)
                dve.wait_ge(s["ob_ok"], n + 1)
                for j in range(4):
                    v.scalar_tensor_tensor(og[:, j, :], ob[:, j, :], orr[:, j:j + 1], nw, ALU.mult, ALU.mult
                                           ).then_inc(s["on_ok"], 1)
                dve.wait_ge(s["on_ok"], at(n, 4, 4))
                dve.wait_ge(s["z_ok"], n + 1)
                v.tensor_tensor(og.rearrange("p (e t) n -> p e t n", e=2), og.rearrange("p (e t) n -> p e t n", e=2),
                                zs.rearrange("p t (e n) -> p e t n", e=2), ALU.mult).then_inc(s["og_ok"], 1)
                low(Q_DN + N_DN + 3, l, pp, N_DN)
                dve.wait_ge(s["oh_ok"], at(l, 1 + PAIRS, 2 + pp))
                v.tensor_tensor(oTl[:, bass.ds(pp * 2 + 2, 2), :], odT, oTh[:, bass.ds(pp * 2 + 2, 2), :].bitcast(F32),
                                ALU.subtract).then_inc(s["ol_ok"], 1)

            def final(l):
                for k in range(4, 7):
                    low(Q_FIN + k, l)
                for dc in range(KC):
                    par = dc % 2
                    dve.wait_ge(s["used"], l * NQ + q_branch(dc) + 1)
                    dve.wait_ge(s["gs_ok"], at(l, 2 * PAIRS, 2 * PAIRS))
                    dve.wait_ge(s["gt_ok"], at(l, 2, 2))
                    if dc >= 2:
                        dve.wait_ge(s["y_ok"], at(l, KC, dc - 1))
                    gate = GS[:, dc, :] if dc < 6 else GS2[:, dc - 6, :]
                    v.tensor_tensor(m12[:, par, :], gate, PS[:, par, :], ALU.mult).then_inc(s["m12_ok"], 1)
                    dve.wait_ge(s["m12_ok"], at(l, KC, dc + 1))
                    if dc >= 2:
                        dve.wait_ge(s["ach_ok"], q_hidden(l, 0) + UNITS + dc - 1)
                        dve.wait_ge(s["acl_ok"], q_hidden(l, 0) + UNITS + dc - 1)
                    v.tensor_tensor(yT[:, par, :], m12[:, par, 0:S], m12[:, par, S:2 * S], ALU.add
                                    ).then_inc(s["y_ok"], 1)
                    dve.wait_ge(s["y_ok"], at(l, KC, dc + 1))
                    dve.wait_ge(s["ach_ok"], q_hidden(l, 0) + UNITS + dc + 1)
                    v.tensor_tensor(ACl[:, par, 0:S], yT[:, par, :], ACh[:, par, 0:S].bitcast(F32), ALU.subtract
                                    ).then_inc(s["acl_ok"], 1)
                    for q in (Q_FIN + 7 + 2 * dc, Q_FIN + 8 + 2 * dc):
                        if q < Q_FFN[1]:
                            low(q, l)

            made = [0]

            def link(instruction):
                made[0] += 1
                instruction.then_inc(s["sd"], 1)
                dve.wait_ge(s["sd"], made[0])

            v.memset(ones[:, :], 1.0).then_inc(s["layer_done"], 1)
            v.memset(acc[:, :], 0.0).then_inc(s["acc_zero"], 1)
            v.memset(eps[:, :], EPS).then_inc(s["setup_dve"], 1)
            dve.wait_ge(s["setup_dve"], 1)
            dve.wait_ge(s["pos_in"], 16)
            dve.wait_ge(s["table_in"], 16)
            link(v.tensor_copy(posf[:, :], posi[:, :]))
            for t in range(TT):
                link(v.tensor_scalar(ang[:, t, :], freq, posf[:, t:t + 1], None, ALU.mult))
            angf = ang.rearrange("p t f -> p (t f)")
            W = TT * AE // 2
            for k, quarter in ((0, 0.25), (1, 0.0)):
                turns, a = turn_[:, k * W:(k + 1) * W], angle[:, k * W:(k + 1) * W]
                link(v.tensor_scalar(turns, angf, 1.0 / TWO_PI, quarter, ALU.mult, ALU.add))
                link(v.tensor_scalar(turns, turns, ROUND, None, ALU.add))
                link(v.tensor_scalar(turns, turns, -ROUND, None, ALU.add))
                link(v.scalar_tensor_tensor(a, turns, -PI1, angf, ALU.mult, ALU.add))
                link(v.scalar_tensor_tensor(a, turns, -PI2, a, ALU.mult, ALU.add))
                link(v.scalar_tensor_tensor(a, turns, -PI3, a, ALU.mult, ALU.add))
                link(v.tensor_scalar(a, a, quarter * TWO_PI, None, ALU.add))
                link(v.tensor_scalar(a, a, 3.1415925, -3.1415925, ALU.min, ALU.max))
            assert made[0] == SD_ANGLE
            dve.wait_ge(s["setup_pe"], 1)
            link(v.tensor_copy(cols[:, :], PS[:, 7, 0:56]))
            for l in range(DEPTH):
                link(v.tensor_copy(cw[:, l, :], PS[:, 7, 128 * (l + 1):128 * (l + 1) + 90]))
            assert made[0] == SD_COLS
            dve.wait_ge(s["sa"], 2)
            dve.wait_ge(s["bias_in"], 16)
            for kc in range(KC):
                for half in range(2):
                    ada_block(0, kc, half)
            mod_columns(0, 0, 0)
            dve.wait_ge(s["x_in"], 16)
            with dve.Fori(0, DEPTH) as l:
                norm(l * 3, l, Q_FFN[0], 0)
                ffn(l, 0, l * 3 + 1)
                mod_columns(l * 3 + 1, l, 1)
                post(l * 3)
                norm(l * 3 + 1, l, Q_ATT, 1)
                attention(l, l * 3 + 2)
                coefficients(l)
                with dve.Fori(0, PAIRS) as pp:
                    pair(l, pp)
                final(l)
                mod_columns(l * 3 + 2, l, 2)
                post(l * 3 + 1)
                norm(l * 3 + 2, l, Q_FFN[1], 2)
                ffn(l, 1, l * 3 + 3)
                mod_columns(l * 3 + 3, l * -1 + 1, 0, end_of_layer=True)
                post(l * 3 + 2)


_INS = ['x', 'c', 'positions', 'w_ada', 'b_ada', 'norm_pre', 'norm_post', 'ffn_w_in', 'ffn_w_out', 'w_in', 'conv_w',
        'a_log', 'dt_bias', 'dn_norm_w', 'w_branch_att', 'w_branch_dn', 'w_out']


def kernel(**inputs):
    import concourse.bacc as bacc
    from concourse.bass_utils import run_bass_kernel_spmd

    nc = bacc.Bacc("TRN2", target_bir_lowering=False, num_devices=1)
    arrays, args = {}, []
    given = [(name, np.ascontiguousarray(inputs[name])) for name in _INS] + [("table", constant_table())]
    for name, a in given:
        arrays[f"in_{name}"] = a
        args.append(nc.dram_tensor(f"in_{name}", a.shape, mybir.dt.from_np(a.dtype), kind="ExternalInput").ap())
    out = nc.dram_tensor("out_x", (1, S, D), F32, kind="ExternalOutput").ap()
    build(nc, *args, out)
    return run_bass_kernel_spmd(nc, [arrays], core_ids=[0]).results[0]["out_x"]
```
